# Optimizing a Trainium2 kernel written in Bass

```python
import jax, jax.numpy as jnp
from jax import lax
import numpy as np

D_MODEL = 1024
BATCH = 1
SEQ = 1024
DEPTH = 1

GRID_W = 64
CTX_LEN = 256
M_HEADS = 8
M_HEAD_DIM = D_MODEL // M_HEADS
M_WIDTH = M_HEADS * M_HEAD_DIM
CHUNK = 128
SC_WIDTH = D_MODEL
FF_HIDDEN = ((8 * D_MODEL // 3 + 127) // 128) * 128
EPS = 1e-6
M_INIT = -1e30
N_GATES = 4 * M_HEADS

OFF_Q = 0
OFF_K = M_WIDTH
OFF_V = 2 * M_WIDTH
OFF_G = 3 * M_WIDTH
OFF_O = OFF_G + N_GATES
OFF_SB = OFF_O + M_WIDTH
OFF_SC = OFF_SB + SC_WIDTH
OFF_SX = OFF_SC + SC_WIDTH
OFF_MG = OFF_SX + SC_WIDTH
IN_COLS = OFF_MG + 2 * D_MODEL
CTX_COLS = OFF_O

kernel_name = "hybrid_mlstm_shortconv_convffn_prefix_block"

def _rmsnorm(x, g):
    x32 = x.astype(jnp.float32)
    y = x32 * lax.rsqrt(jnp.mean(x32 * x32, axis=-1, keepdims=True) + EPS) * g.astype(jnp.float32)
    return y.astype(x.dtype)

def _modulate(x, g, shift, scale):
    return _rmsnorm(x, g) * (1 + scale) + shift

def _conv1d_w3(x, w, b):
    xp = jnp.pad(x, ((0, 0), (1, 1), (0, 0)))
    return xp[:, :-2] * w[0] + xp[:, 1:-1] * w[1] + xp[:, 2:] * w[2] + b

def _conv2d_3x3(x, w, b, rows):
    bsz, t, ch = x.shape
    xg = x.reshape(bsz, rows, GRID_W, ch)
    y = lax.conv_general_dilated(xg, w[:, :, None, :], (1, 1), 'SAME',
                                 dimension_numbers=('NHWC', 'HWIO', 'NHWC'),
                                 feature_group_count=ch)
    return y.reshape(bsz, t, ch) + b

def _mlstm_chunk_scan(q, k, v, ig, lf, state, emit):
    bsz, nh, t, dh = q.shape
    nc = t // CHUNK

    def chunks(a):
        return jnp.moveaxis(a.reshape(bsz, nh, nc, CHUNK, *a.shape[3:]), 2, 0)

    lower_tri = jnp.tril(jnp.ones((CHUNK, CHUNK), dtype=bool))

    def step(carry, inp):
        c_mat, n_vec, m = carry
        qc, kc, vc, ic, fc = inp
        b = jnp.cumsum(fc, axis=-1)
        dmat = b[..., :, None] - b[..., None, :] + ic[..., None, :]
        dmat = jnp.where(lower_tri, dmat, -jnp.inf)
        inter = b + m[..., None]
        m_t = jnp.maximum(inter, jnp.max(dmat, axis=-1))
        w = jnp.exp(dmat - m_t[..., None])
        a_inter = jnp.exp(inter - m_t)
        s = jnp.einsum('bhtd,bhsd->bhts', qc, kc) * w
        num = (a_inter[..., None] * jnp.einsum('bhed,bhtd->bhte', c_mat, qc)
               + jnp.einsum('bhts,bhse->bhte', s, vc))
        den = a_inter * jnp.einsum('bhd,bhtd->bht', n_vec, qc) + jnp.sum(s, axis=-1)
        h = num / jnp.maximum(jnp.abs(den), jnp.exp(-m_t))[..., None]
        b_end = b[..., -1]
        g = b_end[..., None] - b + ic
        m_new = jnp.maximum(b_end + m, jnp.max(g, axis=-1))
        decay = jnp.exp(b_end + m - m_new)
        wk = jnp.exp(g - m_new[..., None])
        c_new = decay[..., None, None] * c_mat + jnp.einsum('bhs,bhse,bhsd->bhed', wk, vc, kc)
        n_new = decay[..., None] * n_vec + jnp.einsum('bhs,bhsd->bhd', wk, kc)
        return (c_new, n_new, m_new), (h if emit else None)

    final, hs = lax.scan(step, state, tuple(chunks(a) for a in (q, k, v, ig, lf)))
    if not emit:
        return final, None
    return final, jnp.moveaxis(hs, 0, 2).reshape(bsz, nh, t, dh)

def _mlstm_prep(p, qk_w, qk_b, g_b):
    bsz, t, _ = p.shape
    qk = jax.nn.silu(_conv1d_w3(p[..., OFF_Q:OFF_V], qk_w, qk_b))

    def heads(a):
        return a.reshape(bsz, t, M_HEADS, M_HEAD_DIM).transpose(0, 2, 1, 3).astype(jnp.float32)

    q = heads(qk[..., :M_WIDTH])
    k = heads(qk[..., M_WIDTH:]) * (M_HEAD_DIM ** -0.5)
    v = heads(p[..., OFF_V:OFF_G])
    g = (p[..., OFF_G:OFF_O] + g_b).astype(jnp.float32).reshape(bsz, t, 4, M_HEADS).transpose(2, 0, 3, 1)
    ig = (g[0], g[2])
    lf = (jax.nn.log_sigmoid(g[1]), jax.nn.log_sigmoid(g[3]))
    return q, k, v, ig, lf

def _mlstm_bidirectional(ctx_parts, lat_parts, emit_ctx):
    qc, kc, vc, igc, lfc = ctx_parts
    ql, kl, vl, igl, lfl = lat_parts
    bsz, nh, _, dh = ql.shape
    h_lat = None
    h_ctx = None
    for d, flip in enumerate((False, True)):
        fl = (lambda a: jnp.flip(a, axis=2)) if flip else (lambda a: a)
        state0 = (jnp.zeros((bsz, nh, dh, dh), jnp.float32),
                  jnp.zeros((bsz, nh, dh), jnp.float32),
                  jnp.full((bsz, nh), M_INIT, jnp.float32))
        st_ctx, hc = _mlstm_chunk_scan(fl(qc), fl(kc), fl(vc), fl(igc[d]), fl(lfc[d]), state0, emit_ctx)
        _, hl = _mlstm_chunk_scan(fl(ql), fl(kl), fl(vl), fl(igl[d]), fl(lfl[d]), st_ctx, True)
        h_lat = fl(hl) if h_lat is None else h_lat + fl(hl)
        if emit_ctx:
            h_ctx = fl(hc) if h_ctx is None else h_ctx + fl(hc)
    return h_lat, h_ctx

def _mlstm_out(h, p, norm_g, w_out):
    bsz, nh, t, dh = h.shape
    h = h * lax.rsqrt(jnp.mean(h * h, axis=-1, keepdims=True) + EPS) \
        * norm_g.astype(jnp.float32).reshape(M_HEADS, 1, M_HEAD_DIM)
    h = h.transpose(0, 2, 1, 3).reshape(bsz, t, M_WIDTH).astype(p.dtype)
    return (h * jax.nn.sigmoid(p[..., OFF_O:OFF_SB])) @ w_out

def _shortconv_branch(p, w, b, w_out):
    bg = p[..., OFF_SB:OFF_SC]
    cg = p[..., OFF_SC:OFF_SX]
    xin = p[..., OFF_SX:OFF_MG]
    return (bg * _conv1d_w3(cg * xin, w, b)) @ w_out

def _merge(p, y_m, y_c, w_o):
    gm = jax.nn.sigmoid(p[..., OFF_MG:OFF_MG + D_MODEL])
    gc = jax.nn.sigmoid(p[..., OFF_MG + D_MODEL:IN_COLS])
    return (gm * y_m + gc * y_c) @ w_o

def _conv_ffn(h, w_up, conv_w, conv_b, w_down, rows):
    u = h @ w_up
    a, g = u[..., :FF_HIDDEN], u[..., FF_HIDDEN:]
    if rows is None:
        a = _conv1d_w3(a, conv_w[1], conv_b)
    else:
        a = _conv2d_3x3(a, conv_w, conv_b, rows)
    return (jax.nn.gelu(a, approximate=True) * g) @ w_down

def setup_inputs(seed: int = 0) -> dict:
    key = jax.random.key(seed)
    ks = jax.random.split(key, 24)
    f32 = jnp.float32

    def nrm(k, shape, s):
        return jax.random.normal(k, shape, f32) * s

    L = DEPTH
    fb = jnp.linspace(3.0, 6.0, M_HEADS, dtype=f32)
    gk = jax.random.split(ks[11], 4)
    gate_b = jnp.concatenate([nrm(gk[0], (L, M_HEADS), 0.1),
                              fb + nrm(gk[1], (L, M_HEADS), 0.1),
                              nrm(gk[2], (L, M_HEADS), 0.1),
                              fb + nrm(gk[3], (L, M_HEADS), 0.1)], axis=-1)
    return {
        "x": nrm(ks[0], (BATCH, SEQ, D_MODEL), 1.0),
        "c": nrm(ks[1], (BATCH, D_MODEL), 1.0),
        "ctx": nrm(ks[2], (BATCH, CTX_LEN, D_MODEL), 1.0),
        "c_ctx": nrm(ks[3], (D_MODEL,), 1.0),
        "ada_w": nrm(ks[4], (L, D_MODEL, 6 * D_MODEL), 0.5 * D_MODEL ** -0.5),
        "ada_b": nrm(ks[5], (L, 6 * D_MODEL), 0.01),
        "norm1_g": 1.0 + nrm(ks[6], (L, D_MODEL), 0.02),
        "norm2_g": 1.0 + nrm(ks[7], (L, D_MODEL), 0.02),
        "w_in": nrm(ks[8], (L, D_MODEL, IN_COLS), D_MODEL ** -0.5),
        "qk_conv_w": nrm(ks[9], (L, 3, 2 * M_WIDTH), 3 ** -0.5),
        "qk_conv_b": nrm(ks[10], (L, 2 * M_WIDTH), 0.01),
        "gate_b": gate_b,
        "mnorm_g": 1.0 + nrm(ks[12], (L, M_WIDTH), 0.02),
        "w_m_out": nrm(ks[13], (L, M_WIDTH, D_MODEL), M_WIDTH ** -0.5),
        "sc_conv_w": nrm(ks[14], (L, 3, SC_WIDTH), 3 ** -0.5),
        "sc_conv_b": nrm(ks[15], (L, SC_WIDTH), 0.01),
        "w_c_out": nrm(ks[16], (L, SC_WIDTH, D_MODEL), SC_WIDTH ** -0.5),
        "w_o": nrm(ks[17], (L, D_MODEL, D_MODEL), D_MODEL ** -0.5),
        "w_up": nrm(ks[18], (L, D_MODEL, 2 * FF_HIDDEN), D_MODEL ** -0.5),
        "ff_conv_w": nrm(ks[19], (L, 3, 3, FF_HIDDEN), 1.0 / 3.0),
        "ff_conv_b": nrm(ks[20], (L, FF_HIDDEN), 0.01),
        "w_down": nrm(ks[21], (L, FF_HIDDEN, D_MODEL), FF_HIDDEN ** -0.5),
        "final_g": 1.0 + nrm(ks[22], (D_MODEL,), 0.02),
    }

def reference(x, c, ctx, c_ctx, ada_w, ada_b, norm1_g, norm2_g, w_in, qk_conv_w, qk_conv_b,
              gate_b, mnorm_g, w_m_out, sc_conv_w, sc_conv_b, w_c_out, w_o, w_up,
              ff_conv_w, ff_conv_b, w_down, final_g):
    rows = x.shape[1] // GRID_W
    for l in range(DEPTH):
        last = l == DEPTH - 1
        mod_x = (jax.nn.silu(c) @ ada_w[l] + ada_b[l]).reshape(-1, 6, D_MODEL)[:, :, None, :]
        mod_c = (jax.nn.silu(c_ctx) @ ada_w[l] + ada_b[l]).reshape(6, D_MODEL)

        hx = _modulate(x, norm1_g[l], mod_x[:, 0], mod_x[:, 1])
        hc = _modulate(ctx, norm1_g[l], mod_c[0], mod_c[1])
        px = hx @ w_in[l]
        pc = hc @ (w_in[l][:, :CTX_COLS] if last else w_in[l])

        lat_parts = _mlstm_prep(px, qk_conv_w[l], qk_conv_b[l], gate_b[l])
        ctx_parts = _mlstm_prep(pc, qk_conv_w[l], qk_conv_b[l], gate_b[l])
        h_lat, h_ctx = _mlstm_bidirectional(ctx_parts, lat_parts, not last)

        y_x = _merge(px,
                     _mlstm_out(h_lat, px, mnorm_g[l], w_m_out[l]),
                     _shortconv_branch(px, sc_conv_w[l], sc_conv_b[l], w_c_out[l]),
                     w_o[l])
        x = x + mod_x[:, 2] * y_x
        if not last:
            y_c = _merge(pc,
                         _mlstm_out(h_ctx, pc, mnorm_g[l], w_m_out[l]),
                         _shortconv_branch(pc, sc_conv_w[l], sc_conv_b[l], w_c_out[l]),
                         w_o[l])
            ctx = ctx + mod_c[2] * y_c

        hx = _modulate(x, norm2_g[l], mod_x[:, 3], mod_x[:, 4])
        x = x + mod_x[:, 5] * _conv_ffn(hx, w_up[l], ff_conv_w[l], ff_conv_b[l], w_down[l], rows)
        if not last:
            hc = _modulate(ctx, norm2_g[l], mod_c[3], mod_c[4])
            ctx = ctx + mod_c[5] * _conv_ffn(hc, w_up[l], ff_conv_w[l], ff_conv_b[l], w_down[l], None)

    return _rmsnorm(x, final_g)


_drawn_inputs = setup_inputs


def setup_inputs(seed=0):
    import zlib

    import numpy as np

    out = dict(_drawn_inputs(seed))
    spreads = {}
    factors = {'ctx': 52.84,
     'c_ctx': 32.984,
     'ada_b': 4.43,
     'norm1_g': 7.344,
     'norm2_g': 64.0,
     'qk_conv_b': 200.0,
     'mnorm_g': 200.0,
     'sc_conv_b': 200.0,
     'ff_conv_b': 200.0,
     'final_g': 23.738,
     'qk_conv_w': 8.0,
     'gate_b': 8.0,
     'w_m_out': 4.477}
    for name, (base, spread) in spreads.items():
        noise = np.random.default_rng([zlib.crc32(name.encode()), seed]).standard_normal(out[name].shape)
        drawn = base * np.exp(spread * noise) if base else spread * noise
        out[name] = __import__('jax').numpy.asarray(drawn.astype(out[name].dtype))
    for name, factor in factors.items():
        out[name] = (out[name] * factor).astype(out[name].dtype)
    return out
```

```python
from contextlib import ExitStack

import concourse.bass as bass
from concourse import mybir

F32 = mybir.dt.float32
F32R = mybir.dt.float32r
ALU = mybir.AluOpType
ACT = mybir.ActivationFunctionType
AX_X = mybir.AxisListType.X

P = 128
D = 1024
KT = D // P
T = 1024
TC = 256
TA = TC + T
HALF = 512
H = 8
CH = 128
NC = TA // CH
NCC = TC // CH
NL = T // CH
VW = P + 1
GRID = 64
ROWS = T // GRID
AC = 256
NAL = 6 * D // AC
NAL1 = 2 * D // AC
FF = 2816
FT = FF // P
GROUPS = (8, 7, 7)
EPS = 1e-6
NEG = -1e30
BIG = 1e30
EXP_MAX = 88.0
SCALE = float(P) ** -0.5

OFF_Q, OFF_K, OFF_V, OFF_G = 0, D, 2 * D, 3 * D
OFF_O = OFF_G + 4 * H
OFF_SB, OFF_SC, OFF_SX, OFF_MG = OFF_O + D, OFF_O + 2 * D, OFF_O + 3 * D, OFF_O + 4 * D

ADA_B, N1G, N2G, C_X, C_CTX, MNG, SCB, SCW = 0, 48, 56, 64, 72, 80, 88, 96
QKW, QKB, FFB, FFW = 128, 176, 192, 256
B_CTX, B_S, B_T, B_G, B_O = 2, 3, 5, 6, 7

N_SETUP = 18
N_PAR = 13
SCAN = ([*range(NC - 1)], [*range(NCC)][::-1] + [*range(NCC + 1, NC)][::-1])
OUT = (((0, 1, 2), (3, 4, 5), (6, 7)), ((5, 6, 7), (2, 3, 4), (0, 1)))
ROW_F, ROW_ABS, ROW_U, ROW_M, ROW_AX, ROW_WX, ROW_EX = 1, 2, 11, 19, 27, 28, 30
ROW_EXP, ROW_LN, ROW_A, ROW_WK, ROW_EM = 1, 2, 3, 4, 5

V_HEAD = 37

N_GATE = 0
N_HEAD = 1
N_CONV = N_HEAD + 4 * H
N_MIX_M = N_CONV + 3 * KT
N_MIX_C = N_MIX_M + 2 * KT
N_WO = N_MIX_C + 2 * KT
N_FFN = N_WO + KT
N_ALL = N_FFN + 2 * FT + len(GROUPS) * KT


def at(count):
    return count + 1


class Tile:

    def __init__(self, base, per=0, i=0, down=0):
        self.slot = base % 2
        self.n = base + per * i if per else base
        self.nth = base // 2 + (per // 2) * i if per else base // 2
        self.base, self.per, self.i, self.down = base, per, i, down
        self.p = self.n - down

    def ahead(self, k):
        return Tile(self.base + k, self.per, self.i, self.down)


class Chain:

    def __init__(self, eng, sem):
        self.eng, self.sem, self.count, self.i, self.first = eng, sem, 0, None, 0

    def step(self, ins):
        ins.then_inc(self.sem, 1)
        self.count += 1
        self.eng.wait_ge(self.sem, self.value())

    def value(self):
        if self.i is None:
            return at(self.count)
        return self.per * (self.i - self.first) + at(self.count)

    def enter(self, i, first, per):
        self.i, self.first, self.per, self.began = i, first, per, self.count

    def leave(self, passes):
        assert self.count - self.began == self.per, (self.count - self.began, self.per)
        self.i = None
        self.count = self.began + passes * self.per


def layer(nc, x, c, ctx, c_ctx, ada_w, ada_b, norm1_g, norm2_g, w_in, qk_conv_w, qk_conv_b, gate_b,
          mnorm_g, w_m_out, sc_conv_w, sc_conv_b, w_c_out, w_o, w_up, ff_conv_w, ff_conv_b, w_down,
          final_g, out):
    ds = bass.ds
    m_rows = nc.dram_tensor("m_rows", (2, H, TA), F32, kind="Internal").ap()
    a_rows = nc.dram_tensor("a_rows", (2, H, TA), F32, kind="Internal").ap()
    a_dram = nc.dram_tensor("branch_a", (KT, P, T), F32, kind="Internal").ap()
    z_dram = nc.dram_tensor("branch_z", (KT, P, T), F32, kind="Internal").ap()

    def rows(w):
        return w.rearrange("(k p) n -> p k n", p=P)

    win, wup, wmo, wco, wo_, wdn = (rows(w[0]) for w in (w_in, w_up, w_m_out, w_c_out, w_o, w_down))
    adw = rows(ada_w[0])
    x_tok = x[0].rearrange("(j p) d -> p j d", p=P)
    ctx_tok = ctx[0].rearrange("(j p) d -> p j d", p=P)
    out_tok = out[0].rearrange("(j p) d -> j p d", p=P)

    ctx_ = ExitStack()
    with ctx_:
        def keep(name, shape, dt=F32):
            return ctx_.enter_context(nc.sbuf_tensor(name, shape, dt))

        def sem(name):
            s = ctx_.enter_context(nc.semaphore(name))
            return s

        credited = []

        def csem(name):
            s = sem(name)
            credited.append(s)
            return s

        op_hi = keep("op_hi", [P, KT, T], F32R)
        op_lo = keep("op_lo", [P, KT, T], F32R)
        w_raw = keep("w_raw", [P, 2, KT, P])
        w_hi = keep("w_hi", [P, 2, KT, P], F32R)
        w_lo = keep("w_lo", [P, 2, KT, P], F32R)
        ident = keep("ident", [P, P])
        ones = keep("ones", [P, P])
        par = keep("par", [P, 4 * P])
        mod = keep("mod", [P, 48, 2])
        gain = keep("gain", [P, 3, KT])
        power = keep("power", [P, KT])
        zero8 = keep("zero8", [P, NL])
        gate5 = keep("gate5", [P, KT])

        def scoped(*tensors):
            with ExitStack() as s:
                return [s.enter_context(nc.sbuf_tensor(n, sh, dt)) for n, sh, dt in tensors]

        with ExitStack() as s1:
            def shared(n, sh, dt=F32):
                return s1.enter_context(nc.sbuf_tensor(n, sh, dt))
            ctx_hi = shared("ctx_hi", [P, KT, TC], F32R)
            ctx_lo = shared("ctx_lo", [P, KT, TC], F32R)
            cols = shared("cols", [P, 3, NC, 2, H])
            late, early = shared("late", [P, P]), shared("early", [P, P])
            x_in, ht = scoped(("x_in", [P, 2, 4, D], F32), ("ht", [P, 2, 512], F32))
            raw = shared("raw", [P, T + TC + 4])
            conv = shared("conv", [P, TA])
            q_t, og = shared("q_t", [P, T]), shared("og", [P, T])
            k_t, v_t = shared("k_t", [P, TA]), shared("v_t", [P, TA])
            (g_i, g_f, g_e, g_b, g_m, g_d, g_r, g_s, aw, prow, cs, stat, gbias, mp) = scoped(
                *[(f"g_{n}", [64, TA], F32) for n in "ifebmdrs"],
                ("aw", [P, 2, KT, AC], F32), ("prow", [P, 4, P], F32), ("cs", [P, KT, 2], F32),
                ("stat", [P, 3, 16], F32), ("gbias", [64, 2], F32), ("mp", [64, 2, NC], F32))
            (m_bc, a_bc, k_tok, v_tok, wgt, pt, qs, vw, state, h_tok, tiny, h_tmp) = scoped(
                ("m_bc", [P, 2, T], F32), ("a_bc", [P, 2, TA], F32), ("k_tok", [P, NC, P], F32),
                ("v_tok", [P, NC, VW], F32), ("wgt", [P, NL, CH], F32), ("pt", [P, NL, CH], F32),
                ("qs", [P, 2, T], F32), ("vw", [P, NC, VW], F32), ("state", [P, 2, NC - 1, VW], F32),
                ("h_tok", [P, NL, P], F32), ("tiny", [P, 96], F32), ("h_tmp", [P, 3, P], F32))
        with ExitStack() as s3:
            br_hi = s3.enter_context(nc.sbuf_tensor("br_hi", [P, KT, T], F32R))
            br_lo = s3.enter_context(nc.sbuf_tensor("br_lo", [P, KT, T], F32R))
            res = s3.enter_context(nc.sbuf_tensor("res", [P, KT, T], F32))
            gth, b_raw, mtmp = scoped(("gth", [P, T], F32), ("b_raw", [P, 2, T], F32), ("mtmp", [P, T], F32))
            x_j, st2, sqx = scoped(("x_j", [P, NL, P], F32), ("st2", [P, 32], F32), ("sqx", [P, T], F32))
            _, u_t, u_h = scoped(("below_u", [P, T + 32], F32), ("u_t", [P, 2, T], F32), ("u_h", [P, T], F32))
            diag = x_j
            a_pad, cv, gv = scoped(("a_pad", [P, ROWS + 2, GRID + 2], F32), ("cv", [P, T], F32),
                                   ("gv", [P, T], F32))
            o_out, gbc, junk, st3 = scoped(("o_out", [P, 2, D], F32), ("gbc", [P, D], F32),
                                           ("junk", [P, D], F32), ("st3", [P, 24], F32))
        ps = ctx_.enter_context(nc.psum_tensor("ps", [P, 8, 512], F32))

        par_in, gb_in, gb_out = sem("par_in"), sem("gb_in"), sem("rows_out")
        x_loaded = [sem(f"x_loaded{b}") for b in range(2)]
        ada_in = [[sem(f"ada_in{q}{b}") for b in range(2)] for q in range(2)]
        raw_in = [sem(f"raw_in{b}") for b in range(2)]
        bc_in = sem("bc_in")
        a_out, z_out = sem("a_out"), sem("z_out")
        br_in = [sem(f"br_in{b}") for b in range(2)]
        xj_in, gbc_in, y_out = sem("xj_in"), sem("gbc_in"), [sem("y_out0"), sem("y_out1")]
        setup = csem("setup")
        par_turned, par_ready = csem("par_turned"), csem("par_ready")
        cond_ready = csem("cond_ready")
        mod_done, mod_ready = csem("mod_done"), csem("mod_ready")
        sumsq, rms = csem("sumsq"), csem("rms")
        x_scaled, x_turned, x_mod = csem("x_scaled"), csem("x_turned"), csem("x_mod")
        act_hi, act_lo = csem("act_hi"), csem("act_lo")
        hi_ready, lo_ready = csem("hi_ready"), csem("lo_ready")
        full = [csem(f"full{b}") for b in range(2)]
        drained = [csem(f"drained{b}") for b in range(2)]
        ctx_full, ctx_drained = csem("ctx_full"), csem("ctx_drained")
        row_v, row_a, row_turned, row_cols = (csem(n) for n in ("row_v", "row_a", "row_turned", "row_cols"))
        conv_ready, tanh_ready = csem("conv_ready"), csem("tanh_ready")
        q_ready, k_ready, og_ready = (csem(n) for n in ("q_ready", "k_ready", "og_ready"))
        turned, tok_ready = csem("turned"), csem("tok_ready")
        s_full, expo_ready, wexp_ready, pt_ready = (csem(n) for n in ("s_full", "expo_ready", "wexp_ready", "pt_ready"))
        qs_ready, vw_ready, g_full, state_ready = (csem(n) for n in ("qs_ready", "vw_ready", "g_full", "state_ready"))
        o_full, den_ready, h_ready = csem("o_full"), csem("den_ready"), csem("h_ready")
        sq_ready, ss_ready, rn_ready, hn_ready = (csem(n) for n in ("sq_ready", "ss_ready", "rn_ready", "hn_ready"))
        h_turned, at_ready = csem("h_turned"), csem("at_ready")
        a_stored, z_stored = csem("a_stored"), csem("z_stored")
        v_step, a_step, p_step = csem("v_step"), csem("a_step"), csem("p_step")
        br_hi_ready, br_lo_ready = csem("br_hi_ready"), csem("br_lo_ready")
        gth_ready, mix_ready = csem("gth_ready"), csem("mix_ready")
        xj_turned, xres_ready, sqx_ready, stat_done = (
            csem(n) for n in ("xj_turned", "xres_ready", "sqx_ready", "stat_done"))
        bc2_done, n2_ready, ut_ready = csem("bc2_done"), csem("n2_ready"), csem("ut_ready")
        n2_sum, n2_rms, pad_ready = csem("n2_sum"), csem("n2_rms"), csem("pad_ready")
        cv_ready, gelu_ready, u_ready, uh_ready, ul_ready = (
            csem(n) for n in ("cv_ready", "gelu_ready", "u_ready", "uh_ready", "ul_ready"))
        f_turned, f_sum, f_rms, f_ready = (csem(n) for n in ("f_turned", "f_sum", "f_rms", "f_ready"))

        block = ctx_.enter_context(nc.Block())

        def products(t, half, ks, first, last, src, dst=None):
            hi, lo = src
            dst = ps[:, half, :] if dst is None else dst
            sl = slice(half * HALF, half * HALF + HALF) if dst.shape[-1] == HALF else slice(0, TC)
            for k in ks:
                for w, a in ((w_hi, hi), (w_hi, lo), (w_lo, hi)):
                    ins = nc.tensor.matmul(dst, w[:, t.slot, k, :], a[:, k, sl],
                                           start=(k == first and w is w_hi and a is hi),
                                           stop=(k == last and w is w_lo))
            return ins

        op, ctx_op, br = (op_hi, op_lo), (ctx_hi, ctx_lo), (br_hi, br_lo)

        @block.tensor
        def _(pe):
            def weights(t):
                pe.wait_ge(hi_ready, at(t.n + 1))
                pe.wait_ge(lo_ready, at(t.n + 1))

            def half_tile(t, half, between=None, src=op, kt=KT):
                if half == 0:
                    weights(t)
                pe.wait_ge(drained[half], at(t.n))
                products(t, half, range(kt // 2), 0, kt - 1, src)
                if between:
                    between()
                products(t, half, range(kt // 2, kt), 0, kt - 1, src).then_inc(full[half], 1)

            def ctx_tile(t, nth):
                weights(t)
                pe.wait_ge(ctx_drained, at(nth))
                products(t, 0, range(KT), 0, KT - 1, ctx_op, ps[:, B_CTX, 0:TC]).then_inc(ctx_full, 1)

            pe.wait_ge(setup, at(2))
            pe.wait_ge(par_in, 16 * N_PAR)
            for r, n in enumerate((120, 86, 128, 70)):
                nc.tensor.transpose(ps[:, B_S, r * P:r * P + n], prow[0:n, r, :],
                                    ident[0:n, 0:n]).then_inc(par_turned, 1)
            pe.wait_ge(cond_ready, at(2))

            def modulation(load):
                bank = B_O if load < NAL1 else B_G
                q = int(load >= NAL1)
                pe.wait_ge(ada_in[q][load % 2], 16 * ((load - q * NAL1) // 2 + 1))
                for q in range(AC // P):
                    jt = load * (AC // P) + q
                    for k in range(KT):
                        ins = nc.tensor.matmul(ps[:, bank, 2 * jt:2 * jt + 2], aw[:, load % 2, k, q * P:(q + 1) * P],
                                               cs[:, k, :], start=(k == 0), stop=(k == KT - 1))
                ins.then_inc(mod_done, 1)

            def turn_input(b):
                n = 4 if b < 2 else NCC
                pe.wait_ge(x_scaled, at(4 * b + n))
                for k in range(KT):
                    t = b * KT + k
                    if t >= 3:
                        pe.wait_ge(x_mod, at(t - 2))
                    elif t == 0:
                        pe.wait_ge(par_ready, at(4))
                    for j in range(n):
                        ins = nc.tensor.transpose(ps[:, B_S + t % 3, j * P:(j + 1) * P],
                                                  x_in[:, b % 2, j, k * P:(k + 1) * P], ident[:, :])
                    ins.then_inc(x_turned, 1)

            for load in range(NAL1):
                modulation(load)
            for b in range(3):
                turn_input(b)

            t = Tile(N_GATE)
            pe.wait_ge(act_lo, at(3 * KT))
            ctx_tile(t, 0)
            half_tile(t, 0)
            half_tile(t, 1)
            loads = iter(range(NAL1, NAL))
            for k in range(4):
                t = Tile(N_HEAD + k)
                if k in (1, 2):
                    ctx_tile(t, k)
                for half in range(2):
                    half_tile(t, half, lambda: modulation(next(loads)))
                    modulation(next(loads))
            for q in range(3):
                pe.wait_ge(row_v if q == 0 else row_a, at(ROW_U if q == 0 else (ROW_WK if q == 1 else ROW_EM)))
                pe.wait_ge(row_cols, at(q))
                for ch in range(NC):
                    ins = nc.tensor.transpose(ps[:, B_S + ch // 8, (ch % 8) * 64:(ch % 8) * 64 + 64],
                                              (g_i, g_e, g_s)[q][:, ch * P:(ch + 1) * P], ident[0:64, 0:64])
                ins.then_inc(row_turned, 1)

            def turn_kv(g, j):
                if j == 0:
                    pe.wait_ge(at_ready, at(2 * g))
                    pe.wait_ge(k_ready, at(g + 1))
                    pe.wait_ge(drained[0], at(N_HEAD + 4 * g + 3))
                    pe.wait_ge(drained[1], at(N_HEAD + 4 * g + 3))
                    pe.wait_ge(ctx_drained, at(2 * g + 3))
                else:
                    pe.wait_ge(tok_ready, at(5 * g + j))
                src = ((k_t, 2), (k_t, 6), (v_t, 2), (v_t, 6), (None, 0))[j]
                for q in range(4):
                    if j < 4:
                        a = src[0][:, (src[1] + q) * P:(src[1] + q + 1) * P]
                    else:
                        a = (k_t if q < 2 else v_t)[:, (q % 2) * P:(q % 2 + 1) * P]
                    ins = nc.tensor.transpose(ps[:, B_T, q * P:(q + 1) * P], a, ident[:, :])
                ins.then_inc(turned, 1)

            def scores(g, j):
                pe.wait_ge(q_ready, at(g + 1))
                pe.wait_ge(k_ready, at(g + 1))
                pe.wait_ge(pt_ready, at(4 * g))
                if j == 0:
                    pe.wait_ge(row_cols, at(3))
                for q in range(4):
                    l = 4 * j + q
                    ins = nc.tensor.matmul(ps[:, B_S + j, q * CH:(q + 1) * CH], k_t[:, TC + l * CH:TC + (l + 1) * CH],
                                           q_t[:, l * CH:(l + 1) * CH], start=True, stop=True)
                ins.then_inc(s_full, 1)

            def outer(g, d, j):
                pe.wait_ge(tok_ready, at(5 * g + 5))
                pe.wait_ge(vw_ready, at(2 * g + d + 1))
                pe.wait_ge(state_ready, at(6 * g + 3 * d + j))
                for q in range(3):
                    ch = SCAN[d][3 * j + q]
                    ins = nc.tensor.matmul(ps[:, B_G, q * VW:(q + 1) * VW], k_tok[:, ch, :], vw[:, ch, :],
                                           start=True, stop=True)
                ins.then_inc(g_full, 1)

            def outputs(g, d, j):
                pe.wait_ge(pt_ready, at(4 * g + 2 * d + 2))
                pe.wait_ge(qs_ready, at(2 * g + d + 1))
                pe.wait_ge(state_ready, at(6 * g + 3 * d + 3))
                pe.wait_ge(h_ready, at(6 * g + 3 * d + j))
                for q, l in enumerate(OUT[d][j]):
                    o = ps[:, B_O, q * VW:(q + 1) * VW]
                    nc.tensor.matmul(o, pt[:, l, :], v_tok[:, NCC + l, :], start=True, stop=False)
                    ins = nc.tensor.matmul(o, qs[:, d, l * CH:(l + 1) * CH],
                                           state[:, d, 1 + (l if d == 0 else NL - 1 - l), :], start=False, stop=True)
                ins.then_inc(o_full, 1)

            def turn_h(g, j):
                if j == 0:
                    pe.wait_ge(hn_ready, at(g + 1))
                    pe.wait_ge(tok_ready, at(5 * g + 5))
                else:
                    pe.wait_ge(at_ready, at(2 * g + 1))
                for q in range(4):
                    ins = nc.tensor.transpose(ps[:, B_T, q * P:(q + 1) * P], h_tok[:, 4 * j + q, :], ident[:, :])
                ins.then_inc(h_turned, 1)

            def mlstm(g):
                yield lambda: (turn_kv(g, 0), scores(g, 0))
                yield lambda: (turn_kv(g, 1), scores(g, 1))
                yield lambda: turn_kv(g, 2)
                yield lambda: turn_kv(g, 3)
                yield lambda: turn_kv(g, 4)
                yield lambda: None
                yield lambda: outer(g, 0, 0)
                yield lambda: outer(g, 0, 1)
                yield lambda: outer(g, 0, 2)
                yield lambda: outputs(g, 0, 0)
                yield lambda: outputs(g, 0, 1)
                yield lambda: (outputs(g, 0, 2), outer(g, 1, 0))
                yield lambda: outer(g, 1, 1)
                yield lambda: outer(g, 1, 2)
                yield lambda: outputs(g, 1, 0)
                yield lambda: outputs(g, 1, 1)
                yield lambda: outputs(g, 1, 2)
                yield lambda: None
                yield lambda: (turn_h(g, 0), turn_h(g, 1))

            with pe.Fori(1, H) as i:
                steps = mlstm(i - 1)
                for k in range(4):
                    t = Tile(N_HEAD + k, 4, i)
                    if k in (1, 2):
                        ctx_tile(t, 2 * i + k)
                        next(steps)()
                    for half in range(2):
                        half_tile(t, half, next(steps))
                        if (k, half) != (3, 1):
                            next(steps)()
                for step in steps:
                    step()

            steps = mlstm(H - 1)
            for k in range(6):
                for half in range(2):
                    half_tile(Tile(N_CONV + k), half, next(steps, None))
                    next(steps, lambda: None)()
            with pe.Fori(1, KT // 2) as i:
                for k in range(6):
                    for half in range(2):
                        half_tile(Tile(N_CONV + k, 6, i), half)

            for stage, base in enumerate((N_MIX_M, N_MIX_C)):
                def mix(i):
                    for half in range(2):
                        half_tile(Tile(base, 2, i), half)
                    pe.wait_ge(br_lo_ready, at(KT * (stage + 1)))
                    for half in range(2):
                        half_tile(Tile(base + 1, 2, i), half, src=br)
                with pe.Fori(0, KT) as i:
                    mix(i)

            nc.tensor.matmul(ps[:, B_O, 0:NL], ones[:, :], zero8[:, :], start=True, stop=True)

            def sums(j):
                pe.wait_ge(sqx_ready, at(j + 1))
                for l in range(NL):
                    ins = nc.tensor.matmul(ps[:, B_O, l:l + 1], sqx[:, l * P:(l + 1) * P], ones[:, 0:1],
                                           start=False, stop=True, skip_group_check=True)
                ins.then_inc(stat_done, 1)

            def turn_x(j):
                pe.wait_ge(xj_in, 16 * (j + 1))
                pe.wait_ge(xres_ready, at(j))
                for l in range(NL):
                    ins = nc.tensor.transpose(ps[:, B_S + l // 4, (l % 4) * P:(l % 4 + 1) * P], x_j[:, l, :], ident[:, :])
                ins.then_inc(xj_turned, 1)

            pe.wait_ge(act_lo, at(4 * KT))
            with pe.Fori(0, KT // 2) as i:
                for k in range(2):
                    turn_x(2 * i + k)
                    half_tile(Tile(N_WO + k, 2, i), 0)
                    sums(2 * i + k)
                    half_tile(Tile(N_WO + k, 2, i), 1)
            sums(KT)
            pe.wait_ge(n2_ready, at(1))
            for half in range(2):
                ins = nc.tensor.matmul(ps[:, B_S + half, :], ones[:, :], diag[:, 4 * half:4 * half + 4, :],
                                       start=True, stop=True)
            ins.then_inc(bc2_done, 1)

            n, done = N_FFN, 0
            pe.wait_ge(act_lo, at(5 * KT))
            for size in GROUPS:
                with pe.Fori(0, size) as i:
                    for k in range(2):
                        for half in range(2):
                            half_tile(Tile(n + k, 2, i), half)
                n += 2 * size
                done += size

                def down(t):
                    weights(t)
                    for half in range(2):
                        pe.wait_ge(drained[half], at(t.n))
                        products(t, half, range(size - 1), 0, size - 1, br)
                    pe.wait_ge(ul_ready, at(done))
                    for half in range(2):
                        products(t, half, (size - 1,), 0, size - 1, br).then_inc(full[half], 1)
                pe.wait_ge(ul_ready, at(done - 1))
                with pe.Fori(0, KT // 2) as i:
                    for k in range(2):
                        down(Tile(n + k, 2, i))
                n += KT

            for l in range(NL):
                if l == 0:
                    pe.wait_ge(drained[0], at(N_ALL))
                    pe.wait_ge(drained[1], at(N_ALL))
                if l >= 4:
                    pe.wait_ge(f_ready, at(l - 3))
                for k in range(KT):
                    ins = nc.tensor.transpose(ps[:, 2 * (l % 4) + k // 4, (k % 4) * P:(k % 4 + 1) * P],
                                              res[:, k, l * P:(l + 1) * P], ident[:, :])
                ins.then_inc(f_turned, 1)

        @block.scalar
        def _(act):
            def hi_split(t):
                act.wait_ge(raw_in[t.slot], 16 * (t.nth + 1) + (48 if t.slot == 0 else 0))
                act.wait_ge(full[1], at(t.n - 1))
                nc.scalar.copy(w_hi[:, t.slot], w_raw[:, t.slot]).then_inc(hi_ready, 1)

            act.wait_ge(par_ready, at(4))
            for v, col in enumerate((C_X, C_CTX)):
                nc.scalar.activation(cs[:, :, v], par[:, col:col + KT], ACT.Silu).then_inc(cond_ready, 1)

            def sums_of_squares(b):
                act.wait_ge(x_loaded[b % 2], 16 * (b // 2 + 1))
                for j in range(4 if b < 2 else NCC):
                    act.wait_ge(sumsq, at(4 * b + j))
                    nc.scalar.activation(ps[:, 0:2, :].rearrange("p b n -> p (b n)"), x_in[:, b % 2, j, :],
                                         ACT.Square, accum_out=stat[:, 0, 4 * b + j:4 * b + j + 1]).then_inc(sumsq, 1)

            def modulate(b):
                v, n = (0, HALF) if b < 2 else (1, TC)
                hi = op_hi[:, :, b * HALF:(b + 1) * HALF] if b < 2 else ctx_hi[:, :, :]
                for k in range(KT):
                    t = b * KT + k
                    act.wait_ge(x_turned, at(t + 1))
                    if t >= 2:
                        act.wait_ge(act_lo, at(t - 1))
                    nc.scalar.activation(ht[:, t % 2, 0:n], ps[:, B_S + t % 3, 0:n], ACT.Identity,
                                         scale=gain[:, v, k:k + 1], bias=mod[:, k, v:v + 1]).then_inc(x_mod, 1)
                    act.wait_ge(x_mod, at(t + 1))
                    nc.scalar.copy(hi[:, k, :], ht[:, t % 2, 0:n]).then_inc(act_hi, 1)

            sums_of_squares(0)
            sums_of_squares(1)
            act.wait_ge(mod_ready, at(3))
            modulate(0)
            sums_of_squares(2)
            modulate(1)
            modulate(2)
            for n in range(2):
                act.wait_ge(raw_in[n], 64 if n == 0 else 16)
                nc.scalar.copy(w_hi[:, n], w_raw[:, n]).then_inc(hi_ready, 1)

            for src, lo, n, f, d in ((B_CTX, 0, TC, ctx_full, ctx_drained), (0, TC, HALF, full[0], drained[0]),
                                     (1, TC + HALF, HALF, full[1], drained[1])):
                act.wait_ge(f, at(1))
                nc.scalar.copy(g_i[:, lo:lo + n], ps[0:64, src, 0:n])
                nc.scalar.copy(g_f[:, lo:lo + n], ps[64:128, src, 0:n]).then_inc(d, 1)
            hi_split(Tile(2))
            act.wait_ge(row_v, at(ROW_ABS))
            nc.scalar.activation(g_e[:, :], g_e[:, :], ACT.Exp).then_inc(row_a, 1)
            act.wait_ge(row_a, at(ROW_EXP))
            nc.scalar.activation(g_s[:, :], g_e[:, :], ACT.Ln, bias=1.0).then_inc(row_a, 1)

            def drain_half(i, k, half, dst, waits=()):
                n = N_HEAD + 4 * i + k
                act.wait_ge(full[half], at(n + 1))
                for s, c in waits:
                    act.wait_ge(s, at(c))
                nc.scalar.copy(dst, ps[:, half, :]).then_inc(drained[half], 1)

            def drain_ctx(i, k, dst, waits=()):
                act.wait_ge(ctx_full, at(2 * i + k + 1))
                for s, c in waits:
                    act.wait_ge(s, at(c))
                nc.scalar.copy(dst, ps[:, B_CTX, 0:TC]).then_inc(ctx_drained, 1)

            def o_half(i, half):
                act.wait_ge(full[half], at(N_HEAD + 4 * i + 4))
                act.wait_ge(k_ready, at(i + 1))
                nc.scalar.activation(conv[:, half * HALF:(half + 1) * HALF], ps[:, half, :], ACT.Tanh,
                                     scale=0.5).then_inc(drained[half], 1)

            def tanh_q(i):
                act.wait_ge(conv_ready, at(2 * i + 1))
                act.wait_ge(s_full, at(2 * i))
                act.wait_ge(qs_ready, at(2 * i))
                nc.scalar.activation(q_t[:, :], conv[:, TC:TA], ACT.Tanh, scale=0.5).then_inc(tanh_ready, 1)

            def tanh_k(i):
                act.wait_ge(conv_ready, at(2 * i + 2))
                act.wait_ge(turned, at(5 * i))
                act.wait_ge(s_full, at(2 * i))
                nc.scalar.activation(k_t[:, :], conv[:, :], ACT.Tanh, scale=0.5).then_inc(tanh_ready, 1)

            def q_half(i, half):
                drain_half(i, 0, half, raw[:, 1 + half * HALF:1 + (half + 1) * HALF], ((conv_ready, 2 * i),))

            def k_half(i, half):
                drain_half(i, 1, half, raw[:, 1 + half * HALF:1 + (half + 1) * HALF], ((conv_ready, 2 * i + 1),))

            def k_ctx(i):
                drain_ctx(i, 1, raw[:, T + 3:T + 3 + TC], ((conv_ready, 2 * i),))

            def v_half(i, half):
                drain_half(i, 2, half, v_t[:, TC + half * HALF:TC + (half + 1) * HALF], ((turned, 5 * i),))

            def v_ctx(i):
                drain_ctx(i, 2, v_t[:, 0:TC], ((turned, 5 * i),))

            def kv_tokens(g, j):
                act.wait_ge(turned, at(5 * g + j + 1))
                if j == 0:
                    act.wait_ge(g_full, at(6 * g))
                    act.wait_ge(o_full, at(6 * g))
                    act.wait_ge(row_cols, at(3))
                    act.wait_ge(setup, at(N_SETUP))
                src = ps[:, B_T, :].rearrange("p (c n) -> p c n", n=P)
                if j < 2:
                    nc.scalar.copy(k_tok[:, NCC + 4 * j:NCC + 4 * j + 4, :], src).then_inc(tok_ready, 1)
                elif j < 4:
                    nc.scalar.copy(v_tok[:, NCC + 4 * j - 8:NCC + 4 * j - 4, 0:P], src).then_inc(tok_ready, 1)
                else:
                    nc.scalar.copy(k_tok[:, 0:NCC, :], src[:, 0:NCC, :])
                    nc.scalar.copy(v_tok[:, 0:NCC, 0:P], src[:, NCC:2 * NCC, :]).then_inc(tok_ready, 1)

            def exp_weights(g, d):
                act.wait_ge(expo_ready, at(2 * g + d + 1))
                nc.scalar.activation(wgt[:, :, :], wgt[:, :, :], ACT.Exp, scale=-1.0).then_inc(wexp_ready, 1)

            def denominators(g, d, j):
                m = len(OUT[d][j])
                l0 = OUT[d][j][0]
                act.wait_ge(o_full, at(6 * g + 3 * d + j + 1))
                act.wait_ge(h_ready, at(6 * g + 3 * d))
                nc.scalar.activation(tiny[:, 8 * d + l0:8 * d + l0 + m],
                                     ps[:, B_O, 0:m * VW].rearrange("p (c n) -> p c n", n=VW)[:, :, P],
                                     ACT.Abs).then_inc(den_ready, 1)

            def squares(g):
                act.wait_ge(h_ready, at(6 * g + 6))
                act.wait_ge(pt_ready, at(4 * g + 4))
                nc.scalar.activation(wgt[:, :, :], h_tok[:, :, :], ACT.Square).then_inc(sq_ready, 1)

            def head_tile(i, k):
                return Tile(N_HEAD + k, 4, i)

            q_half(0, 0); q_half(0, 1); hi_split(head_tile(0, 2))
            tanh_q(0); k_ctx(0); k_half(0, 0); k_half(0, 1); hi_split(head_tile(0, 3))
            tanh_k(0); v_ctx(0); v_half(0, 0); v_half(0, 1); hi_split(head_tile(0, 4))
            o_half(0, 0); o_half(0, 1); hi_split(head_tile(0, 5))
            for row, need, scale in ((g_f, ROW_AX, 1.0), (g_e, ROW_WX, 1.0), (g_s, ROW_EX, -1.0)):
                act.wait_ge(row_v, at(need))
                nc.scalar.activation(row[:, :], row[:, :], ACT.Exp, scale=scale).then_inc(row_a, 1)

            with act.Fori(1, H) as i:
                g = i - 1
                kv_tokens(g, 0); q_half(i, 0); kv_tokens(g, 1); exp_weights(g, 0)
                kv_tokens(g, 2); kv_tokens(g, 3); q_half(i, 1); hi_split(head_tile(i, 2))
                kv_tokens(g, 4); tanh_q(i); k_ctx(i); exp_weights(g, 1)
                k_half(i, 0); k_half(i, 1); hi_split(head_tile(i, 3))
                denominators(g, 0, 0); tanh_k(i); v_ctx(i); denominators(g, 0, 1); v_half(i, 0)
                denominators(g, 0, 2); v_half(i, 1); hi_split(head_tile(i, 4))
                denominators(g, 1, 0); o_half(i, 0); denominators(g, 1, 1); denominators(g, 1, 2)
                squares(g); o_half(i, 1); hi_split(head_tile(i, 5))

            def c_half(half, n):
                act.wait_ge(full[half], at(n + 1))
                act.wait_ge(drained[1], at(n - 1))
                nc.scalar.copy(q_t[:, half * HALF:(half + 1) * HALF], ps[:, half, :]).then_inc(drained[half], 1)

            def conv_tile(k, i=0):
                return Tile(N_CONV + k, 6, i)

            g = H - 1
            kv_tokens(g, 0); kv_tokens(g, 1); exp_weights(g, 0)
            act.wait_ge(qs_ready, at(2 * H)); c_half(0, N_CONV)
            kv_tokens(g, 2); kv_tokens(g, 3)
            c_half(1, N_CONV); hi_split(conv_tile(2)); kv_tokens(g, 4); exp_weights(g, 1)
            hi_split(conv_tile(3))
            denominators(g, 0, 0); denominators(g, 0, 1); denominators(g, 0, 2)
            hi_split(conv_tile(4))
            denominators(g, 1, 0); c_half(0, N_CONV + 3); c_half(1, N_CONV + 3); hi_split(conv_tile(5))
            denominators(g, 1, 1); denominators(g, 1, 2); squares(g)
            hi_split(conv_tile(6)); hi_split(conv_tile(7))
            with act.Fori(1, KT // 2) as i:
                for k in range(6):
                    if k % 3 == 0:
                        for half in range(2):
                            c_half(half, N_CONV + 6 * i + k)
                    hi_split(conv_tile(k + 2, i))

            def load_branch(stage):
                act.wait_ge(full[1], at((N_MIX_M, N_MIX_C)[stage]))
                act.wait_ge(drained[1], at((N_MIX_M, N_MIX_C)[stage]))
                for k in range(KT):
                    act.wait_ge(br_in[k % 2], 16 * (4 * stage + k // 2 + 1))
                    nc.scalar.copy(br_hi[:, k, :], b_raw[:, k % 2, :]).then_inc(br_hi_ready, 1)

            for stage, base in enumerate((N_MIX_M, N_MIX_C)):
                def gates(i):
                    t = Tile(base, 2, i)
                    for half in range(2):
                        act.wait_ge(full[half], at(t.n + 1))
                        act.wait_ge(drained[1], at(t.n))
                        nc.scalar.activation(gth[:, half * HALF:(half + 1) * HALF], ps[:, half, :], ACT.Tanh,
                                             scale=0.5).then_inc(drained[half], 1)
                    hi_split(t.ahead(2))
                load_branch(stage)
                with act.Fori(0, KT - stage) as i:
                    gates(i)
                    hi_split(Tile(base + 1, 2, i).ahead(2))

            def merged(j):
                nc.scalar.mul(op_hi[:, j, :], res[:, j, :], 0.5).then_inc(act_hi, 1)
            gates(KT - 1)
            act.wait_ge(mix_ready, at(2 * KT - 2))
            for j in range(KT - 1):
                merged(j)
            hi_split(Tile(N_WO + 1))
            act.wait_ge(mix_ready, at(2 * KT))
            merged(KT - 1)

            def residual(j):
                act.wait_ge(xj_turned, at(j + 1))
                act.wait_ge(act_lo, at(4 * KT))
                nc.scalar.copy(res[:, ds(j, 1), :].rearrange("p a (b n) -> p (a b) n", n=HALF),
                               ps[:, B_S:B_S + 2, :]).then_inc(xres_ready, 1)

            with act.Fori(0, KT // 2) as i:
                for k in range(2):
                    residual(2 * i + k)
                    hi_split(Tile(N_WO + k, 2, i).ahead(2))

            for k in range(KT):
                act.wait_ge(ut_ready, at(k + 1))
                if k >= 1:
                    act.wait_ge(act_lo, at(4 * KT + k))
                nc.scalar.activation(u_h[:, :], u_t[:, k % 2, :], ACT.Identity, scale=gain[:, 2, k:k + 1],
                                     bias=mod[:, 3 * KT + k, 0:1]).then_inc(uh_ready, 1)
                act.wait_ge(uh_ready, at(k + 1))
                nc.scalar.copy(op_hi[:, k, :], u_h[:, :]).then_inc(act_hi, 1)

            n, done = N_FFN, 0
            act.wait_ge(pad_ready, at(1))
            for group, size in enumerate(GROUPS):
                with act.Fori(0, size) as i:
                    f = done + i
                    ta, tg = Tile(n, 2, i), Tile(n + 1, 2, i)
                    for half in range(2):
                        act.wait_ge(full[half], at(ta.n + 1))
                        act.wait_ge(cv_ready, at(f))
                        r0 = 1 + half * ROWS // 2
                        nc.scalar.copy(a_pad[:, r0:r0 + ROWS // 2, 1:1 + GRID],
                                       ps[:, half, :].rearrange("p (r w) -> p r w", w=GRID)).then_inc(drained[half], 1)
                    hi_split(ta.ahead(2))
                    for half in range(2):
                        act.wait_ge(full[half], at(tg.n + 1))
                        act.wait_ge(ul_ready, at(f))
                        nc.scalar.copy(gv[:, half * HALF:(half + 1) * HALF], ps[:, half, :]).then_inc(drained[half], 1)
                    hi_split(tg.ahead(2))
                    act.wait_ge(cv_ready, at(f + 1))
                    nc.scalar.activation(cv[:, :], cv[:, :], ACT.Gelu_apprx_tanh).then_inc(gelu_ready, 1)
                    act.wait_ge(u_ready, at(f + 1))
                    act.wait_ge(full[1], at(n))
                    nc.scalar.copy(br_hi[:, ds(i, 1), :], gv[:, :]).then_inc(uh_ready, 1)
                n += 2 * size
                done += size
                last = group == len(GROUPS) - 1
                with act.Fori(0, KT // 2 - last) as i:
                    for k in range(2):
                        hi_split(Tile(n + k, 2, i).ahead(2))
                n += KT

            for l in range(NL):
                act.wait_ge(f_turned, at(l + 1))
                act.wait_ge(f_sum, at(l))
                nc.scalar.activation(junk[:, :], ps[:, 2 * (l % 4):2 * (l % 4) + 2, :].rearrange("p b n -> p (b n)"),
                                     ACT.Square, accum_out=st3[:, l:l + 1]).then_inc(f_sum, 1)

        @block.vector
        def _(dve):
            vec = nc.vector
            chain = Chain(dve, v_step)

            def lo_split(t):
                dve.wait_ge(hi_ready, at(t.n + 1))
                vec.tensor_tensor(w_lo[:, t.slot], w_raw[:, t.slot], w_hi[:, t.slot].bitcast(F32),
                                  ALU.subtract).then_inc(lo_ready, 1)

            for r, n in enumerate((120, 86, 128, 70)):
                dve.wait_ge(par_turned, at(4))
                vec.tensor_copy(par[:, r * P:r * P + n], ps[:, B_S, r * P:r * P + n]).then_inc(par_ready, 1)
            dve.wait_ge(par_ready, at(4))
            chain.step(vec.tensor_scalar(gate5[:, :], par[:, MNG:MNG + KT], 0.5, None, ALU.mult))
            dve.wait_ge(mod_done, at(NAL1))

            def modulation(bank, j0, j1):
                return vec.tensor_tensor(mod[:, j0:j1, :], ps[:, bank, 2 * j0:2 * j1].rearrange("p (j v) -> p j v", v=2),
                                         par[:, ADA_B + j0:ADA_B + j1].unsqueeze(2).broadcast_to([P, j1 - j0, 2]), ALU.add)
            modulation(B_O, 0, 2 * KT).then_inc(mod_ready, 1)
            dve.wait_ge(mod_ready, at(1))
            for v in range(2):
                vec.scalar_tensor_tensor(out=gain[:, v, :], in0=mod[:, KT:2 * KT, v], scalar=1.0,
                                         in1=par[:, N1G:N1G + KT], op0=ALU.add, op1=ALU.mult).then_inc(mod_ready, 1)

            def scale_tokens(b):
                dve.wait_ge(rms, at(b + 1))
                for j in range(4 if b < 2 else NCC):
                    vec.tensor_scalar(x_in[:, b % 2, j, :], x_in[:, b % 2, j, :],
                                      stat[:, 2, 4 * b + j:4 * b + j + 1], None, ALU.mult).then_inc(x_scaled, 1)

            def low_parts(b):
                n = HALF if b < 2 else TC
                hi, lo = ((a[:, :, b * HALF:(b + 1) * HALF] for a in op) if b < 2 else ctx_op)
                for k in range(KT):
                    t = b * KT + k
                    dve.wait_ge(act_hi, at(t + 1))
                    vec.tensor_tensor(lo[:, k, :], ht[:, t % 2, 0:n], hi[:, k, :].bitcast(F32),
                                      ALU.subtract).then_inc(act_lo, 1)

            scale_tokens(0)
            scale_tokens(1)
            low_parts(0)
            scale_tokens(2)
            low_parts(1)
            low_parts(2)
            lo_split(Tile(0))
            lo_split(Tile(1))

            def row(ins):
                ins.then_inc(row_v, 1)
                rows_done[0] += 1
                dve.wait_ge(row_v, at(rows_done[0]))
            rows_done = [0]
            F, B = slice(0, 32), slice(32, 64)

            dve.wait_ge(ctx_drained, at(1))
            dve.wait_ge(drained[0], at(1))
            dve.wait_ge(drained[1], at(1))
            dve.wait_ge(gb_in, 64)
            row(vec.tensor_scalar(g_f[:, :], g_f[:, :], gbias[:, 1:2], None, ALU.add))
            row(vec.scalar_tensor_tensor(out=g_e[:, :], in0=g_f[:, :], scalar=-1.0, in1=g_f[:, :],
                                         op0=ALU.mult, op1=ALU.min))
            lo_split(Tile(2))
            dve.wait_ge(row_a, at(ROW_EXP))
            row(vec.tensor_scalar(g_b[:, :], g_e[:, :], 1.0, None, ALU.add))
            row(vec.scalar_tensor_tensor(out=g_b[:, :], in0=g_b[:, :], scalar=-1.0, in1=g_e[:, :],
                                         op0=ALU.add, op1=ALU.subtract))
            dve.wait_ge(row_a, at(ROW_LN))
            row(vec.tensor_scalar(g_e[:, :], g_e[:, :], -0.5, 1.0, ALU.mult, ALU.add))
            row(vec.tensor_tensor(g_b[:, :], g_b[:, :], g_e[:, :], ALU.mult))
            row(vec.tensor_tensor(g_s[:, :], g_s[:, :], g_b[:, :], ALU.subtract))
            row(vec.scalar_tensor_tensor(out=g_f[:, :], in0=g_f[:, :], scalar=0.0, in1=g_s[:, :],
                                         op0=ALU.min, op1=ALU.subtract))

            def row_sums():
                dve.wait_ge(setup, at(14))
                row(vec.tensor_tensor_scan(g_b[F, :], g_r[F, :], g_f[F, :], 0.0, ALU.mult, ALU.add))
                row(vec.tensor_tensor_scan(g_b[B, ::-1], g_r[B, ::-1], g_f[B, ::-1], 0.0, ALU.mult, ALU.add))
                row(vec.scalar_tensor_tensor(out=g_i[:, :], in0=g_i[:, :], scalar=gbias[:, 0:1], in1=g_b[:, :],
                                             op0=ALU.add, op1=ALU.subtract))

            def row_maxima():
                row(vec.memset(g_d[:, :], 0.0))
                row(vec.tensor_copy(g_d[F, CH::CH], g_b[F, CH - 1:TA - CH:CH]))
                row(vec.tensor_copy(g_d[B, CH - 1:CH], g_b[B, CH:CH + 1]))
                row(vec.tensor_copy(g_d[B, TC + CH - 1:TA - CH:CH], g_b[B, TC + CH::CH]))
                row(vec.tensor_copy(g_d[B, TA - 1:TA], g_b[B, 0:1]))
                row(vec.tensor_tensor_scan(g_m[F, :], g_d[F, :], g_i[F, :], NEG, ALU.add, ALU.max))
                row(vec.tensor_tensor_scan(g_m[B, TC - 1::-1], g_d[B, TC - 1::-1], g_i[B, TC - 1::-1], NEG,
                                           ALU.add, ALU.max))
                row(vec.tensor_tensor_scan(g_m[B, TA - 1:TC - 1:-1], g_d[B, TA - 1:TC - 1:-1],
                                           g_i[B, TA - 1:TC - 1:-1], g_m[B, 0:1], ALU.add, ALU.max))

            def row_factors():
                row(vec.memset(mp[:, :, :], NEG))
                row(vec.tensor_tensor(mp[F, 0, 1:NC], g_m[F, CH - 1:TA - CH:CH], g_d[F, CH::CH], ALU.add))
                row(vec.tensor_tensor(mp[B, 0, 0:1], g_m[B, CH:CH + 1], g_d[B, CH - 1:CH], ALU.add))
                row(vec.tensor_tensor(mp[B, 0, NCC:NC - 1], g_m[B, TC + CH::CH], g_d[B, TC + CH - 1:TA - CH:CH],
                                      ALU.add))
                row(vec.tensor_tensor(mp[B, 0, NC - 1:NC], g_m[B, 0:1], g_d[B, TA - 1:TA], ALU.add))
                row(vec.tensor_copy(mp[F, 1, :], g_m[F, CH - 1::CH]))
                row(vec.tensor_copy(mp[B, 1, :], g_m[B, 0::CH]))

                def chunks(a):
                    return a[:, :].rearrange("p (c n) -> p c n", n=CH)

                def ends(v):
                    return mp[:, v, :].unsqueeze(2).broadcast_to([64, NC, CH])
                row(vec.tensor_tensor(chunks(g_f), ends(0), chunks(g_m), ALU.subtract))
                row(vec.tensor_tensor(chunks(g_e), chunks(g_i), ends(1), ALU.subtract))
                row(vec.tensor_tensor(g_s[:, :], g_b[:, :], g_m[:, :], ALU.add))
                row(vec.tensor_scalar(g_s[:, :], g_s[:, :], -EXP_MAX, None, ALU.max))

            def conv3(src, dst, n, w, b, last):
                chain.step(vec.tensor_scalar(dst, src[:, 1:1 + n], w(1), b, ALU.mult, ALU.add))
                chain.step(vec.scalar_tensor_tensor(out=dst, in0=src[:, 0:n], scalar=w(0), in1=dst,
                                                    op0=ALU.mult, op1=ALU.add))
                ins = vec.scalar_tensor_tensor(out=dst, in0=src[:, 2:2 + n], scalar=w(2), in1=dst,
                                               op0=ALU.mult, op1=ALU.add)
                ins.then_inc(conv_ready, 1) if last else chain.step(ins)

            def qk_conv(i, k, n):
                dve.wait_ge(drained[0], at(n + 1))
                dve.wait_ge(drained[1], at(n + 1))
                dve.wait_ge(setup, at(17))

                def w(tap):
                    return par[:, ds(i + (QKW + 16 * tap + 8 * k), 1)]
                b = par[:, ds(i + (QKB + 8 * k), 1)]
                if k:
                    dve.wait_ge(ctx_drained, at(2 * i + 2))
                    conv3(raw[:, T + 2:], conv[:, 0:TC], TC, w, b, False)
                conv3(raw, conv[:, TC:TA], T, w, b, True)

            def q_silu(i):
                dve.wait_ge(tanh_ready, at(2 * i + 1))
                vec.scalar_tensor_tensor(out=q_t[:, :], in0=q_t[:, :], scalar=1.0, in1=conv[:, TC:TA],
                                         op0=ALU.add, op1=ALU.mult).then_inc(q_ready, 1)
                dve.wait_ge(q_ready, at(i + 1))

            def k_silu(i):
                dve.wait_ge(tanh_ready, at(2 * i + 2))
                vec.scalar_tensor_tensor(out=k_t[:, :], in0=k_t[:, :], scalar=1.0, in1=conv[:, :],
                                         op0=ALU.add, op1=ALU.mult).then_inc(k_ready, 1)

            def o_gate(i, n):
                dve.wait_ge(drained[0], at(n + 1))
                dve.wait_ge(drained[1], at(n + 1))
                dve.wait_ge(at_ready, at(2 * i))
                vec.tensor_scalar(og[:, :], conv[:, 0:T], 1.0, None, ALU.add).then_inc(og_ready, 1)
                dve.wait_ge(og_ready, at(i + 1))

            def col(q, g, d, c0, c1, width):
                return cols[:, q, c0:c1, d, ds(g, 1)].broadcast_to([P, c1 - c0, width])

            def exponents(g, d):
                if d == 0:
                    dve.wait_ge(bc_in, 64 * (g + 1))
                    dve.wait_ge(row_cols, at(3))
                else:
                    dve.wait_ge(pt_ready, at(4 * g + 2))
                mask = (late, early)[d][:, :].unsqueeze(1).broadcast_to([P, NL, CH])
                chain.step(vec.tensor_tensor(wgt[:, :, :], m_bc[:, d, :].rearrange("p (c n) -> p c n", n=CH),
                                             col(0, g, d, NCC, NC, CH), ALU.subtract))
                vec.tensor_tensor(wgt[:, :, :], wgt[:, :, :], mask, ALU.max).then_inc(expo_ready, 1)

            def scaled_queries(g, d):
                dve.wait_ge(q_ready, at(g + 1))
                dve.wait_ge(o_full, at(6 * g))
                vec.scalar_tensor_tensor(out=qs[:, d, :], in0=q_t[:, :], scalar=0.5, in1=a_bc[:, d, TC:TA],
                                         op0=ALU.mult, op1=ALU.mult).then_inc(qs_ready, 1)

            def weighted_scores(g, d):
                dve.wait_ge(wexp_ready, at(2 * g + d + 1))
                if d == 0:
                    dve.wait_ge(a_stored, at(g))
                else:
                    dve.wait_ge(o_full, at(6 * g + 3))
                for j in range(2):
                    dve.wait_ge(s_full, at(2 * g + j + 1))
                    vec.scalar_tensor_tensor(out=pt[:, 4 * j:4 * j + 4, :], in0=ps[:, B_S + j, :].rearrange("p (c n) -> p c n", n=CH),
                                             scalar=SCALE / 4, in1=wgt[:, 4 * j:4 * j + 4, :],
                                             op0=ALU.mult, op1=ALU.mult).then_inc(pt_ready, 1)

            def weighted_values(g, d):
                dve.wait_ge(tok_ready, at(5 * g + 5))
                dve.wait_ge(g_full, at(6 * g + 3 * d))
                vec.scalar_tensor_tensor(out=vw[:, :, :], in0=v_tok[:, :, :], scalar=SCALE / 2,
                                         in1=col(1, g, d, 0, NC, VW), op0=ALU.mult,
                                         op1=ALU.mult).then_inc(vw_ready, 1)

            def carry(g, d, j):
                dve.wait_ge(g_full, at(6 * g + 3 * d + j + 1))
                dve.wait_ge(o_full, at(6 * g))
                for q in range(3):
                    k = 3 * j + q
                    add = ps[:, B_G, q * VW:(q + 1) * VW]
                    if k == 0:
                        ins = vec.tensor_copy(state[:, d, 0, :], add)
                    else:
                        ch = SCAN[d][k]
                        end = ch * CH + (CH - 1 if d == 0 else 0)
                        ins = vec.scalar_tensor_tensor(out=state[:, d, k, :], in0=state[:, d, k - 1, :],
                                                       scalar=a_bc[:, d, end:end + 1], in1=add,
                                                       op0=ALU.mult, op1=ALU.add)
                    if q < 2:
                        chain.step(ins)
                ins.then_inc(state_ready, 1)
                dve.wait_ge(state_ready, at(6 * g + 3 * d + j + 1))

            def heads_out(g, d, j):
                ls = OUT[d][j]
                m, l0 = len(ls), ls[0]
                dve.wait_ge(den_ready, at(6 * g + 3 * d + j + 1))
                dve.wait_ge(h_turned, at(2 * g))
                den, top, rec = (tiny[:, 16 * q + 8 * d + l0:16 * q + 8 * d + l0 + m] for q in range(3))
                chain.step(vec.tensor_tensor(top, den, cols[:, 2, NCC + l0:NCC + l0 + m, d, ds(g, 1)].rearrange(
                    "p c a -> p (c a)"), ALU.max))
                chain.step(vec.reciprocal(rec, top))
                num = ps[:, B_O, 0:m * VW].rearrange("p (c n) -> p c n", n=VW)[:, :, 0:P]
                rec = rec.unsqueeze(2).broadcast_to([P, m, P])
                if d == 0:
                    vec.tensor_tensor(h_tok[:, l0:l0 + m, :], num, rec, ALU.mult).then_inc(h_ready, 1)
                else:
                    chain.step(vec.tensor_tensor(h_tmp[:, 0:m, :], num, rec, ALU.mult))
                    dve.wait_ge(h_ready, at(6 * g + 3))
                    vec.tensor_tensor(h_tok[:, l0:l0 + m, :], h_tok[:, l0:l0 + m, :], h_tmp[:, 0:m, :],
                                      ALU.add).then_inc(h_ready, 1)

            def head_norm(g):
                dve.wait_ge(sq_ready, at(g + 1))
                dve.wait_ge(rn_ready, at(g))
                chain.step(vec.tensor_reduce(tiny[:, 48:56], wgt[:, :, :], AX_X, ALU.add))
                vec.tensor_scalar(tiny[:, 56:64], tiny[:, 48:56], 1.0 / P, EPS, ALU.mult, ALU.add).then_inc(ss_ready, 1)
                dve.wait_ge(rn_ready, at(g + 1))
                vec.tensor_tensor(h_tok[:, :, :], h_tok[:, :, :], tiny[:, 64:72].unsqueeze(2).broadcast_to([P, NL, P]),
                                  ALU.mult).then_inc(hn_ready, 1)

            def head_result(g):
                dve.wait_ge(og_ready, at(g + 1))
                dve.wait_ge(o_full, at(6 * g + 6))
                for j in range(2):
                    dve.wait_ge(h_turned, at(2 * g + j + 1))
                    vec.scalar_tensor_tensor(out=pt[:, 4 * j:4 * j + 4, :].rearrange("p c n -> p (c n)"),
                                             in0=ps[:, B_T, :], scalar=gate5[:, ds(g, 1)],
                                             in1=og[:, j * HALF:(j + 1) * HALF], op0=ALU.mult,
                                             op1=ALU.mult).then_inc(at_ready, 1)

            def head_tile(i, k):
                return Tile(N_HEAD + k, 4, i)

            lo_split(head_tile(0, 2))
            qk_conv(0, 0, N_HEAD); q_silu(0)
            row_sums()
            lo_split(head_tile(0, 3))
            qk_conv(0, 1, N_HEAD + 1); k_silu(0)
            row_maxima()
            lo_split(head_tile(0, 4))
            row_factors()
            dve.wait_ge(k_ready, at(1))
            o_gate(0, N_HEAD + 3)
            lo_split(head_tile(0, 5))
            dve.wait_ge(mod_done, at(NAL))
            modulation(B_G, 2 * KT, 6 * KT).then_inc(mod_ready, 1)
            dve.wait_ge(mod_ready, at(4))
            vec.scalar_tensor_tensor(out=gain[:, 2, :], in0=mod[:, 4 * KT:5 * KT, 0], scalar=1.0,
                                     in1=par[:, N2G:N2G + KT], op0=ALU.add, op1=ALU.mult).then_inc(mod_ready, 1)
            for q in range(3):
                dve.wait_ge(row_turned, at(q + 1))
                src = ps[:, B_S:B_S + 2, :].rearrange("p b n -> p (b n)")[:, 0:64 * NC].rearrange(
                    "p (c d h) -> p c d h", d=2, h=32)[:, :, :, 0:H]
                vec.tensor_copy(cols[:, q], src).then_inc(row_cols, 1)

            with dve.Fori(1, H) as i:
                g = i - 1
                chain.enter(i, 1, V_HEAD)
                exponents(g, 0); scaled_queries(g, 0); scaled_queries(g, 1); weighted_scores(g, 0)
                exponents(g, 1); lo_split(head_tile(i, 2))
                qk_conv(i, 0, N_HEAD + 4 * i); weighted_values(g, 0); q_silu(i)
                carry(g, 0, 0); carry(g, 0, 1); carry(g, 0, 2); weighted_values(g, 1)
                lo_split(head_tile(i, 3)); qk_conv(i, 1, N_HEAD + 4 * i + 1)
                heads_out(g, 0, 0); k_silu(i); heads_out(g, 0, 1); heads_out(g, 0, 2)
                weighted_scores(g, 1); carry(g, 1, 0); carry(g, 1, 1); carry(g, 1, 2)
                lo_split(head_tile(i, 4))
                heads_out(g, 1, 0); heads_out(g, 1, 1); heads_out(g, 1, 2)
                head_norm(g); head_result(g)
                o_gate(i, N_HEAD + 4 * i + 3); lo_split(head_tile(i, 5))
                chain.leave(H - 1)

            def conv_tile(k, i=0):
                return Tile(N_CONV + k, 6, i)

            def c_times_x(half, n):
                dve.wait_ge(full[half], at(n + 1))
                dve.wait_ge(drained[half], at(n))
                vec.tensor_tensor(raw[:, 1 + half * HALF:1 + (half + 1) * HALF], q_t[:, half * HALF:(half + 1) * HALF],
                                  ps[:, half, :], ALU.mult).then_inc(drained[half], 1)

            def sc_conv(j, n):
                dve.wait_ge(drained[0], at(n + 1))
                dve.wait_ge(drained[1], at(n + 1))
                b = par[:, ds(j + SCB, 1)]
                dst = conv[:, TC:TA]
                chain.step(vec.tensor_scalar(dst, raw[:, 1:1 + T], par[:, ds(j + SCW + 8, 1)], b, ALU.mult, ALU.add))
                for tap in (0, 2):
                    chain.step(vec.scalar_tensor_tensor(out=dst, in0=raw[:, tap:tap + T], scalar=par[:, ds(j + SCW + 8 * tap, 1)],
                                                        in1=dst, op0=ALU.mult, op1=ALU.add))

            def times_b(j, half, n):
                dve.wait_ge(full[half], at(n + 1))
                dve.wait_ge(z_stored, at(j))
                vec.tensor_tensor(k_t[:, half * HALF:(half + 1) * HALF], conv[:, TC + half * HALF:TC + (half + 1) * HALF],
                                  ps[:, half, :], ALU.mult).then_inc(drained[half], 1)

            g, n = H - 1, N_CONV
            exponents(g, 0); scaled_queries(g, 0); scaled_queries(g, 1); weighted_scores(g, 0)
            exponents(g, 1); lo_split(conv_tile(2)); weighted_values(g, 0)
            c_times_x(0, n + 1); carry(g, 0, 0); carry(g, 0, 1); c_times_x(1, n + 1); lo_split(conv_tile(3))
            sc_conv(0, n + 1); carry(g, 0, 2); weighted_values(g, 1)
            heads_out(g, 0, 0); heads_out(g, 0, 1)
            dve.wait_ge(turned, at(5 * H))
            times_b(0, 0, n + 2); heads_out(g, 0, 2); weighted_scores(g, 1); carry(g, 1, 0); times_b(0, 1, n + 2)
            lo_split(conv_tile(4)); carry(g, 1, 1); carry(g, 1, 2)
            heads_out(g, 1, 0); lo_split(conv_tile(5)); heads_out(g, 1, 1); heads_out(g, 1, 2)
            c_times_x(0, n + 4); head_norm(g); head_result(g); c_times_x(1, n + 4); lo_split(conv_tile(6))
            sc_conv(1, n + 4); times_b(1, 0, n + 5); times_b(1, 1, n + 5); lo_split(conv_tile(7))
            with dve.Fori(1, KT // 2) as i:
                chain.enter(i, 1, 6)
                for k in range(2):
                    j, n = 2 * i + k, N_CONV + 3 * k + 6 * i
                    lo_split(conv_tile(3 * k + 2, i))
                    c_times_x(0, n + 1); c_times_x(1, n + 1); lo_split(conv_tile(3 * k + 3, i))
                    sc_conv(j, n + 1)
                    times_b(j, 0, n + 2); times_b(j, 1, n + 2); lo_split(conv_tile(3 * k + 4, i))
                chain.leave(KT // 2 - 1)

            def mixed(stage, j, t):
                for half in range(2):
                    sl = slice(half * HALF, (half + 1) * HALF)
                    dve.wait_ge(full[half], at(t.n + 1))
                    dve.wait_ge(drained[half], at(t.n))
                    dst = res[:, ds(j, 1), sl].rearrange("p a n -> p (a n)")
                    if stage:
                        dve.wait_ge(mix_ready, at(2 * j + half))
                    vec.scalar_tensor_tensor(out=mtmp[:, sl] if stage else dst, in0=gth[:, sl], scalar=1.0,
                                             in1=ps[:, half, :], op0=ALU.add, op1=ALU.mult).then_inc(drained[half], 1)
                    if stage:
                        dve.wait_ge(drained[half], at(t.n + 1))
                        vec.tensor_tensor(dst, dst, mtmp[:, sl], ALU.add).then_inc(mix_ready, 1)

            for stage, base in enumerate((N_MIX_M, N_MIX_C)):
                for k in range(KT):
                    dve.wait_ge(br_hi_ready, at(KT * stage + k + 1))
                    vec.tensor_tensor(br_lo[:, k, :], b_raw[:, k % 2, :], br_hi[:, k, :].bitcast(F32),
                                      ALU.subtract).then_inc(br_lo_ready, 1)
                with dve.Fori(0, KT - stage) as i:
                    lo_split(Tile(base + 2, 2, i))
                    mixed(stage, i, Tile(base + 1, 2, i))
                    lo_split(Tile(base + 3, 2, i))

            def merged(j):
                dve.wait_ge(act_hi, at(3 * KT + j + 1))
                vec.scalar_tensor_tensor(out=op_lo[:, j, :], in0=res[:, j, :], scalar=0.5,
                                         in1=op_hi[:, j, :].bitcast(F32), op0=ALU.mult,
                                         op1=ALU.subtract).then_inc(act_lo, 1)
            lo_split(Tile(N_WO))
            for j in range(KT - 1):
                merged(j)
            mixed(1, KT - 1, Tile(N_WO - 1))
            lo_split(Tile(N_WO + 1))
            merged(KT - 1)

            dve.wait_ge(mod_ready, at(5))
            chain.step(vec.memset(sqx[:, :], 0.0))
            dve.sem_inc(sqx_ready, 1)
            with dve.Fori(0, KT // 2) as i:
                for k in range(2):
                    t = Tile(N_WO + k, 2, i)
                    dve.wait_ge(xres_ready, at(2 * i + k + 1))
                    for half in range(2):
                        dve.wait_ge(full[half], at(t.n + 1))
                        dst = res[:, ds(2 * i + k, 1), half * HALF:(half + 1) * HALF].rearrange("p a n -> p (a n)")
                        vec.scalar_tensor_tensor(out=dst, in0=ps[:, half, :], scalar=mod[:, ds(2 * i + (2 * KT + k), 1), 0],
                                                 in1=dst, op0=ALU.mult, op1=ALU.add).then_inc(drained[half], 1)
                    dve.wait_ge(drained[0], at(t.n + 1))
                    dve.wait_ge(drained[1], at(t.n + 1))
                    dve.wait_ge(stat_done, at(2 * i + k + 1))
                    tile_j = res[:, ds(2 * i + k, 1), :].rearrange("p a n -> p (a n)")
                    vec.tensor_tensor(sqx[:, :], tile_j, tile_j, ALU.mult).then_inc(sqx_ready, 1)
                    lo_split(t.ahead(2))

            dve.wait_ge(stat_done, at(KT + 1))
            vec.tensor_copy(st2[:, 0:NL], ps[:, B_O, 0:NL]).then_inc(n2_sum, 1)
            dve.wait_ge(n2_rms, at(1))
            vec.tensor_tensor(diag[:, :, :], ident[:, :].unsqueeze(1).broadcast_to([P, NL, P]),
                              st2[:, 16:16 + NL].unsqueeze(2).broadcast_to([P, NL, P]), ALU.mult).then_inc(n2_ready, 1)
            dve.wait_ge(bc2_done, at(1))

            def low(k):
                dve.wait_ge(act_hi, at(4 * KT + k + 1))
                vec.tensor_tensor(op_lo[:, k, :], u_h[:, :], op_hi[:, k, :].bitcast(F32), ALU.subtract).then_inc(act_lo, 1)
            for k in range(KT):
                if k >= 2:
                    dve.wait_ge(uh_ready, at(k - 1))
                vec.tensor_tensor(u_t[:, k % 2, :], res[:, k, :], ps[:, B_S:B_S + 2, :].rearrange("p b n -> p (b n)"),
                                  ALU.mult).then_inc(ut_ready, 1)
                if k:
                    low(k - 1)
            low(KT - 1)

            chain.step(vec.memset(a_pad[:, :, :], 0.0))
            dve.sem_inc(pad_ready, 1)
            n, done = N_FFN, 0
            out3 = cv[:, :].rearrange("p (r w) -> p r w", w=GRID)
            for group, size in enumerate(GROUPS):
                with dve.Fori(0, size) as i:
                    chain.enter(i, 0, 8)
                    f = done + i
                    ta, tg = Tile(n, 2, i), Tile(n + 1, 2, i)
                    lo_split(ta.ahead(2))
                    dve.wait_ge(drained[0], at(ta.n + 1))
                    dve.wait_ge(drained[1], at(ta.n + 1))
                    dve.wait_ge(ul_ready, at(f))
                    chain.step(vec.tensor_scalar(out3, a_pad[:, 1:1 + ROWS, 1:1 + GRID], par[:, ds(f + (FFW + 4 * FT), 1)],
                                                 par[:, ds(f + FFB, 1)], ALU.mult, ALU.add))
                    for tap in (0, 1, 2, 3, 5, 6, 7, 8):
                        r, w = tap // 3, tap % 3
                        ins = vec.scalar_tensor_tensor(out=out3, in0=a_pad[:, r:r + ROWS, w:w + GRID],
                                                       scalar=par[:, ds(f + (FFW + tap * FT), 1)], in1=out3,
                                                       op0=ALU.mult, op1=ALU.add)
                        if tap < 8:
                            chain.step(ins)
                    ins.then_inc(cv_ready, 1)
                    lo_split(tg.ahead(2))
                    dve.wait_ge(drained[0], at(tg.n + 1))
                    dve.wait_ge(drained[1], at(tg.n + 1))
                    dve.wait_ge(gelu_ready, at(f + 1))
                    vec.tensor_tensor(gv[:, :], cv[:, :], gv[:, :], ALU.mult).then_inc(u_ready, 1)
                    dve.wait_ge(uh_ready, at(KT + f + 1))
                    vec.tensor_tensor(br_lo[:, ds(i, 1), :].rearrange("p a n -> p (a n)"), gv[:, :],
                                      br_hi[:, ds(i, 1), :].rearrange("p a n -> p (a n)").bitcast(F32),
                                      ALU.subtract).then_inc(ul_ready, 1)
                    chain.leave(size)
                n += 2 * size
                done += size

                def down(j, t, more):
                    for half in range(2):
                        dve.wait_ge(full[half], at(t.n + 1))
                        dst = res[:, ds(j, 1), half * HALF:(half + 1) * HALF].rearrange("p a n -> p (a n)")
                        vec.scalar_tensor_tensor(out=dst, in0=ps[:, half, :], scalar=mod[:, ds(j + 5 * KT, 1), 0],
                                                 in1=dst, op0=ALU.mult, op1=ALU.add).then_inc(drained[half], 1)
                    if more:
                        lo_split(t.ahead(2))
                last = group == len(GROUPS) - 1
                with dve.Fori(0, KT // 2 - last) as i:
                    for k in range(2):
                        down(2 * i + k, Tile(n + k, 2, i), True)
                if last:
                    for k in range(2):
                        down(KT - 2 + k, Tile(n + KT - 2 + k), False)
                n += KT

            dve.wait_ge(gbc_in, 16)
            for l in range(NL):
                dve.wait_ge(f_rms, at(l + 1))
                if l >= 2:
                    dve.wait_ge(y_out[l % 2], 16 * (l // 2))
                vec.scalar_tensor_tensor(out=o_out[:, l % 2, :],
                                         in0=ps[:, 2 * (l % 4):2 * (l % 4) + 2, :].rearrange("p b n -> p (b n)"),
                                         scalar=st3[:, 16 + l:17 + l], in1=gbc[:, :], op0=ALU.mult,
                                         op1=ALU.mult).then_inc(f_ready, 1)

        @block.gpsimd
        def _(pool):
            for s_ in credited:
                pool.sem_inc(s_, 1)
            made = [0]

            def make(ins):
                ins.then_inc(setup, 1)
                made[0] += 1
                pool.wait_ge(setup, at(made[0]))

            gp = nc.gpsimd
            gp.dma_start(x_in[:, 0], x_tok[:, 0:4, :]).then_inc(x_loaded[0], 16)
            gp.dma_start(x_in[:, 1], x_tok[:, 4:8, :]).then_inc(x_loaded[1], 16)
            make(gp.memset(ident[:, :], 0.0))
            make(gp.affine_select(out=ident[:, :], in_=ident[:, :], compare_op=ALU.not_equal, fill=1.0, base=0,
                                  pattern=[[-1, P]], channel_multiplier=1))
            make(gp.memset(ones[:, :], 1.0))
            for tri, sign in ((late, 1), (early, -1)):
                make(gp.memset(tri[:, :], 0.0))
                make(gp.affine_select(out=tri[:, :], in_=tri[:, :], compare_op=ALU.is_ge, fill=BIG, base=0,
                                      pattern=[[sign, P]], channel_multiplier=-sign))
            make(gp.memset(power[:, :], -0.5))
            make(gp.memset(zero8[:, :], 0.0))
            make(gp.memset(gbias[:, :], 0.0))
            make(gp.memset(w_raw[:, 0], 0.0))

            def inverse_root(src, tmp, dst, scale, n, count):
                gp.tensor_scalar(tmp, src, scale, EPS, ALU.mult, ALU.add).then_inc(p_step, 1)
                pool.wait_ge(p_step, at(count))
                return gp.tensor_tensor(dst, tmp, power[:, 0:n], ALU.pow)

            for b in range(3):
                n = 4 if b < 2 else NCC
                if b == 2:
                    pool.wait_ge(x_turned, at(KT))
                    gp.dma_start(x_in[:, 0, 0:NCC], ctx_tok).then_inc(x_loaded[0], 16)
                pool.wait_ge(sumsq, at(4 * b + n))
                inverse_root(*(stat[:, q, 4 * b:4 * b + n] for q in range(3)), 1.0 / D, n, b + 1).then_inc(rms, 1)

            def ada_load(load):
                pool.wait_ge(mod_done, at(load - 1))
                gp.dma_start(aw[:, load % 2], adw[:, :, load * AC:(load + 1) * AC]).then_inc(ada_in[1][load % 2], 16)
            ada_load(NAL1)
            ada_load(NAL1 + 1)
            pool.wait_ge(act_lo, at(3 * KT))
            make(gp.memset(g_r[:, :], 1.0))
            make(gp.memset(g_r[0:32, 0::CH], 0.0))
            make(gp.memset(g_r[32:64, CH - 1::CH], 0.0))
            make(gp.memset(raw[:, 0:1], 0.0))
            make(gp.memset(raw[:, T + 1:T + 3], 0.0))
            make(gp.memset(raw[:, T + TC + 3:T + TC + 4], 0.0))
            for load in range(NAL1 + 2, NAL):
                ada_load(load)
            pool.wait_ge(row_v, at(ROW_M))
            for d in range(2):
                gp.dma_start(m_rows[d], g_m[32 * d:32 * d + H, :]).then_inc(gb_out, 16)
            pool.wait_ge(row_a, at(ROW_A))
            for d in range(2):
                gp.dma_start(a_rows[d], g_f[32 * d:32 * d + H, :]).then_inc(gb_out, 16)
            pool.wait_ge(gb_out, 64)
            pool.wait_ge(row_cols, at(3))
            pool.wait_ge(mod_ready, at(5))

            def broadcast_rows(g):
                for d in range(2):
                    gp.dma_start(m_bc[:, d, :], m_rows[d, ds(g, 1), TC:TA].broadcast_to([P, T])).then_inc(bc_in, 16)
                    gp.dma_start(a_bc[:, d, :], a_rows[d, ds(g, 1), :].broadcast_to([P, TA])).then_inc(bc_in, 16)
            broadcast_rows(0)
            make(gp.memset(v_tok[:, :, P:VW], 1.0))

            def head_norm(g):
                pool.wait_ge(ss_ready, at(g + 1))
                pool.wait_ge(hn_ready, at(g))
                gp.tensor_tensor(tiny[:, 64:72], tiny[:, 56:64], power[:, :], ALU.pow).then_inc(rn_ready, 1)

            def store_head(g):
                pool.wait_ge(at_ready, at(2 * g + 2))
                gp.dma_start(a_dram[ds(g, 1)].rearrange("a p n -> p (a n)"),
                             pt[:, :, :].rearrange("p c n -> p (c n)")).then_inc(a_out, 16)
                pool.wait_ge(a_out, 16 * (g + 1))
                pool.sem_inc(a_stored, 1)

            with pool.Fori(1, H) as i:
                pool.wait_ge(state_ready, at(6 * i))
                broadcast_rows(i)
                head_norm(i - 1)
                store_head(i - 1)

            def store_conv(j):
                n = N_CONV + 3 * j + 2
                pool.wait_ge(drained[0], at(n + 1))
                pool.wait_ge(drained[1], at(n + 1))
                gp.dma_start(z_dram[ds(j, 1)].rearrange("a p n -> p (a n)"), k_t[:, 0:T]).then_inc(z_out, 16)
                pool.wait_ge(z_out, 16 * (j + 1))
                pool.sem_inc(z_stored, 1)
            store_conv(0)
            head_norm(H - 1)
            store_head(H - 1)
            with pool.Fori(1, KT) as j:
                store_conv(j)

            for stage, src in enumerate((a_dram, z_dram)):
                for k in range(KT):
                    pool.wait_ge(br_lo_ready, at(KT * stage + k - 1 if k >= 2 or stage else 0))
                    gp.dma_start(b_raw[:, k % 2, :], src[k]).then_inc(br_in[k % 2], 16)

            pool.wait_ge(mix_ready, at(2 * KT))
            with pool.Fori(0, KT) as j:
                pool.wait_ge(xj_turned, at(j))
                gp.dma_start(x_j[:, :, :], x_tok[:, :, ds(j * P, P)]).then_inc(xj_in, 16)
            pool.wait_ge(n2_sum, at(1))
            inverse_root(*(st2[:, 8 * q:8 * q + NL] for q in range(3)), 1.0 / D, NL, 4).then_inc(n2_rms, 1)

            pool.wait_ge(ul_ready, at(FT))
            gp.dma_start(gbc[:, :], final_g.rearrange("(a d) -> a d", a=1).broadcast_to([P, D])).then_inc(gbc_in, 16)
            for l in range(NL):
                pool.wait_ge(f_sum, at(l + 1))
                inverse_root(*(st3[:, 8 * q + l:8 * q + l + 1] for q in range(3)), 1.0 / D, 1, 5 + l).then_inc(f_rms, 1)

        @block.sync
        def _(sp):
            def par_rows(row, src, n):
                sp.dma_start(prow[row % P:row % P + n, row // P, :], src).then_inc(par_in, 16)

            def tiles(v, pattern="(t p) -> t p"):
                return v.rearrange(pattern, p=P)
            par_rows(ADA_B, tiles(ada_b[0]), 48)
            par_rows(N1G, tiles(norm1_g[0]), KT)
            par_rows(N2G, tiles(norm2_g[0]), KT)
            par_rows(C_X, tiles(c[0]), KT)
            par_rows(C_CTX, tiles(c_ctx), KT)
            par_rows(MNG, tiles(mnorm_g[0]), KT)
            par_rows(SCB, tiles(sc_conv_b[0]), KT)
            par_rows(SCW, tiles(sc_conv_w[0], "a (t p) -> (a t) p"), 3 * KT)
            par_rows(QKW, tiles(qk_conv_w[0], "a (t p) -> (a t) p"), 6 * KT)
            par_rows(QKB, tiles(qk_conv_b[0]), 2 * KT)
            par_rows(FFB, tiles(ff_conv_b[0]), FT)
            ffw = tiles(ff_conv_w[0], "a b (t p) -> (a b t) p")
            par_rows(FFW, ffw[0:P], P)
            par_rows(FFW + P, ffw[P:9 * FT], 9 * FT - P)
            sp.wait_ge(setup, at(10))
            gb = gate_b[0].rearrange("(g h a) -> g h a", g=4, a=1)
            for d in range(2):
                for k in range(2):
                    sp.dma_start(gbias[32 * d:32 * d + H, k:k + 1], gb[2 * d + k]).then_inc(gb_in, 16)
            for load in range(NAL1):
                if load >= 2:
                    sp.wait_ge(mod_done, at(load - 1))
                sp.dma_start(aw[:, load % 2], adw[:, :, load * AC:(load + 1) * AC]).then_inc(ada_in[0][load % 2], 16)
            sp.wait_ge(setup, at(11))
            for k in range(2):
                for d in range(2):
                    c0 = 64 * k + 32 * d
                    w0 = OFF_G + H * (2 * d + k)
                    sp.dma_start(w_raw[:, 0, :, c0:c0 + H], win[:, :, w0:w0 + H]).then_inc(raw_in[0], 16)

            def load(t, src, col, kt=KT):
                columns = src[:, :, ds(col, P)]
                sp.wait_ge(lo_ready, at(t.n - 1))
                sp.dma_start(w_raw[:, t.slot, 0:kt], columns).then_inc(raw_in[t.slot], 16)

            with sp.Fori(0, H) as i:
                for k, off in enumerate((OFF_Q, OFF_K, OFF_V, OFF_O)):
                    load(Tile(N_HEAD + k, 4, i), win, i * P + off)
            with sp.Fori(0, KT // 2) as i:
                for k in range(6):
                    load(Tile(N_CONV + k, 6, i), win, i * (2 * P) + (k // 3 * P + (OFF_SC, OFF_SX, OFF_SB)[k % 3]))
            for base, off, w in ((N_MIX_M, OFF_MG, wmo), (N_MIX_C, OFF_MG + D, wco)):
                with sp.Fori(0, KT) as i:
                    load(Tile(base, 2, i), win, i * P + off)
                    load(Tile(base + 1, 2, i), w, (i + 1) * P - P)
            with sp.Fori(0, KT // 2) as i:
                for k in range(2):
                    load(Tile(N_WO + k, 2, i), wo_, i * (2 * P) + k * P)
            n, done = N_FFN, 0
            for size in GROUPS:
                with sp.Fori(0, size) as i:
                    load(Tile(n, 2, i), wup, i * P + done * P)
                    load(Tile(n + 1, 2, i), wup, i * P + (FF + done * P))
                n += 2 * size
                with sp.Fori(0, KT // 2) as i:
                    for k in range(2):
                        load(Tile(n + k, 2, i), wdn[:, done:done + size, :], i * (2 * P) + k * P, size)
                n += KT
                done += size
            for l in range(NL):
                sp.wait_ge(f_ready, at(l + 1))
                sp.dma_start(out_tok[l], o_out[:, l % 2, :]).then_inc(y_out[l % 2], 16)
            for s_ in y_out:
                sp.wait_ge(s_, 16 * (NL // 2))


_INS = ["x", "c", "ctx", "c_ctx", "ada_w", "ada_b", "norm1_g", "norm2_g", "w_in", "qk_conv_w", "qk_conv_b",
        "gate_b", "mnorm_g", "w_m_out", "sc_conv_w", "sc_conv_b", "w_c_out", "w_o", "w_up", "ff_conv_w",
        "ff_conv_b", "w_down", "final_g"]


def kernel(**inputs):
    import numpy as np
    import concourse.bacc as bacc
    from concourse.bass_utils import run_bass_kernel_spmd

    nc = bacc.Bacc("TRN2", target_bir_lowering=False, num_devices=1)
    arrays, args = {}, []
    for name in _INS:
        a = np.ascontiguousarray(inputs[name])
        arrays[f"in_{name}"] = a
        args.append(nc.dram_tensor(f"in_{name}", a.shape, mybir.dt.from_np(a.dtype), kind="ExternalInput").ap())
    out = nc.dram_tensor("out_x", (1, T, D), F32, kind="ExternalOutput").ap()
    layer(nc, *args, out)
    r = run_bass_kernel_spmd(nc, [arrays], core_ids=[0])
    return r.results[0]["out_x"]
```

```python
from contextlib import ExitStack

import concourse.bass as bass
from concourse import mybir

F32 = mybir.dt.float32
F32R = mybir.dt.float32r
ALU = mybir.AluOpType
ACT = mybir.ActivationFunctionType
AX_X = mybir.AxisListType.X

P = 128
D = 1024
KT = D // P
T = 1024
TC = 256
TA = TC + T
HALF = 512
H = 8
CH = 128
NC = TA // CH
NCC = TC // CH
NL = T // CH
VW = P + 1
GRID = 64
ROWS = T // GRID
AC = 256
NAL = 6 * D // AC
NAL1 = 2 * D // AC
NAS = 5
PASS = 4
JP = PASS * AC // P
FF = 2816
FT = FF // P
GROUPS = (8, 7, 7)
EPS = 1e-6
NEG = -1e30
BIG = 1e30
EXP_MAX = 88.0
SCALE = float(P) ** -0.5

OFF_Q, OFF_K, OFF_V, OFF_G = 0, D, 2 * D, 3 * D
OFF_O = OFF_G + 4 * H
OFF_SB, OFF_SC, OFF_SX, OFF_MG = OFF_O + D, OFF_O + 2 * D, OFF_O + 3 * D, OFF_O + 4 * D

ADA_B, N1G, N2G, C_X, C_CTX, MNG, SCB, SCW = 0, 48, 56, 64, 72, 80, 88, 96
QKW, QKB, FFB, FFW = 128, 176, 192, 256
B_CTX, B_S, B_T, B_G, B_O = 2, 3, 5, 6, 7
B_KV = (B_T, B_G, B_O, B_T, B_G)

N_SETUP = 18
N_PAR = 13
SCAN = ([*range(NC - 1)], [*range(NCC)][::-1] + [*range(NCC + 1, NC)][::-1])
OUT = (((0, 1, 2), (3, 4, 5), (6, 7)), ((5, 6, 7), (2, 3, 4), (0, 1)))
ROW_F, ROW_ABS, ROW_U, ROW_M, ROW_AX, ROW_WX, ROW_EX = 1, 2, 11, 19, 27, 28, 30
ROW_EXP, ROW_LN, ROW_A, ROW_WK, ROW_EM = 1, 2, 3, 4, 5

V_HEAD = 37

N_GATE = 0
N_HEAD = 1
N_CONV = N_HEAD + 4 * H
N_MIX_C = N_CONV + 3 * KT
N_MIX_M = N_MIX_C + 2 * KT
N_WO = N_MIX_M + 2 * KT
N_FFN = N_WO + KT
N_ALL = N_FFN + 2 * FT + len(GROUPS) * KT


def at(count):
    return count + 1


class Tile:

    def __init__(self, base, per=0, i=0, down=0):
        self.slot = base % 2
        self.n = base + per * i if per else base
        self.nth = base // 2 + (per // 2) * i if per else base // 2
        self.base, self.per, self.i, self.down = base, per, i, down
        self.p = self.n - down

    def ahead(self, k):
        return Tile(self.base + k, self.per, self.i, self.down)


class Chain:

    def __init__(self, eng, sem):
        self.eng, self.sem, self.count, self.i, self.first = eng, sem, 0, None, 0

    def step(self, ins):
        ins.then_inc(self.sem, 1)
        self.count += 1
        self.eng.wait_ge(self.sem, self.value())

    def value(self):
        if self.i is None:
            return at(self.count)
        return self.per * (self.i - self.first) + at(self.count)

    def enter(self, i, first, per):
        self.i, self.first, self.per, self.began = i, first, per, self.count

    def leave(self, passes):
        assert self.count - self.began == self.per, (self.count - self.began, self.per)
        self.i = None
        self.count = self.began + passes * self.per


def layer(nc, x, c, ctx, c_ctx, ada_w, ada_b, norm1_g, norm2_g, w_in, qk_conv_w, qk_conv_b, gate_b,
          mnorm_g, w_m_out, sc_conv_w, sc_conv_b, w_c_out, w_o, w_up, ff_conv_w, ff_conv_b, w_down,
          final_g, out):
    ds = bass.ds
    m_rows = nc.dram_tensor("m_rows", (2, H, TA), F32, kind="Internal").ap()
    a_rows = nc.dram_tensor("a_rows", (2, H, TA), F32, kind="Internal").ap()
    a_dram = nc.dram_tensor("branch_a", (KT, P, T), F32, kind="Internal").ap()
    z_dram = nc.dram_tensor("branch_z", (KT, P, T), F32, kind="Internal").ap()

    def rows(w):
        return w.rearrange("(k p) n -> p k n", p=P)

    win, wup, wmo, wco, wo_, wdn = (rows(w[0]) for w in (w_in, w_up, w_m_out, w_c_out, w_o, w_down))
    adw = rows(ada_w[0])
    x_tok = x[0].rearrange("(j p) d -> p j d", p=P)
    ctx_tok = ctx[0].rearrange("(j p) d -> p j d", p=P)
    out_tok = out[0].rearrange("(j p) d -> j p d", p=P)

    ctx_ = ExitStack()
    with ctx_:
        def keep(name, shape, dt=F32):
            return ctx_.enter_context(nc.sbuf_tensor(name, shape, dt))

        def sem(name):
            s = ctx_.enter_context(nc.semaphore(name))
            return s

        credited = []

        def csem(name):
            s = sem(name)
            credited.append(s)
            return s

        op_hi = keep("op_hi", [P, KT, T], F32R)
        op_lo = keep("op_lo", [P, KT, T], F32R)
        w_raw = keep("w_raw", [P, 2, KT, P])
        w_hi = keep("w_hi", [P, 2, KT, P], F32R)
        w_lo = keep("w_lo", [P, 2, KT, P], F32R)
        ident = keep("ident", [P, P])
        ones = keep("ones", [P, P])
        par = keep("par", [P, 4 * P])
        mod = keep("mod", [P, 48, 2])
        gain = keep("gain", [P, 3, KT])
        power = keep("power", [P, KT])
        zero8 = keep("zero8", [P, NL])
        gate5 = keep("gate5", [P, KT])

        def scoped(*tensors):
            with ExitStack() as s:
                return [s.enter_context(nc.sbuf_tensor(n, sh, dt)) for n, sh, dt in tensors]

        cs = keep("cs", [P, KT, 2])
        st2 = keep("st2", [P, 2, NL])
        st3 = keep("st3", [P, 24])
        ctx_hi, ctx_lo, cols, late, early, *above = scoped(
            ("ctx_hi", [P, KT, TC], F32R), ("ctx_lo", [P, KT, TC], F32R),
            ("cols", [P, 3, NC, 2, H], F32),
            ("late", [P, P], F32), ("early", [P, P], F32),
            ("raw", [P, T + TC + 8], F32),
            ("conv", [P, TA], F32), ("q_t", [P, T], F32), ("og", [P, T], F32), ("k_t", [P, TA], F32),
            ("v_t", [P, TA], F32),
            ("m_bc", [P, 2, T], F32), ("a_bc", [P, 2, TA], F32), ("k_tok", [P, NC, P], F32),
            ("v_tok", [P, NC, VW], F32), ("wgt", [P, NL, CH], F32), ("pt", [P, NL, CH], F32),
            ("qs", [P, 2, T], F32), ("vw", [P, NC, VW], F32), ("state", [P, 2, NC - 1, VW], F32),
            ("h_tok", [P, NL, P], F32), ("tiny", [P, 96], F32), ("h_tmp", [P, 3, P], F32))
        (raw, conv, q_t, og, k_t, v_t, m_bc, a_bc, k_tok, v_tok, wgt, pt, qs, vw, state, h_tok, tiny, h_tmp) = above
        LOW = 2 * KT * TC
        SHARED = LOW + 3 * NC * 2 * H + 2 * P
        HEADS = SHARED + (T + TC + 8) + 3 * TA + 2 * T
        _, x_in, ht, aw0, prow, mrow, stat, gbias, mp = scoped(
            ("below_x", [P, SHARED], F32), ("x_in", [P, NC, D], F32), ("ht", [P, 2, HALF], F32),
            ("aw0", [P, NAS, KT, AC], F32), ("prow", [P, 4, P], F32),
            ("mrow", [2, 2 * D], F32), ("stat", [P, 3, 16], F32), ("gbias", [64, 2], F32), ("mp", [64, 2, NC], F32))
        _, g_i, g_f, g_e, g_b, g_m, g_d, g_r, g_s = scoped(
            ("below_g", [P, HEADS], F32), *[(f"g_{n}", [64, TA], F32) for n in "ifebmdrs"])
        _, aw, acc = scoped(("below_aw", [P, HEADS], F32), ("aw", [P, 2, KT, AC], F32),
                            ("acc", [P, PASS, AC], F32))
        (br_hi01, br_lo01, res, gth, mtmp, b_raw, br_hi27, br_lo27) = scoped(
            ("br_hi01", [P, 2, T], F32R), ("br_lo01", [P, 2, T], F32R),
            ("res", [P, KT, T], F32),
            ("gth", [P, 2, T], F32), ("mtmp", [P, T], F32), ("b_raw", [P, 2, T], F32),
            ("br_hi27", [P, KT - 2, T], F32R), ("br_lo27", [P, KT - 2, T], F32R))
        _, sq, sqsum, _, x_j = scoped(("below_sq", [P, LOW + KT * T], F32), ("sq", [P, T], F32),
                                      ("sqsum", [P, T], F32), ("below_xj", [P, T], F32),
                                      ("x_j", [P, 2, NL, P], F32))
        u_t, u_h, diag = scoped(("u_t", [P, 2, T], F32), ("u_h", [P, T], F32), ("diag", [P, NL, P], F32))
        _, hid_hi, hid_lo = scoped(("below_hid", [P, LOW + KT * T], F32), ("hid_hi", [P, KT, T], F32R),
                                   ("hid_lo", [P, KT, T], F32R))
        a_pad, cv, gv = scoped(("a_pad", [P, ROWS + 2, GRID + 2], F32), ("cv", [P, T], F32), ("gv", [P, T], F32))
        o_out, gbc, junk = scoped(("o_out", [P, 2, D], F32), ("gbc", [P, D], F32), ("junk", [P, D], F32))
        ps = ctx_.enter_context(nc.psum_tensor("ps", [P, 8, 512], F32))

        par_in, gb_in, gb_out = sem("par_in"), sem("gb_in"), sem("rows_out")
        x_loaded = [sem(f"x_loaded{b}") for b in range(3)]
        ada_in, late_in = [sem(f"ada_in{b}") for b in range(NAS)], [sem(f"late_in{b}") for b in range(2)]
        raw_in = [sem(f"raw_in{b}") for b in range(2)]
        bc_in = sem("bc_in")
        a_out = sem("a_out")
        br_in = [sem(f"br_in{b}") for b in range(2)]
        xj_in, gbc_in = [sem("xj_in0"), sem("xj_in1")], sem("gbc_in")
        y_out = [sem("y_out0"), sem("y_out1")]
        setup = csem("setup")
        par_turned, par_ready = csem("par_turned"), csem("par_ready")
        cond_ready = csem("cond_ready")
        mod_done, mod_ready = csem("mod_done"), csem("mod_ready")
        sumsq, rms = csem("sumsq"), csem("rms")
        x_scaled, x_turned, x_mod = csem("x_scaled"), csem("x_turned"), csem("x_mod")
        act_hi, act_lo = csem("act_hi"), csem("act_lo")
        hi_ready, lo_ready = csem("hi_ready"), csem("lo_ready")
        full = [csem(f"full{b}") for b in range(2)]
        drained = [csem(f"drained{b}") for b in range(2)]
        ctx_full, ctx_drained = csem("ctx_full"), csem("ctx_drained")
        row_v, row_a, row_turned, row_cols = (csem(n) for n in ("row_v", "row_a", "row_turned", "row_cols"))
        conv_ready, tanh_ready = csem("conv_ready"), csem("tanh_ready")
        q_ready, k_ready, og_ready = (csem(n) for n in ("q_ready", "k_ready", "og_ready"))
        turned, tok_ready = csem("turned"), csem("tok_ready")
        s_full, expo_ready, wexp_ready, pt_ready = (csem(n) for n in ("s_full", "expo_ready", "wexp_ready", "pt_ready"))
        qs_ready, vw_ready, g_full, state_ready = (csem(n) for n in ("qs_ready", "vw_ready", "g_full", "state_ready"))
        o_full, den_ready, h_ready = csem("o_full"), csem("den_ready"), csem("h_ready")
        sq_ready, ss_ready, rn_ready, hn_ready = (csem(n) for n in ("sq_ready", "ss_ready", "rn_ready", "hn_ready"))
        h_turned, at_ready = csem("h_turned"), csem("at_ready")
        a_stored = csem("a_stored")
        z_hi_ready, mod_read = csem("z_hi_ready"), csem("mod_read")
        mrow_ready, mod_turned, acc_ready = csem("mrow_ready"), csem("mod_turned"), csem("acc_ready")
        v_step, a_step, p_step = csem("v_step"), csem("a_step"), csem("p_step")
        br_hi_ready, br_lo_ready = csem("br_hi_ready"), csem("br_lo_ready")
        gth_ready, mix_ready = csem("gth_ready"), csem("mix_ready")
        xj_turned, xres_ready, sqsum_ready, stat_done = (
            csem(n) for n in ("xj_turned", "xres_ready", "sqsum_ready", "stat_done"))
        n2_ready, factor_spread, ut_ready = csem("n2_ready"), csem("factor_spread"), csem("ut_ready")
        n2_sum, n2_rms, pad_ready = csem("n2_sum"), csem("n2_rms"), csem("pad_ready")
        cv_ready, gelu_ready, u_ready, uh_ready, ul_ready = (
            csem(n) for n in ("cv_ready", "gelu_ready", "u_ready", "uh_ready", "ul_ready"))
        f_turned, f_sum, f_rms, f_ready = (csem(n) for n in ("f_turned", "f_sum", "f_rms", "f_ready"))

        block = ctx_.enter_context(nc.Block())

        op = [(op_hi[:, k, :], op_lo[:, k, :]) for k in range(KT)]
        ctx_op = [(ctx_hi[:, k, :], ctx_lo[:, k, :]) for k in range(KT)]
        br = [(br_hi01[:, k, :], br_lo01[:, k, :]) for k in range(2)] + \
             [(br_hi27[:, k, :], br_lo27[:, k, :]) for k in range(KT - 2)]
        hid = [(hid_hi[:, k, :], hid_lo[:, k, :]) for k in range(KT)]

        def products(dst, t, src, sl, ks, first, last, ready=None):
            for k in ks:
                if ready is not None:
                    nc.tensor.wait_ge(act_lo, at(ready + k + 1))
                hi, lo = src[k]
                for w, a in ((w_hi, hi), (w_hi, lo), (w_lo, hi)):
                    ins = nc.tensor.matmul(dst, w[:, t.slot, k, :], a[:, sl],
                                           start=(k == first and w is w_hi and a is hi),
                                           stop=(k == last and w is w_lo))
            return ins

        HALVES = (slice(0, HALF), slice(HALF, T))

        @block.tensor
        def _(pe):
            def weights(t):
                pe.wait_ge(hi_ready, at(t.n + 1))
                pe.wait_ge(lo_ready, at(t.n + 1))

            def half_tile(t, half, between=None, src=op, ready=None):
                if half == 0:
                    weights(t)
                pe.wait_ge(drained[half], at(t.n))
                products(ps[:, half, :], t, src, HALVES[half], range(KT // 2), 0, KT - 1, ready)
                if between:
                    between()
                products(ps[:, half, :], t, src, HALVES[half], range(KT // 2, KT), 0, KT - 1,
                         ready).then_inc(full[half], 1)

            def ctx_tile(t, nth):
                weights(t)
                pe.wait_ge(ctx_drained, at(nth))
                products(ps[:, B_CTX, 0:TC], t, ctx_op, slice(0, TC), range(KT), 0, KT - 1).then_inc(ctx_full, 1)

            pe.wait_ge(setup, at(2))
            pe.wait_ge(par_in, 16 * N_PAR)
            for r, n in enumerate((120, 86, 128, 70)):
                nc.tensor.transpose(ps[:, B_S, r * P:r * P + n], prow[0:n, r, :],
                                    ident[0:n, 0:n]).then_inc(par_turned, 1)
            pe.wait_ge(cond_ready, at(2))

            def turn_input(b):
                n = 4 if b < 2 else NCC
                pe.wait_ge(x_scaled, at(4 * b + n))
                for k in range(KT):
                    t = b * KT + k
                    if t >= 3:
                        pe.wait_ge(x_mod, at(t - 2))
                    elif t == 0:
                        pe.wait_ge(par_ready, at(4))
                    for j in range(n):
                        ins = nc.tensor.transpose(ps[:, B_S + t % 3, j * P:(j + 1) * P],
                                                  x_in[:, 4 * b + j, k * P:(k + 1) * P], ident[:, :])
                    ins.then_inc(x_turned, 1)

            for load in range(NAL1):
                pe.wait_ge(ada_in[load % NAS], 16 * (load // NAS + 1))
                for k in range(KT):
                    ins = nc.tensor.matmul(ps[0:2, B_CTX + load // 2, (load % 2) * AC:(load % 2 + 1) * AC], cs[:, k, :],
                                           aw0[:, load % NAS, k, :], start=(k == 0), stop=(k == KT - 1))
                ins.then_inc(mod_done, 1)
            for jt in range(2 * KT):
                pe.wait_ge(mrow_ready, at(jt // 4 + 1))
                ins = nc.tensor.transpose(ps[:, 0, 2 * jt:2 * jt + 2], mrow[:, jt * P:(jt + 1) * P], ident[0:2, 0:2])
            ins.then_inc(mod_turned, 1)
            turn_input(0)
            turn_input(1)

            t = Tile(N_GATE)
            half_tile(t, 0, ready=0)
            turn_input(2)
            half_tile(t, 1, ready=KT)
            pe.wait_ge(act_lo, at(3 * KT))
            ctx_tile(t, 0)
            for k in range(4):
                t = Tile(N_HEAD + k)
                if k in (1, 2):
                    ctx_tile(t, k)
                for half in range(2):
                    half_tile(t, half)
            for q in range(3):
                pe.wait_ge(row_v if q == 0 else row_a, at(ROW_U if q == 0 else (ROW_WK if q == 1 else ROW_EM)))
                pe.wait_ge(row_cols, at(q))
                for ch in range(NC):
                    ins = nc.tensor.transpose(ps[:, B_S + ch // 8, (ch % 8) * 64:(ch % 8) * 64 + 64],
                                              (g_i, g_e, g_s)[q][:, ch * P:(ch + 1) * P], ident[0:64, 0:64])
                ins.then_inc(row_turned, 1)

            def turn_kv(g, j):
                if j == 0:
                    pe.wait_ge(at_ready, at(2 * g))
                    pe.wait_ge(state_ready, at(6 * g))
                    pe.wait_ge(h_ready, at(6 * g))
                    pe.wait_ge(k_ready, at(g + 1))
                    pe.wait_ge(drained[0], at(N_HEAD + 4 * g + 3))
                    pe.wait_ge(drained[1], at(N_HEAD + 4 * g + 3))
                    pe.wait_ge(ctx_drained, at(2 * g + 3))
                elif j >= 3:
                    pe.wait_ge(tok_ready, at(5 * g + j - 2))
                src = ((k_t, 2), (k_t, 6), (v_t, 2), (v_t, 6), (None, 0))[j]
                for q in range(4):
                    if j < 4:
                        a = src[0][:, (src[1] + q) * P:(src[1] + q + 1) * P]
                    else:
                        a = (k_t if q < 2 else v_t)[:, (q % 2) * P:(q % 2 + 1) * P]
                    ins = nc.tensor.transpose(ps[:, B_KV[j], q * P:(q + 1) * P], a, ident[:, :])
                ins.then_inc(turned, 1)

            def scores(g, j):
                pe.wait_ge(q_ready, at(g + 1))
                pe.wait_ge(k_ready, at(g + 1))
                pe.wait_ge(pt_ready, at(4 * g))
                if j == 0:
                    pe.wait_ge(row_cols, at(3))
                for q in range(4):
                    l = 4 * j + q
                    ins = nc.tensor.matmul(ps[:, B_S + j, q * CH:(q + 1) * CH], k_t[:, TC + l * CH:TC + (l + 1) * CH],
                                           q_t[:, l * CH:(l + 1) * CH], start=True, stop=True)
                ins.then_inc(s_full, 1)

            def outer(g, d, j):
                pe.wait_ge(tok_ready, at(5 * g + 5))
                pe.wait_ge(vw_ready, at(2 * g + d + 1))
                pe.wait_ge(state_ready, at(6 * g + 3 * d + j))
                for q in range(3):
                    ch = SCAN[d][3 * j + q]
                    ins = nc.tensor.matmul(ps[:, B_G, q * VW:(q + 1) * VW], k_tok[:, ch, :], vw[:, ch, :],
                                           start=True, stop=True)
                ins.then_inc(g_full, 1)

            def outputs(g, d, j):
                pe.wait_ge(pt_ready, at(4 * g + 2 * d + 2))
                pe.wait_ge(qs_ready, at(2 * g + d + 1))
                pe.wait_ge(state_ready, at(6 * g + 3 * d + 3))
                pe.wait_ge(h_ready, at(6 * g + 3 * d + j))
                for q, l in enumerate(OUT[d][j]):
                    o = ps[:, B_O, q * VW:(q + 1) * VW]
                    nc.tensor.matmul(o, pt[:, l, :], v_tok[:, NCC + l, :], start=True, stop=False)
                    ins = nc.tensor.matmul(o, qs[:, d, l * CH:(l + 1) * CH],
                                           state[:, d, 1 + (l if d == 0 else NL - 1 - l), :], start=False, stop=True)
                ins.then_inc(o_full, 1)

            def turn_h(g, j):
                if j == 0:
                    pe.wait_ge(hn_ready, at(g + 1))
                    pe.wait_ge(tok_ready, at(5 * g + 5))
                else:
                    pe.wait_ge(at_ready, at(2 * g + 1))
                for q in range(4):
                    ins = nc.tensor.transpose(ps[:, B_T, q * P:(q + 1) * P], h_tok[:, 4 * j + q, :], ident[:, :])
                ins.then_inc(h_turned, 1)

            def mlstm(g):
                yield lambda: (turn_kv(g, 0), turn_kv(g, 1), scores(g, 0), scores(g, 1))
                yield lambda: (turn_kv(g, 2), turn_kv(g, 3))
                yield lambda: turn_kv(g, 4)
                yield lambda: outer(g, 0, 0)
                yield lambda: outer(g, 0, 1)
                yield lambda: outer(g, 0, 2)
                yield lambda: None
                yield lambda: outputs(g, 0, 0)
                yield lambda: outputs(g, 0, 1)
                yield lambda: (outputs(g, 0, 2), outer(g, 1, 0))
                yield lambda: outer(g, 1, 1)
                yield lambda: outer(g, 1, 2)
                yield lambda: outputs(g, 1, 0)
                yield lambda: outputs(g, 1, 1)
                yield lambda: outputs(g, 1, 2)
                yield lambda: None
                yield lambda: None
                yield lambda: (turn_h(g, 0), turn_h(g, 1))

            with pe.Fori(1, H) as i:
                steps = mlstm(i - 1)
                for k in range(4):
                    t = Tile(N_HEAD + k, 4, i)
                    if k in (1, 2):
                        ctx_tile(t, 2 * i + k)
                        next(steps)()
                    for half in range(2):
                        half_tile(t, half, next(steps))
                        if (k, half) != (3, 1):
                            next(steps)()
                for step in steps:
                    step()

            def late_modulation(p):
                pe.wait_ge(acc_ready, at(PASS * p + PASS))
                for jt in range(JP):
                    ins = nc.tensor.matmul(ps[:, B_G, jt:jt + 1], acc[:, jt // 2, (jt % 2) * P:(jt % 2 + 1) * P],
                                           ones[:, 0:1], start=True, stop=True)
                ins.then_inc(mod_done, 1)

            steps = mlstm(H - 1)
            for k in range(6):
                for half in range(2):
                    half_tile(Tile(N_CONV + k), half, next(steps, None))
                    next(steps, lambda: None)()
            with pe.Fori(1, KT // 2) as i:
                for k in range(6):
                    for half in range(2):
                        half_tile(Tile(N_CONV + k, 6, i), half)
                    if k == 1:
                        late_modulation(i - 1)

            for stage, base in enumerate((N_MIX_C, N_MIX_M)):
                for k in range(2):
                    for half in range(2):
                        half_tile(Tile(base + k), half)
                if not stage:
                    late_modulation(KT // 2 - 1)
                pe.wait_ge(br_lo_ready, at(KT * (stage + 1)))
                with pe.Fori(0, KT // 2 - 1) as i:
                    for k in range(2):
                        for half in range(2):
                            half_tile(Tile(base + 2 * k + 2, 4, i), half, src=br)
                        for half in range(2):
                            half_tile(Tile(base + 2 * k + 3, 4, i), half)
                for k in range(2):
                    for half in range(2):
                        half_tile(Tile(base + 2 * KT - 2 + k), half, src=br)

            def turn_x(i, slot):
                j = 2 * i + slot
                pe.wait_ge(xj_in[slot], 16 * (i + 1))
                pe.wait_ge(xres_ready, at(j))
                for l in range(NL):
                    ins = nc.tensor.transpose(ps[:, B_S + l // 4, (l % 4) * P:(l % 4 + 1) * P],
                                              x_j[:, slot, l, :], ident[:, :])
                ins.then_inc(xj_turned, 1)

            with pe.Fori(0, KT // 2) as i:
                for k in range(2):
                    turn_x(i, k)
                    half_tile(Tile(N_WO + k, 2, i), 0, ready=3 * KT)
                    half_tile(Tile(N_WO + k, 2, i), 1)
            pe.wait_ge(sqsum_ready, at(KT + 1))
            for l in range(NL):
                ins = nc.tensor.matmul(ps[:, B_O, l:l + 1], sqsum[:, l * P:(l + 1) * P], ones[:, 0:1],
                                       start=True, stop=True)
            ins.then_inc(stat_done, 1)
            pe.wait_ge(n2_ready, at(1))
            for half in range(2):
                nc.tensor.matmul(ps[:, B_S + half, :], ones[:, :], diag[:, 4 * half:4 * half + 4, :],
                                 start=True, stop=True).then_inc(factor_spread, 1)

            n, done = N_FFN, 0
            for size in GROUPS:
                with pe.Fori(0, size) as i:
                    for k in range(2):
                        for half in range(2):
                            half_tile(Tile(n + k, 2, i), half,
                                      ready=None if done or k or half else 4 * KT)
                n += 2 * size
                done += size

                def down(t):
                    weights(t)
                    for half in range(2):
                        pe.wait_ge(drained[half], at(t.n))
                        products(ps[:, half, :], t, hid, HALVES[half], range(size - 1), 0, size - 1)
                    pe.wait_ge(ul_ready, at(done))
                    for half in range(2):
                        products(ps[:, half, :], t, hid, HALVES[half], (size - 1,), 0,
                                 size - 1).then_inc(full[half], 1)
                pe.wait_ge(ul_ready, at(done - 1))
                with pe.Fori(0, KT // 2) as i:
                    for k in range(2):
                        down(Tile(n + k, 2, i))
                n += KT

            for l in range(NL):
                if l == 0:
                    pe.wait_ge(drained[0], at(N_ALL))
                    pe.wait_ge(drained[1], at(N_ALL))
                if l >= 4:
                    pe.wait_ge(f_ready, at(l - 3))
                for k in range(KT):
                    ins = nc.tensor.transpose(ps[:, 2 * (l % 4) + k // 4, (k % 4) * P:(k % 4 + 1) * P],
                                              res[:, k, l * P:(l + 1) * P], ident[:, :])
                ins.then_inc(f_turned, 1)

        @block.scalar
        def _(act):
            def hi_split(t):
                act.wait_ge(raw_in[t.slot], 16 * (t.nth + 1) + (48 if t.slot == 0 else 0))
                act.wait_ge(full[1], at(t.n - 1))
                nc.scalar.copy(w_hi[:, t.slot], w_raw[:, t.slot]).then_inc(hi_ready, 1)

            act.wait_ge(par_ready, at(4))
            for v, col in enumerate((C_X, C_CTX)):
                nc.scalar.activation(cs[:, :, v], par[:, col:col + KT], ACT.Silu).then_inc(cond_ready, 1)

            for b in range(3):
                act.wait_ge(x_loaded[b], 16)
                for j in range(4 if b < 2 else NCC):
                    act.wait_ge(sumsq, at(4 * b + j))
                    nc.scalar.activation(ps[:, B_G:B_G + 2, :].rearrange("p b n -> p (b n)"), x_in[:, 4 * b + j, :],
                                         ACT.Square, accum_out=stat[:, 0, 4 * b + j:4 * b + j + 1]).then_inc(sumsq, 1)

            def modulate(b):
                v, n = (0, HALF) if b < 2 else (1, TC)
                hi = op_hi[:, :, b * HALF:(b + 1) * HALF] if b < 2 else ctx_hi[:, :, :]
                for k in range(KT):
                    t = b * KT + k
                    act.wait_ge(x_turned, at(t + 1))
                    if t >= 2:
                        act.wait_ge(act_lo, at(t - 1))
                    nc.scalar.activation(ht[:, t % 2, 0:n], ps[:, B_S + t % 3, 0:n], ACT.Identity,
                                         scale=gain[:, v, k:k + 1], bias=mod[:, k, v:v + 1]).then_inc(x_mod, 1)
                    act.wait_ge(x_mod, at(t + 1))
                    nc.scalar.copy(hi[:, k, :], ht[:, t % 2, 0:n]).then_inc(act_hi, 1)

            for n in range(2):
                act.wait_ge(raw_in[n], 64 if n == 0 else 16)
                nc.scalar.copy(w_hi[:, n], w_raw[:, n]).then_inc(hi_ready, 1)
            act.wait_ge(mod_ready, at(3))
            for b in range(3):
                modulate(b)

            for src, lo, n, f, d in ((B_CTX, 0, TC, ctx_full, ctx_drained), (0, TC, HALF, full[0], drained[0]),
                                     (1, TC + HALF, HALF, full[1], drained[1])):
                act.wait_ge(f, at(1))
                act.wait_ge(act_lo, at(3 * KT))
                nc.scalar.copy(g_i[:, lo:lo + n], ps[0:64, src, 0:n])
                nc.scalar.copy(g_f[:, lo:lo + n], ps[64:128, src, 0:n]).then_inc(d, 1)
            hi_split(Tile(2))
            act.wait_ge(row_v, at(ROW_ABS))
            nc.scalar.activation(g_e[:, :], g_e[:, :], ACT.Exp).then_inc(row_a, 1)
            act.wait_ge(row_a, at(ROW_EXP))
            nc.scalar.activation(g_s[:, :], g_e[:, :], ACT.Ln, bias=1.0).then_inc(row_a, 1)

            def drain_half(i, k, half, dst, waits=()):
                n = N_HEAD + 4 * i + k
                act.wait_ge(full[half], at(n + 1))
                for s, c in waits:
                    act.wait_ge(s, at(c))
                nc.scalar.copy(dst, ps[:, half, :]).then_inc(drained[half], 1)

            def drain_ctx(i, k, dst, waits=()):
                act.wait_ge(ctx_full, at(2 * i + k + 1))
                for s, c in waits:
                    act.wait_ge(s, at(c))
                nc.scalar.copy(dst, ps[:, B_CTX, 0:TC]).then_inc(ctx_drained, 1)

            def o_half(i, half):
                act.wait_ge(full[half], at(N_HEAD + 4 * i + 4))
                act.wait_ge(k_ready, at(i + 1))
                nc.scalar.activation(conv[:, half * HALF:(half + 1) * HALF], ps[:, half, :], ACT.Tanh,
                                     scale=0.5).then_inc(drained[half], 1)

            def tanh_q(i):
                act.wait_ge(conv_ready, at(2 * i + 1))
                act.wait_ge(s_full, at(2 * i))
                act.wait_ge(qs_ready, at(2 * i))
                nc.scalar.activation(q_t[:, :], conv[:, TC:TA], ACT.Tanh, scale=0.5).then_inc(tanh_ready, 1)

            def tanh_k(i):
                act.wait_ge(conv_ready, at(2 * i + 2))
                act.wait_ge(turned, at(5 * i))
                act.wait_ge(s_full, at(2 * i))
                nc.scalar.activation(k_t[:, :], conv[:, :], ACT.Tanh, scale=0.5).then_inc(tanh_ready, 1)

            def q_half(i, half):
                drain_half(i, 0, half, raw[:, 1 + half * HALF:1 + (half + 1) * HALF], ((conv_ready, 2 * i),))

            def k_half(i, half):
                drain_half(i, 1, half, raw[:, 1 + half * HALF:1 + (half + 1) * HALF], ((conv_ready, 2 * i + 1),))

            def k_ctx(i):
                drain_ctx(i, 1, raw[:, T + 3:T + 3 + TC], ((conv_ready, 2 * i),))

            def v_half(i, half):
                drain_half(i, 2, half, v_t[:, TC + half * HALF:TC + (half + 1) * HALF], ((turned, 5 * i),))

            def v_ctx(i):
                drain_ctx(i, 2, v_t[:, 0:TC], ((turned, 5 * i),))

            def kv_tokens(g, j):
                act.wait_ge(turned, at(5 * g + j + 1))
                if j == 0:
                    act.wait_ge(g_full, at(6 * g))
                    act.wait_ge(o_full, at(6 * g))
                    act.wait_ge(row_cols, at(3))
                    act.wait_ge(setup, at(N_SETUP))
                src = ps[:, B_KV[j], :].rearrange("p (c n) -> p c n", n=P)
                if j < 2:
                    nc.scalar.copy(k_tok[:, NCC + 4 * j:NCC + 4 * j + 4, :], src).then_inc(tok_ready, 1)
                elif j < 4:
                    nc.scalar.copy(v_tok[:, NCC + 4 * j - 8:NCC + 4 * j - 4, 0:P], src).then_inc(tok_ready, 1)
                else:
                    nc.scalar.copy(k_tok[:, 0:NCC, :], src[:, 0:NCC, :])
                    nc.scalar.copy(v_tok[:, 0:NCC, 0:P], src[:, NCC:2 * NCC, :]).then_inc(tok_ready, 1)

            def exp_weights(g, d):
                act.wait_ge(expo_ready, at(2 * g + d + 1))
                nc.scalar.activation(wgt[:, :, :], wgt[:, :, :], ACT.Exp, scale=-1.0).then_inc(wexp_ready, 1)

            def denominators(g, d, j):
                m = len(OUT[d][j])
                l0 = OUT[d][j][0]
                act.wait_ge(o_full, at(6 * g + 3 * d + j + 1))
                act.wait_ge(h_ready, at(6 * g + 3 * d))
                nc.scalar.activation(tiny[:, 8 * d + l0:8 * d + l0 + m],
                                     ps[:, B_O, 0:m * VW].rearrange("p (c n) -> p c n", n=VW)[:, :, P],
                                     ACT.Abs).then_inc(den_ready, 1)

            def squares(g):
                act.wait_ge(h_ready, at(6 * g + 6))
                act.wait_ge(pt_ready, at(4 * g + 4))
                nc.scalar.activation(wgt[:, :, :], h_tok[:, :, :], ACT.Square).then_inc(sq_ready, 1)

            def head_tile(i, k):
                return Tile(N_HEAD + k, 4, i)

            q_half(0, 0); q_half(0, 1); hi_split(head_tile(0, 2))
            tanh_q(0); k_ctx(0); k_half(0, 0); k_half(0, 1); hi_split(head_tile(0, 3))
            tanh_k(0); v_ctx(0); v_half(0, 0); v_half(0, 1); hi_split(head_tile(0, 4))
            o_half(0, 0); o_half(0, 1); hi_split(head_tile(0, 5))
            for row, need, scale in ((g_f, ROW_AX, 1.0), (g_e, ROW_WX, 1.0), (g_s, ROW_EX, -1.0)):
                act.wait_ge(row_v, at(need))
                nc.scalar.activation(row[:, :], row[:, :], ACT.Exp, scale=scale).then_inc(row_a, 1)

            with act.Fori(1, H) as i:
                g = i - 1
                kv_tokens(g, 0); kv_tokens(g, 1); exp_weights(g, 0); q_half(i, 0)
                kv_tokens(g, 2); kv_tokens(g, 3); kv_tokens(g, 4); q_half(i, 1); hi_split(head_tile(i, 2))
                exp_weights(g, 1); k_ctx(i); tanh_q(i); k_half(i, 0)
                denominators(g, 0, 0); k_half(i, 1); hi_split(head_tile(i, 3)); denominators(g, 0, 1)
                v_ctx(i); denominators(g, 0, 2); v_half(i, 0); tanh_k(i)
                denominators(g, 1, 0); v_half(i, 1); hi_split(head_tile(i, 4))
                denominators(g, 1, 1); denominators(g, 1, 2); o_half(i, 0)
                squares(g); o_half(i, 1); hi_split(head_tile(i, 5))

            def c_half(half, n):
                act.wait_ge(full[half], at(n + 1))
                act.wait_ge(drained[1], at(n - 1))
                nc.scalar.copy(q_t[:, half * HALF:(half + 1) * HALF], ps[:, half, :]).then_inc(drained[half], 1)

            def conv_tile(k, i=0):
                return Tile(N_CONV + k, 6, i)

            def z_part(hi_tile, n):
                act.wait_ge(drained[0], at(n + 1))
                act.wait_ge(drained[1], at(n + 1))
                nc.scalar.copy(hi_tile, k_t[:, 0:T]).then_inc(z_hi_ready, 1)

            g = H - 1
            kv_tokens(g, 0); kv_tokens(g, 1); exp_weights(g, 0)
            act.wait_ge(qs_ready, at(2 * H)); act.wait_ge(s_full, at(2 * H)); c_half(0, N_CONV)
            kv_tokens(g, 2); kv_tokens(g, 3); kv_tokens(g, 4)
            c_half(1, N_CONV); hi_split(conv_tile(2)); exp_weights(g, 1)
            denominators(g, 0, 0); hi_split(conv_tile(3)); denominators(g, 0, 1); denominators(g, 0, 2)
            hi_split(conv_tile(4)); z_part(br_hi01[:, 0, :], N_CONV + 2)
            denominators(g, 1, 0); c_half(0, N_CONV + 3); denominators(g, 1, 1); denominators(g, 1, 2)
            c_half(1, N_CONV + 3); hi_split(conv_tile(5)); squares(g)
            hi_split(conv_tile(6)); z_part(br_hi01[:, 1, :], N_CONV + 5); hi_split(conv_tile(7))
            act.wait_ge(a_stored, at(H))
            with act.Fori(1, KT // 2) as i:
                for k in range(6):
                    if k % 3 == 0:
                        for half in range(2):
                            c_half(half, N_CONV + 6 * i + k)
                    hi_split(conv_tile(k + 2, i))
                    if k % 3 == 2:
                        z_part(br_hi27[:, ds(2 * i + (k // 3 - 2), 1), :].rearrange("p a n -> p (a n)"),
                               N_CONV + 6 * i + k)

            def gate_half(t, slot, half):
                act.wait_ge(full[half], at(t.n + 1))
                act.wait_ge(drained[half], at(t.n))
                nc.scalar.activation(gth[:, slot, HALVES[half]], ps[:, half, :], ACT.Tanh,
                                     scale=0.5).then_inc(drained[half], 1)

            def branch_hi(k):
                act.wait_ge(br_in[k % 2], 16 * (k // 2 + 1))
                nc.scalar.copy(br[k][0], b_raw[:, k % 2, :]).then_inc(br_hi_ready, 1)

            for stage, base in enumerate((N_MIX_C, N_MIX_M)):
                if stage:
                    act.wait_ge(full[1], at(N_MIX_M))
                else:
                    act.wait_ge(acc_ready, at(4 * PASS))
                for k in range(2):
                    for half in range(2):
                        if stage:
                            branch_hi(4 * k + 2 * half)
                            branch_hi(4 * k + 2 * half + 1)
                        gate_half(Tile(base + k), k, half)
                    hi_split(Tile(base + k).ahead(2))
                with act.Fori(0, KT // 2 - 1) as i:
                    for k in range(2):
                        hi_split(Tile(base + 2 * k + 2, 4, i).ahead(2))
                        t = Tile(base + 2 * k + 3, 4, i)
                        for half in range(2):
                            gate_half(t, k, half)
                        hi_split(t.ahead(2))
                if not stage:
                    for k in range(2):
                        hi_split(Tile(base + 2 * KT - 2 + k).ahead(2))

            act.wait_ge(full[1], at(N_MIX_M + 2 * KT - 2))

            def merged(j):
                act.wait_ge(mix_ready, at(2 * j + 2))
                nc.scalar.mul(op_hi[:, j, :], res[:, j, :], 0.5).then_inc(act_hi, 1)
            for j in range(4):
                merged(j)
            hi_split(Tile(N_WO))
            for j in range(4, KT - 1):
                merged(j)
            hi_split(Tile(N_WO + 1))
            merged(KT - 1)

            def residual(j):
                act.wait_ge(xj_turned, at(j + 1))
                act.wait_ge(act_lo, at(4 * KT))
                nc.scalar.copy(res[:, ds(j, 1), :].rearrange("p a (b n) -> p (a b) n", n=HALF),
                               ps[:, B_S:B_S + 2, :]).then_inc(xres_ready, 1)

            with act.Fori(0, KT // 2) as i:
                for k in range(2):
                    residual(2 * i + k)
                    hi_split(Tile(N_WO + k, 2, i).ahead(2))

            for k in range(KT):
                act.wait_ge(ut_ready, at(k + 1))
                if k >= 1:
                    act.wait_ge(act_lo, at(4 * KT + k))
                nc.scalar.activation(u_h[:, :], u_t[:, k % 2, :], ACT.Identity, scale=gain[:, 2, k:k + 1],
                                     bias=mod[:, 3 * KT + k, 0:1]).then_inc(uh_ready, 1)
                act.wait_ge(uh_ready, at(k + 1))
                nc.scalar.copy(op_hi[:, k, :], u_h[:, :]).then_inc(act_hi, 1)

            n, done = N_FFN, 0
            act.wait_ge(pad_ready, at(1))
            for group, size in enumerate(GROUPS):
                with act.Fori(0, size) as i:
                    f = done + i
                    ta, tg = Tile(n, 2, i), Tile(n + 1, 2, i)
                    for half in range(2):
                        act.wait_ge(full[half], at(ta.n + 1))
                        act.wait_ge(cv_ready, at(f))
                        r0 = 1 + half * ROWS // 2
                        nc.scalar.copy(a_pad[:, r0:r0 + ROWS // 2, 1:1 + GRID],
                                       ps[:, half, :].rearrange("p (r w) -> p r w", w=GRID)).then_inc(drained[half], 1)
                    hi_split(ta.ahead(2))
                    for half in range(2):
                        act.wait_ge(full[half], at(tg.n + 1))
                        act.wait_ge(ul_ready, at(f))
                        nc.scalar.copy(gv[:, half * HALF:(half + 1) * HALF], ps[:, half, :]).then_inc(drained[half], 1)
                    hi_split(tg.ahead(2))
                    act.wait_ge(cv_ready, at(f + 1))
                    nc.scalar.activation(cv[:, :], cv[:, :], ACT.Gelu_apprx_tanh).then_inc(gelu_ready, 1)
                    act.wait_ge(u_ready, at(f + 1))
                    act.wait_ge(full[1], at(n))
                    nc.scalar.copy(hid_hi[:, ds(i, 1), :], gv[:, :]).then_inc(uh_ready, 1)
                n += 2 * size
                done += size
                last = group == len(GROUPS) - 1
                with act.Fori(0, KT // 2 - last) as i:
                    for k in range(2):
                        hi_split(Tile(n + k, 2, i).ahead(2))
                n += KT

            for l in range(NL):
                act.wait_ge(f_turned, at(l + 1))
                act.wait_ge(f_sum, at(l))
                nc.scalar.activation(junk[:, :], ps[:, 2 * (l % 4):2 * (l % 4) + 2, :].rearrange("p b n -> p (b n)"),
                                     ACT.Square, accum_out=st3[:, l:l + 1]).then_inc(f_sum, 1)

        @block.vector
        def _(dve):
            vec = nc.vector
            chain = Chain(dve, v_step)

            def lo_split(t):
                dve.wait_ge(hi_ready, at(t.n + 1))
                vec.tensor_tensor(w_lo[:, t.slot], w_raw[:, t.slot], w_hi[:, t.slot].bitcast(F32),
                                  ALU.subtract).then_inc(lo_ready, 1)

            for r, n in enumerate((120, 86, 128, 70)):
                dve.wait_ge(par_turned, at(4))
                vec.tensor_copy(par[:, r * P:r * P + n], ps[:, B_S, r * P:r * P + n]).then_inc(par_ready, 1)
            dve.wait_ge(par_ready, at(4))
            chain.step(vec.tensor_scalar(gate5[:, :], par[:, MNG:MNG + KT], 0.5, None, ALU.mult))
            def scale_tokens(b):
                dve.wait_ge(rms, at(b + 1))
                for j in range(4 if b < 2 else NCC):
                    vec.tensor_scalar(x_in[:, 4 * b + j, :], x_in[:, 4 * b + j, :],
                                      stat[:, 2, 4 * b + j:4 * b + j + 1], None, ALU.mult).then_inc(x_scaled, 1)

            def low_parts(b):
                n = HALF if b < 2 else TC
                for k in range(KT):
                    t = b * KT + k
                    hi, lo = (a[:, HALVES[b]] for a in op[k]) if b < 2 else ctx_op[k]
                    dve.wait_ge(act_hi, at(t + 1))
                    vec.tensor_tensor(lo, ht[:, t % 2, 0:n], hi.bitcast(F32), ALU.subtract).then_inc(act_lo, 1)

            for b in range(3):
                scale_tokens(b)
            lo_split(Tile(0))
            lo_split(Tile(1))
            for b in range(4):
                dve.wait_ge(mod_done, at(2 * b + 2))
                vec.tensor_copy(mrow[:, b * HALF:(b + 1) * HALF], ps[0:2, B_CTX + b, :]).then_inc(mrow_ready, 1)
            dve.wait_ge(mod_turned, at(1))
            vec.tensor_tensor(mod[:, 0:2 * KT, :], ps[:, 0, 0:4 * KT].rearrange("p (j v) -> p j v", v=2),
                              par[:, ADA_B:ADA_B + 2 * KT].unsqueeze(2).broadcast_to([P, 2 * KT, 2]),
                              ALU.add).then_inc(mod_ready, 1)
            dve.wait_ge(mod_ready, at(1))
            for v in range(2):
                vec.scalar_tensor_tensor(out=gain[:, v, :], in0=mod[:, KT:2 * KT, v], scalar=1.0,
                                         in1=par[:, N1G:N1G + KT], op0=ALU.add, op1=ALU.mult).then_inc(mod_ready, 1)
            for b in range(3):
                low_parts(b)

            def row(ins):
                ins.then_inc(row_v, 1)
                rows_done[0] += 1
                dve.wait_ge(row_v, at(rows_done[0]))
            rows_done = [0]
            F, B = slice(0, 32), slice(32, 64)

            dve.wait_ge(ctx_drained, at(1))
            dve.wait_ge(drained[0], at(1))
            dve.wait_ge(drained[1], at(1))
            dve.wait_ge(gb_in, 64)
            row(vec.tensor_scalar(g_f[:, :], g_f[:, :], gbias[:, 1:2], None, ALU.add))
            row(vec.scalar_tensor_tensor(out=g_e[:, :], in0=g_f[:, :], scalar=-1.0, in1=g_f[:, :],
                                         op0=ALU.mult, op1=ALU.min))
            lo_split(Tile(2))
            dve.wait_ge(row_a, at(ROW_EXP))
            row(vec.tensor_scalar(g_b[:, :], g_e[:, :], 1.0, None, ALU.add))
            row(vec.scalar_tensor_tensor(out=g_b[:, :], in0=g_b[:, :], scalar=-1.0, in1=g_e[:, :],
                                         op0=ALU.add, op1=ALU.subtract))
            dve.wait_ge(row_a, at(ROW_LN))
            row(vec.tensor_scalar(g_e[:, :], g_e[:, :], -0.5, 1.0, ALU.mult, ALU.add))
            row(vec.tensor_tensor(g_b[:, :], g_b[:, :], g_e[:, :], ALU.mult))
            row(vec.tensor_tensor(g_s[:, :], g_s[:, :], g_b[:, :], ALU.subtract))
            row(vec.scalar_tensor_tensor(out=g_f[:, :], in0=g_f[:, :], scalar=0.0, in1=g_s[:, :],
                                         op0=ALU.min, op1=ALU.subtract))

            def row_sums():
                dve.wait_ge(setup, at(14))
                row(vec.tensor_tensor_scan(g_b[F, :], g_r[F, :], g_f[F, :], 0.0, ALU.mult, ALU.add))
                row(vec.tensor_tensor_scan(g_b[B, ::-1], g_r[B, ::-1], g_f[B, ::-1], 0.0, ALU.mult, ALU.add))
                row(vec.scalar_tensor_tensor(out=g_i[:, :], in0=g_i[:, :], scalar=gbias[:, 0:1], in1=g_b[:, :],
                                             op0=ALU.add, op1=ALU.subtract))

            def row_maxima():
                row(vec.memset(g_d[:, :], 0.0))
                row(vec.tensor_copy(g_d[F, CH::CH], g_b[F, CH - 1:TA - CH:CH]))
                row(vec.tensor_copy(g_d[B, CH - 1:CH], g_b[B, CH:CH + 1]))
                row(vec.tensor_copy(g_d[B, TC + CH - 1:TA - CH:CH], g_b[B, TC + CH::CH]))
                row(vec.tensor_copy(g_d[B, TA - 1:TA], g_b[B, 0:1]))
                row(vec.tensor_tensor_scan(g_m[F, :], g_d[F, :], g_i[F, :], NEG, ALU.add, ALU.max))
                row(vec.tensor_tensor_scan(g_m[B, TC - 1::-1], g_d[B, TC - 1::-1], g_i[B, TC - 1::-1], NEG,
                                           ALU.add, ALU.max))
                row(vec.tensor_tensor_scan(g_m[B, TA - 1:TC - 1:-1], g_d[B, TA - 1:TC - 1:-1],
                                           g_i[B, TA - 1:TC - 1:-1], g_m[B, 0:1], ALU.add, ALU.max))

            def row_factors():
                row(vec.memset(mp[:, :, :], NEG))
                row(vec.tensor_tensor(mp[F, 0, 1:NC], g_m[F, CH - 1:TA - CH:CH], g_d[F, CH::CH], ALU.add))
                row(vec.tensor_tensor(mp[B, 0, 0:1], g_m[B, CH:CH + 1], g_d[B, CH - 1:CH], ALU.add))
                row(vec.tensor_tensor(mp[B, 0, NCC:NC - 1], g_m[B, TC + CH::CH], g_d[B, TC + CH - 1:TA - CH:CH],
                                      ALU.add))
                row(vec.tensor_tensor(mp[B, 0, NC - 1:NC], g_m[B, 0:1], g_d[B, TA - 1:TA], ALU.add))
                row(vec.tensor_copy(mp[F, 1, :], g_m[F, CH - 1::CH]))
                row(vec.tensor_copy(mp[B, 1, :], g_m[B, 0::CH]))

                def chunks(a):
                    return a[:, :].rearrange("p (c n) -> p c n", n=CH)

                def ends(v):
                    return mp[:, v, :].unsqueeze(2).broadcast_to([64, NC, CH])
                row(vec.tensor_tensor(chunks(g_f), ends(0), chunks(g_m), ALU.subtract))
                row(vec.tensor_tensor(chunks(g_e), chunks(g_i), ends(1), ALU.subtract))
                row(vec.tensor_tensor(g_s[:, :], g_b[:, :], g_m[:, :], ALU.add))
                row(vec.tensor_scalar(g_s[:, :], g_s[:, :], -EXP_MAX, None, ALU.max))

            def conv3(src, dst, n, w, b, last):
                chain.step(vec.tensor_scalar(dst, src[:, 1:1 + n], w(1), b, ALU.mult, ALU.add))
                chain.step(vec.scalar_tensor_tensor(out=dst, in0=src[:, 0:n], scalar=w(0), in1=dst,
                                                    op0=ALU.mult, op1=ALU.add))
                ins = vec.scalar_tensor_tensor(out=dst, in0=src[:, 2:2 + n], scalar=w(2), in1=dst,
                                               op0=ALU.mult, op1=ALU.add)
                ins.then_inc(conv_ready, 1) if last else chain.step(ins)

            def qk_conv(i, k, n):
                dve.wait_ge(drained[0], at(n + 1))
                dve.wait_ge(drained[1], at(n + 1))
                dve.wait_ge(setup, at(17))

                def w(tap):
                    return par[:, ds(i + (QKW + 16 * tap + 8 * k), 1)]
                b = par[:, ds(i + (QKB + 8 * k), 1)]
                if k:
                    dve.wait_ge(ctx_drained, at(2 * i + 2))
                    conv3(raw[:, T + 2:], conv[:, 0:TC], TC, w, b, False)
                conv3(raw, conv[:, TC:TA], T, w, b, True)

            def q_silu(i):
                dve.wait_ge(tanh_ready, at(2 * i + 1))
                vec.scalar_tensor_tensor(out=q_t[:, :], in0=q_t[:, :], scalar=1.0, in1=conv[:, TC:TA],
                                         op0=ALU.add, op1=ALU.mult).then_inc(q_ready, 1)
                dve.wait_ge(q_ready, at(i + 1))

            def k_silu(i):
                dve.wait_ge(tanh_ready, at(2 * i + 2))
                vec.scalar_tensor_tensor(out=k_t[:, :], in0=k_t[:, :], scalar=1.0, in1=conv[:, :],
                                         op0=ALU.add, op1=ALU.mult).then_inc(k_ready, 1)

            def o_gate(i, n):
                dve.wait_ge(drained[0], at(n + 1))
                dve.wait_ge(drained[1], at(n + 1))
                dve.wait_ge(at_ready, at(2 * i))
                vec.tensor_scalar(og[:, :], conv[:, 0:T], 1.0, None, ALU.add).then_inc(og_ready, 1)
                dve.wait_ge(og_ready, at(i + 1))

            def col(q, g, d, c0, c1, width):
                return cols[:, q, c0:c1, d, ds(g, 1)].broadcast_to([P, c1 - c0, width])

            def exponents(g, d):
                if d == 0:
                    dve.wait_ge(bc_in, 64 * (g + 1))
                    dve.wait_ge(row_cols, at(3))
                else:
                    dve.wait_ge(pt_ready, at(4 * g + 2))
                mask = (late, early)[d][:, :].unsqueeze(1).broadcast_to([P, NL, CH])
                chain.step(vec.tensor_tensor(wgt[:, :, :], m_bc[:, d, :].rearrange("p (c n) -> p c n", n=CH),
                                             col(0, g, d, NCC, NC, CH), ALU.subtract))
                vec.tensor_tensor(wgt[:, :, :], wgt[:, :, :], mask, ALU.max).then_inc(expo_ready, 1)

            def scaled_queries(g, d):
                dve.wait_ge(q_ready, at(g + 1))
                dve.wait_ge(o_full, at(6 * g))
                vec.scalar_tensor_tensor(out=qs[:, d, :], in0=q_t[:, :], scalar=0.5, in1=a_bc[:, d, TC:TA],
                                         op0=ALU.mult, op1=ALU.mult).then_inc(qs_ready, 1)

            def weighted_scores(g, d):
                dve.wait_ge(wexp_ready, at(2 * g + d + 1))
                if d == 0:
                    dve.wait_ge(a_stored, at(g))
                else:
                    dve.wait_ge(o_full, at(6 * g + 3))
                for j in range(2):
                    dve.wait_ge(s_full, at(2 * g + j + 1))
                    vec.scalar_tensor_tensor(out=pt[:, 4 * j:4 * j + 4, :], in0=ps[:, B_S + j, :].rearrange("p (c n) -> p c n", n=CH),
                                             scalar=SCALE / 4, in1=wgt[:, 4 * j:4 * j + 4, :],
                                             op0=ALU.mult, op1=ALU.mult).then_inc(pt_ready, 1)

            def weighted_values(g, d):
                dve.wait_ge(tok_ready, at(5 * g + 5))
                dve.wait_ge(g_full, at(6 * g + 3 * d))
                vec.scalar_tensor_tensor(out=vw[:, :, :], in0=v_tok[:, :, :], scalar=SCALE / 2,
                                         in1=col(1, g, d, 0, NC, VW), op0=ALU.mult,
                                         op1=ALU.mult).then_inc(vw_ready, 1)

            def carry(g, d, j):
                dve.wait_ge(g_full, at(6 * g + 3 * d + j + 1))
                dve.wait_ge(o_full, at(6 * g))
                for q in range(3):
                    k = 3 * j + q
                    add = ps[:, B_G, q * VW:(q + 1) * VW]
                    if k == 0:
                        ins = vec.tensor_copy(state[:, d, 0, :], add)
                    else:
                        ch = SCAN[d][k]
                        end = ch * CH + (CH - 1 if d == 0 else 0)
                        ins = vec.scalar_tensor_tensor(out=state[:, d, k, :], in0=state[:, d, k - 1, :],
                                                       scalar=a_bc[:, d, end:end + 1], in1=add,
                                                       op0=ALU.mult, op1=ALU.add)
                    if q < 2:
                        chain.step(ins)
                ins.then_inc(state_ready, 1)
                dve.wait_ge(state_ready, at(6 * g + 3 * d + j + 1))

            def heads_out(g, d, j):
                ls = OUT[d][j]
                m, l0 = len(ls), ls[0]
                dve.wait_ge(den_ready, at(6 * g + 3 * d + j + 1))
                dve.wait_ge(h_turned, at(2 * g))
                den, top, rec = (tiny[:, 16 * q + 8 * d + l0:16 * q + 8 * d + l0 + m] for q in range(3))
                chain.step(vec.tensor_tensor(top, den, cols[:, 2, NCC + l0:NCC + l0 + m, d, ds(g, 1)].rearrange(
                    "p c a -> p (c a)"), ALU.max))
                chain.step(vec.reciprocal(rec, top))
                num = ps[:, B_O, 0:m * VW].rearrange("p (c n) -> p c n", n=VW)[:, :, 0:P]
                rec = rec.unsqueeze(2).broadcast_to([P, m, P])
                if d == 0:
                    vec.tensor_tensor(h_tok[:, l0:l0 + m, :], num, rec, ALU.mult).then_inc(h_ready, 1)
                else:
                    chain.step(vec.tensor_tensor(h_tmp[:, 0:m, :], num, rec, ALU.mult))
                    dve.wait_ge(h_ready, at(6 * g + 3))
                    vec.tensor_tensor(h_tok[:, l0:l0 + m, :], h_tok[:, l0:l0 + m, :], h_tmp[:, 0:m, :],
                                      ALU.add).then_inc(h_ready, 1)

            def head_norm(g):
                dve.wait_ge(sq_ready, at(g + 1))
                dve.wait_ge(rn_ready, at(g))
                chain.step(vec.tensor_reduce(tiny[:, 48:56], wgt[:, :, :], AX_X, ALU.add))
                vec.tensor_scalar(tiny[:, 56:64], tiny[:, 48:56], 1.0 / P, EPS, ALU.mult, ALU.add).then_inc(ss_ready, 1)
                dve.wait_ge(rn_ready, at(g + 1))
                vec.tensor_tensor(h_tok[:, :, :], h_tok[:, :, :], tiny[:, 64:72].unsqueeze(2).broadcast_to([P, NL, P]),
                                  ALU.mult).then_inc(hn_ready, 1)

            def head_result(g):
                dve.wait_ge(og_ready, at(g + 1))
                dve.wait_ge(o_full, at(6 * g + 6))
                for j in range(2):
                    dve.wait_ge(h_turned, at(2 * g + j + 1))
                    vec.scalar_tensor_tensor(out=pt[:, 4 * j:4 * j + 4, :].rearrange("p c n -> p (c n)"),
                                             in0=ps[:, B_T, :], scalar=gate5[:, ds(g, 1)],
                                             in1=og[:, j * HALF:(j + 1) * HALF], op0=ALU.mult,
                                             op1=ALU.mult).then_inc(at_ready, 1)

            def head_tile(i, k):
                return Tile(N_HEAD + k, 4, i)

            lo_split(head_tile(0, 2))
            qk_conv(0, 0, N_HEAD); q_silu(0)
            row_sums()
            lo_split(head_tile(0, 3))
            qk_conv(0, 1, N_HEAD + 1); k_silu(0)
            row_maxima()
            lo_split(head_tile(0, 4))
            row_factors()
            dve.wait_ge(k_ready, at(1))
            o_gate(0, N_HEAD + 3)
            lo_split(head_tile(0, 5))
            for q in range(3):
                dve.wait_ge(row_turned, at(q + 1))
                src = ps[:, B_S:B_S + 2, :].rearrange("p b n -> p (b n)")[:, 0:64 * NC].rearrange(
                    "p (c d h) -> p c d h", d=2, h=32)[:, :, :, 0:H]
                vec.tensor_copy(cols[:, q], src).then_inc(row_cols, 1)

            with dve.Fori(1, H) as i:
                g = i - 1
                chain.enter(i, 1, V_HEAD)
                exponents(g, 0); scaled_queries(g, 0); scaled_queries(g, 1); weighted_scores(g, 0)
                exponents(g, 1); weighted_values(g, 0); carry(g, 0, 0); lo_split(head_tile(i, 2))
                carry(g, 0, 1); qk_conv(i, 0, N_HEAD + 4 * i); carry(g, 0, 2); q_silu(i)
                weighted_values(g, 1); heads_out(g, 0, 0); lo_split(head_tile(i, 3)); heads_out(g, 0, 1)
                qk_conv(i, 1, N_HEAD + 4 * i + 1); heads_out(g, 0, 2)
                weighted_scores(g, 1); carry(g, 1, 0); k_silu(i); carry(g, 1, 1); carry(g, 1, 2)
                heads_out(g, 1, 0); lo_split(head_tile(i, 4)); heads_out(g, 1, 1); heads_out(g, 1, 2)
                head_norm(g); head_result(g)
                o_gate(i, N_HEAD + 4 * i + 3); lo_split(head_tile(i, 5))
                chain.leave(H - 1)

            def conv_tile(k, i=0):
                return Tile(N_CONV + k, 6, i)

            def c_times_x(half, n):
                dve.wait_ge(full[half], at(n + 1))
                dve.wait_ge(drained[half], at(n))
                vec.tensor_tensor(raw[:, 1 + half * HALF:1 + (half + 1) * HALF], q_t[:, half * HALF:(half + 1) * HALF],
                                  ps[:, half, :], ALU.mult).then_inc(drained[half], 1)

            def sc_conv(j, n):
                dve.wait_ge(drained[0], at(n + 1))
                dve.wait_ge(drained[1], at(n + 1))
                b = par[:, ds(j + SCB, 1)]
                dst = conv[:, TC:TA]
                chain.step(vec.tensor_scalar(dst, raw[:, 1:1 + T], par[:, ds(j + SCW + 8, 1)], b, ALU.mult, ALU.add))
                for tap in (0, 2):
                    chain.step(vec.scalar_tensor_tensor(out=dst, in0=raw[:, tap:tap + T], scalar=par[:, ds(j + SCW + 8 * tap, 1)],
                                                        in1=dst, op0=ALU.mult, op1=ALU.add))

            def times_b(j, half, n):
                dve.wait_ge(full[half], at(n + 1))
                dve.wait_ge(br_lo_ready, at(j))
                vec.tensor_tensor(k_t[:, half * HALF:(half + 1) * HALF], conv[:, TC + half * HALF:TC + (half + 1) * HALF],
                                  ps[:, half, :], ALU.mult).then_inc(drained[half], 1)

            def z_low(tiles, j, k):
                hi, lo = (a[:, ds(k, 1), :].rearrange("p a n -> p (a n)") for a in tiles)
                dve.wait_ge(z_hi_ready, at(j + 1))
                vec.tensor_tensor(lo, k_t[:, 0:T], hi.bitcast(F32), ALU.subtract).then_inc(br_lo_ready, 1)

            def mac(p, q):
                dve.wait_ge(late_in[q % 2], 16 * (PASS // 2) * p + 16 * (q // 2 + 1))
                if q == 0:
                    dve.wait_ge(mod_done, at(NAL1 + p))
                for k in range(KT):
                    if k == 0:
                        ins = vec.tensor_scalar(acc[:, q, :], aw[:, q % 2, k, :], cs[:, k, 0:1], None, ALU.mult)
                    else:
                        ins = vec.scalar_tensor_tensor(out=acc[:, q, :], in0=aw[:, q % 2, k, :], scalar=cs[:, k, 0:1],
                                                       in1=acc[:, q, :], op0=ALU.mult, op1=ALU.add)
                    if k < KT - 1:
                        chain.step(ins)
                ins.then_inc(acc_ready, 1)

            def late_modulation(p):
                dve.wait_ge(mod_done, at(NAL1 + 1 + p))
                vec.tensor_tensor(mod[:, ds(JP * p + 2 * KT, JP), 0], ps[:, B_G, 0:JP],
                                  par[:, ds(JP * p + (ADA_B + 2 * KT), JP)], ALU.add).then_inc(mod_read, 1)

            g, n = H - 1, N_CONV
            exponents(g, 0); scaled_queries(g, 0); scaled_queries(g, 1); weighted_scores(g, 0)
            exponents(g, 1); weighted_values(g, 0); carry(g, 0, 0); lo_split(conv_tile(2))
            carry(g, 0, 1); c_times_x(0, n + 1); carry(g, 0, 2); weighted_values(g, 1)
            c_times_x(1, n + 1); lo_split(conv_tile(3)); heads_out(g, 0, 0); heads_out(g, 0, 1)
            sc_conv(0, n + 1)
            dve.wait_ge(turned, at(5 * H))
            heads_out(g, 0, 2); times_b(0, 0, n + 2); weighted_scores(g, 1); carry(g, 1, 0); carry(g, 1, 1)
            times_b(0, 1, n + 2); carry(g, 1, 2); lo_split(conv_tile(4)); z_low((br_hi01, br_lo01), 0, 0)
            heads_out(g, 1, 0); heads_out(g, 1, 1); heads_out(g, 1, 2); lo_split(conv_tile(5))
            head_norm(g); c_times_x(0, n + 4); head_result(g); c_times_x(1, n + 4); lo_split(conv_tile(6))
            sc_conv(1, n + 4); times_b(1, 0, n + 5); times_b(1, 1, n + 5); z_low((br_hi01, br_lo01), 1, 1)
            mac(0, 0); mac(0, 1); lo_split(conv_tile(7)); mac(0, 2); mac(0, 3)
            with dve.Fori(1, KT // 2) as i:
                chain.enter(i, 1, 6 + PASS * (KT - 1))
                for k in range(2):
                    j, n = 2 * i + k, N_CONV + 3 * k + 6 * i
                    lo_split(conv_tile(3 * k + 2, i))
                    c_times_x(0, n + 1); c_times_x(1, n + 1); lo_split(conv_tile(3 * k + 3, i))
                    sc_conv(j, n + 1)
                    times_b(j, 0, n + 2); times_b(j, 1, n + 2); lo_split(conv_tile(3 * k + 4, i))
                    z_low((br_hi27, br_lo27), j, j - 2)
                    if k == 0:
                        late_modulation(i - 1)
                    mac(i, 2 * k); mac(i, 2 * k + 1)
                chain.leave(KT // 2 - 1)

            def mixed(stage, j, t, slot):
                for half, sl in enumerate(HALVES):
                    dve.wait_ge(full[half], at(t.n + 1))
                    dve.wait_ge(drained[half], at(t.n))
                    dst = res[:, ds(j, 1), sl].rearrange("p a n -> p (a n)")
                    if stage:
                        dve.wait_ge(mix_ready, at(2 * j + half))
                    vec.scalar_tensor_tensor(out=mtmp[:, sl] if stage else dst, in0=gth[:, slot, sl], scalar=1.0,
                                             in1=ps[:, half, :], op0=ALU.add, op1=ALU.mult).then_inc(drained[half], 1)
                    if stage:
                        dve.wait_ge(drained[half], at(t.n + 1))
                        vec.tensor_tensor(dst, dst, mtmp[:, sl], ALU.add).then_inc(mix_ready, 1)

            def branch_lo(k):
                dve.wait_ge(br_hi_ready, at(k + 1))
                vec.tensor_tensor(br[k][1], b_raw[:, k % 2, :], br[k][0].bitcast(F32),
                                  ALU.subtract).then_inc(br_lo_ready, 1)

            def merged(j):
                dve.wait_ge(act_hi, at(3 * KT + j + 1))
                vec.scalar_tensor_tensor(out=op_lo[:, j, :], in0=res[:, j, :], scalar=0.5,
                                         in1=op_hi[:, j, :].bitcast(F32), op0=ALU.mult,
                                         op1=ALU.subtract).then_inc(act_lo, 1)

            for stage, base in enumerate((N_MIX_C, N_MIX_M)):
                for k in range(2):
                    if stage:
                        for q in range(4):
                            branch_lo(4 * k + q)
                    lo_split(Tile(base + k + 2))
                if not stage:
                    late_modulation(KT // 2 - 1)
                    dve.wait_ge(mod_read, at(KT // 2))
                    vec.scalar_tensor_tensor(out=gain[:, 2, :], in0=mod[:, 4 * KT:5 * KT, 0], scalar=1.0,
                                             in1=par[:, N2G:N2G + KT], op0=ALU.add, op1=ALU.mult).then_inc(mod_ready, 1)
                with dve.Fori(0, KT // 2 - 1) as i:
                    for k in range(2):
                        t = Tile(base + 2 * k + 2, 4, i)
                        mixed(stage, 2 * i + k, t, k)
                        lo_split(t.ahead(2))
                        lo_split(t.ahead(3))
                if stage:
                    for j in range(4):
                        merged(j)
                mixed(stage, KT - 2, Tile(base + 2 * KT - 2), 0)
                lo_split(Tile(base + 2 * KT))
                if stage:
                    for j in range(4, KT - 1):
                        merged(j)
                mixed(stage, KT - 1, Tile(base + 2 * KT - 1), 1)
                lo_split(Tile(base + 2 * KT + 1))
            merged(KT - 1)

            dve.wait_ge(mod_ready, at(4))
            vec.memset(sqsum[:, :], 0.0).then_inc(sqsum_ready, 1)
            with dve.Fori(0, KT // 2) as i:
                chain.enter(i, 0, 2)
                for k in range(2):
                    t = Tile(N_WO + k, 2, i)
                    dve.wait_ge(xres_ready, at(2 * i + k + 1))
                    for half in range(2):
                        dve.wait_ge(full[half], at(t.n + 1))
                        dst = res[:, ds(2 * i + k, 1), half * HALF:(half + 1) * HALF].rearrange("p a n -> p (a n)")
                        vec.scalar_tensor_tensor(out=dst, in0=ps[:, half, :], scalar=mod[:, ds(2 * i + (2 * KT + k), 1), 0],
                                                 in1=dst, op0=ALU.mult, op1=ALU.add).then_inc(drained[half], 1)
                    dve.wait_ge(drained[0], at(t.n + 1))
                    dve.wait_ge(drained[1], at(t.n + 1))
                    lo_split(t.ahead(2))
                    dve.wait_ge(sqsum_ready, at(2 * i + k + 1))
                    tile_j = res[:, ds(2 * i + k, 1), :].rearrange("p a n -> p (a n)")
                    chain.step(vec.tensor_tensor(sq[:, :], tile_j, tile_j, ALU.mult))
                    vec.tensor_tensor(sqsum[:, :], sqsum[:, :], sq[:, :], ALU.add).then_inc(sqsum_ready, 1)
                chain.leave(KT // 2)

            dve.wait_ge(stat_done, at(1))
            vec.tensor_scalar(st2[:, 0, :], ps[:, B_O, 0:NL], 1.0 / D, EPS, ALU.mult, ALU.add).then_inc(n2_sum, 1)
            dve.wait_ge(n2_rms, at(1))
            vec.tensor_tensor(diag[:, :, :], ident[:, :].unsqueeze(1).broadcast_to([P, NL, P]),
                              st2[:, 1, :].unsqueeze(2).broadcast_to([P, NL, P]), ALU.mult).then_inc(n2_ready, 1)
            dve.wait_ge(factor_spread, at(2))

            def low(k):
                dve.wait_ge(act_hi, at(4 * KT + k + 1))
                vec.tensor_tensor(op_lo[:, k, :], u_h[:, :], op_hi[:, k, :].bitcast(F32), ALU.subtract).then_inc(act_lo, 1)
            for k in range(KT):
                if k >= 2:
                    dve.wait_ge(uh_ready, at(k - 1))
                vec.tensor_tensor(u_t[:, k % 2, :], res[:, k, :],
                                  ps[:, B_S:B_S + 2, :].rearrange("p b n -> p (b n)"), ALU.mult).then_inc(ut_ready, 1)
                if k:
                    low(k - 1)
            low(KT - 1)

            chain.step(vec.memset(a_pad[:, :, :], 0.0))
            dve.sem_inc(pad_ready, 1)
            n, done = N_FFN, 0
            out3 = cv[:, :].rearrange("p (r w) -> p r w", w=GRID)
            for group, size in enumerate(GROUPS):
                with dve.Fori(0, size) as i:
                    chain.enter(i, 0, 8)
                    f = done + i
                    ta, tg = Tile(n, 2, i), Tile(n + 1, 2, i)
                    lo_split(ta.ahead(2))
                    dve.wait_ge(drained[0], at(ta.n + 1))
                    dve.wait_ge(drained[1], at(ta.n + 1))
                    dve.wait_ge(ul_ready, at(f))
                    chain.step(vec.tensor_scalar(out3, a_pad[:, 1:1 + ROWS, 1:1 + GRID], par[:, ds(f + (FFW + 4 * FT), 1)],
                                                 par[:, ds(f + FFB, 1)], ALU.mult, ALU.add))
                    for tap in (0, 1, 2, 3, 5, 6, 7, 8):
                        r, w = tap // 3, tap % 3
                        ins = vec.scalar_tensor_tensor(out=out3, in0=a_pad[:, r:r + ROWS, w:w + GRID],
                                                       scalar=par[:, ds(f + (FFW + tap * FT), 1)], in1=out3,
                                                       op0=ALU.mult, op1=ALU.add)
                        if tap < 8:
                            chain.step(ins)
                    ins.then_inc(cv_ready, 1)
                    lo_split(tg.ahead(2))
                    dve.wait_ge(drained[0], at(tg.n + 1))
                    dve.wait_ge(drained[1], at(tg.n + 1))
                    dve.wait_ge(gelu_ready, at(f + 1))
                    vec.tensor_tensor(gv[:, :], cv[:, :], gv[:, :], ALU.mult).then_inc(u_ready, 1)
                    dve.wait_ge(uh_ready, at(KT + f + 1))
                    vec.tensor_tensor(hid_lo[:, ds(i, 1), :].rearrange("p a n -> p (a n)"), gv[:, :],
                                      hid_hi[:, ds(i, 1), :].rearrange("p a n -> p (a n)").bitcast(F32),
                                      ALU.subtract).then_inc(ul_ready, 1)
                    chain.leave(size)
                n += 2 * size
                done += size

                def down(j, t, more):
                    for half in range(2):
                        dve.wait_ge(full[half], at(t.n + 1))
                        dst = res[:, ds(j, 1), half * HALF:(half + 1) * HALF].rearrange("p a n -> p (a n)")
                        vec.scalar_tensor_tensor(out=dst, in0=ps[:, half, :], scalar=mod[:, ds(j + 5 * KT, 1), 0],
                                                 in1=dst, op0=ALU.mult, op1=ALU.add).then_inc(drained[half], 1)
                    if more:
                        lo_split(t.ahead(2))
                last = group == len(GROUPS) - 1
                with dve.Fori(0, KT // 2 - last) as i:
                    for k in range(2):
                        down(2 * i + k, Tile(n + k, 2, i), True)
                if last:
                    for k in range(2):
                        down(KT - 2 + k, Tile(n + KT - 2 + k), False)
                n += KT

            dve.wait_ge(gbc_in, 16)
            for l in range(NL):
                dve.wait_ge(f_rms, at(l + 1))
                if l >= 2:
                    dve.wait_ge(y_out[l % 2], 16 * (l // 2))
                vec.scalar_tensor_tensor(out=o_out[:, l % 2, :],
                                         in0=ps[:, 2 * (l % 4):2 * (l % 4) + 2, :].rearrange("p b n -> p (b n)"),
                                         scalar=st3[:, 16 + l:17 + l], in1=gbc[:, :], op0=ALU.mult,
                                         op1=ALU.mult).then_inc(f_ready, 1)

        @block.gpsimd
        def _(pool):
            for s_ in credited:
                pool.sem_inc(s_, 1)
            made = [0]

            def make(ins):
                ins.then_inc(setup, 1)
                made[0] += 1
                pool.wait_ge(setup, at(made[0]))

            gp = nc.gpsimd
            for b in range(3):
                src = ctx_tok if b == 2 else x_tok[:, 4 * b:4 * b + 4, :]
                gp.dma_start(x_in[:, 4 * b:4 * b + (NCC if b == 2 else 4), :], src).then_inc(x_loaded[b], 16)
            make(gp.memset(ident[:, :], 0.0))
            make(gp.affine_select(out=ident[:, :], in_=ident[:, :], compare_op=ALU.not_equal, fill=1.0, base=0,
                                  pattern=[[-1, P]], channel_multiplier=1))
            make(gp.memset(ones[:, :], 1.0))
            for tri, sign in ((late, 1), (early, -1)):
                make(gp.memset(tri[:, :], 0.0))
                make(gp.affine_select(out=tri[:, :], in_=tri[:, :], compare_op=ALU.is_ge, fill=BIG, base=0,
                                      pattern=[[sign, P]], channel_multiplier=-sign))
            make(gp.memset(power[:, :], -0.5))
            make(gp.memset(zero8[:, :], 0.0))
            make(gp.memset(gbias[:, :], 0.0))
            make(gp.memset(w_raw[:, 0], 0.0))

            def inverse_root(src, tmp, dst, scale, n, count):
                gp.tensor_scalar(tmp, src, scale, EPS, ALU.mult, ALU.add).then_inc(p_step, 1)
                pool.wait_ge(p_step, at(count))
                return gp.tensor_tensor(dst, tmp, power[:, 0:n], ALU.pow)

            for b in range(3):
                n = 4 if b < 2 else NCC
                pool.wait_ge(sumsq, at(4 * b + n))
                inverse_root(*(stat[:, q, 4 * b:4 * b + n] for q in range(3)), 1.0 / D, n, b + 1).then_inc(rms, 1)

            pool.wait_ge(act_lo, at(3 * KT))
            make(gp.memset(g_r[:, :], 1.0))
            make(gp.memset(g_r[0:32, 0::CH], 0.0))
            make(gp.memset(g_r[32:64, CH - 1::CH], 0.0))
            make(gp.memset(raw[:, 0:1], 0.0))
            make(gp.memset(raw[:, T + 1:T + 3], 0.0))
            make(gp.memset(raw[:, T + TC + 3:T + TC + 4], 0.0))
            pool.wait_ge(row_v, at(ROW_M))
            for d in range(2):
                gp.dma_start(m_rows[d], g_m[32 * d:32 * d + H, :]).then_inc(gb_out, 16)
            pool.wait_ge(row_a, at(ROW_A))
            for d in range(2):
                gp.dma_start(a_rows[d], g_f[32 * d:32 * d + H, :]).then_inc(gb_out, 16)
            pool.wait_ge(gb_out, 64)
            pool.wait_ge(row_cols, at(3))

            def broadcast_rows(g):
                for d in range(2):
                    gp.dma_start(m_bc[:, d, :], m_rows[d, ds(g, 1), TC:TA].broadcast_to([P, T])).then_inc(bc_in, 16)
                    gp.dma_start(a_bc[:, d, :], a_rows[d, ds(g, 1), :].broadcast_to([P, TA])).then_inc(bc_in, 16)
            broadcast_rows(0)
            make(gp.memset(v_tok[:, :, P:VW], 1.0))

            def head_norm(g):
                pool.wait_ge(ss_ready, at(g + 1))
                pool.wait_ge(hn_ready, at(g))
                gp.tensor_tensor(tiny[:, 64:72], tiny[:, 56:64], power[:, :], ALU.pow).then_inc(rn_ready, 1)

            def store_head(g):
                pool.wait_ge(at_ready, at(2 * g + 2))
                gp.dma_start(a_dram[ds(g, 1)].rearrange("a p n -> p (a n)"),
                             pt[:, :, :].rearrange("p c n -> p (c n)")).then_inc(a_out, 16)
                pool.wait_ge(a_out, 16 * (g + 1))
                pool.sem_inc(a_stored, 1)

            with pool.Fori(1, H) as i:
                pool.wait_ge(state_ready, at(6 * i))
                broadcast_rows(i)
                head_norm(i - 1)
                store_head(i - 1)

            def late_load(p, q):
                columns = adw[:, :, ds(PASS * AC * p + (NAL1 + q) * AC, AC)]
                gp.dma_start(aw[:, q % 2], columns).then_inc(late_in[q % 2], 16)
            pool.wait_ge(expo_ready, at(2 * H))
            late_load(0, 0)
            pool.wait_ge(state_ready, at(6 * H))
            late_load(0, 1)
            head_norm(H - 1)
            store_head(H - 1)
            for q in (2, 3):
                pool.wait_ge(acc_ready, at(q - 1))
                late_load(0, q)
            with pool.Fori(1, KT // 2) as p:
                for q in range(PASS):
                    pool.wait_ge(acc_ready, at(PASS * p + (q - 1)))
                    late_load(p, q)

            pool.wait_ge(mod_done, at(NAL1 + KT // 2))
            for k in range(KT):
                if k >= 2:
                    pool.wait_ge(br_lo_ready, at(KT + k - 1))
                gp.dma_start(b_raw[:, k % 2, :], a_dram[k]).then_inc(br_in[k % 2], 16)

            pool.wait_ge(br_lo_ready, at(2 * KT))
            for k in range(2):
                gp.dma_start(x_j[:, k], x_tok[:, :, k * P:(k + 1) * P]).then_inc(xj_in[k], 16)
            with pool.Fori(1, KT // 2) as i:
                for k in range(2):
                    pool.wait_ge(xj_turned, at(2 * i + (k - 1)))
                    gp.dma_start(x_j[:, k], x_tok[:, :, ds(i * (2 * P) + k * P, P)]).then_inc(xj_in[k], 16)
            pool.wait_ge(n2_sum, at(1))
            gp.tensor_tensor(st2[:, 1, :], st2[:, 0, :], power[:, :], ALU.pow).then_inc(n2_rms, 1)

            pool.wait_ge(ul_ready, at(FT))
            gp.dma_start(gbc[:, :], final_g.rearrange("(a d) -> a d", a=1).broadcast_to([P, D])).then_inc(gbc_in, 16)
            for l in range(NL):
                pool.wait_ge(f_sum, at(l + 1))
                inverse_root(*(st3[:, 8 * q + l:8 * q + l + 1] for q in range(3)), 1.0 / D, 1, 4 + l).then_inc(f_rms, 1)

        @block.sync
        def _(sp):
            def par_rows(row, src, n):
                sp.dma_start(prow[row % P:row % P + n, row // P, :], src).then_inc(par_in, 16)

            def tiles(v, pattern="(t p) -> t p"):
                return v.rearrange(pattern, p=P)
            par_rows(ADA_B, tiles(ada_b[0]), 48)
            par_rows(N1G, tiles(norm1_g[0]), KT)
            par_rows(N2G, tiles(norm2_g[0]), KT)
            par_rows(C_X, tiles(c[0]), KT)
            par_rows(C_CTX, tiles(c_ctx), KT)
            par_rows(MNG, tiles(mnorm_g[0]), KT)
            par_rows(SCB, tiles(sc_conv_b[0]), KT)
            par_rows(SCW, tiles(sc_conv_w[0], "a (t p) -> (a t) p"), 3 * KT)
            par_rows(QKW, tiles(qk_conv_w[0], "a (t p) -> (a t) p"), 6 * KT)
            par_rows(QKB, tiles(qk_conv_b[0]), 2 * KT)
            par_rows(FFB, tiles(ff_conv_b[0]), FT)
            ffw = tiles(ff_conv_w[0], "a b (t p) -> (a b t) p")
            par_rows(FFW, ffw[0:P], P)
            par_rows(FFW + P, ffw[P:9 * FT], 9 * FT - P)
            def ada_load(n):
                sp.dma_start(aw0[:, n % NAS], adw[:, :, n * AC:(n + 1) * AC]).then_inc(ada_in[n % NAS], 16)
            for n in range(NAS):
                ada_load(n)
            sp.wait_ge(setup, at(10))
            gb = gate_b[0].rearrange("(g h a) -> g h a", g=4, a=1)
            for d in range(2):
                for k in range(2):
                    sp.dma_start(gbias[32 * d:32 * d + H, k:k + 1], gb[2 * d + k]).then_inc(gb_in, 16)
            sp.wait_ge(setup, at(11))
            for k in range(2):
                for d in range(2):
                    c0 = 64 * k + 32 * d
                    w0 = OFF_G + H * (2 * d + k)
                    sp.dma_start(w_raw[:, 0, :, c0:c0 + H], win[:, :, w0:w0 + H]).then_inc(raw_in[0], 16)

            for n in range(NAS, NAL1):
                sp.wait_ge(mod_done, at(n - NAS + 1))
                ada_load(n)

            def load(t, src, col, kt=KT):
                columns = src[:, :, ds(col, P)]
                sp.wait_ge(lo_ready, at(t.n - 1))
                sp.dma_start(w_raw[:, t.slot, 0:kt], columns).then_inc(raw_in[t.slot], 16)

            with sp.Fori(0, H) as i:
                for k, off in enumerate((OFF_Q, OFF_K, OFF_V, OFF_O)):
                    load(Tile(N_HEAD + k, 4, i), win, i * P + off)
            with sp.Fori(0, KT // 2) as i:
                for k in range(6):
                    load(Tile(N_CONV + k, 6, i), win, i * (2 * P) + (k // 3 * P + (OFF_SC, OFF_SX, OFF_SB)[k % 3]))
            for base, off, w in ((N_MIX_C, OFF_MG + D, wco), (N_MIX_M, OFF_MG, wmo)):
                for k in range(2):
                    load(Tile(base + k), win, off + k * P)
                with sp.Fori(0, KT // 2 - 1) as i:
                    for k in range(2):
                        load(Tile(base + 2 * k + 2, 4, i), w, i * (2 * P) + k * P)
                        load(Tile(base + 2 * k + 3, 4, i), win, i * (2 * P) + (off + (k + 2) * P))
                for k in range(2):
                    load(Tile(base + 2 * KT - 2 + k), w, (KT - 2 + k) * P)
            with sp.Fori(0, KT // 2) as i:
                for k in range(2):
                    load(Tile(N_WO + k, 2, i), wo_, i * (2 * P) + k * P)
            n, done = N_FFN, 0
            for size in GROUPS:
                with sp.Fori(0, size) as i:
                    load(Tile(n, 2, i), wup, i * P + done * P)
                    load(Tile(n + 1, 2, i), wup, i * P + (FF + done * P))
                n += 2 * size
                with sp.Fori(0, KT // 2) as i:
                    for k in range(2):
                        load(Tile(n + k, 2, i), wdn[:, done:done + size, :], i * (2 * P) + k * P, size)
                n += KT
                done += size
            for l in range(NL):
                sp.wait_ge(f_ready, at(l + 1))
                sp.dma_start(out_tok[l], o_out[:, l % 2, :]).then_inc(y_out[l % 2], 16)
            for s_ in y_out:
                sp.wait_ge(s_, 16 * (NL // 2))


_INS = ["x", "c", "ctx", "c_ctx", "ada_w", "ada_b", "norm1_g", "norm2_g", "w_in", "qk_conv_w", "qk_conv_b",
        "gate_b", "mnorm_g", "w_m_out", "sc_conv_w", "sc_conv_b", "w_c_out", "w_o", "w_up", "ff_conv_w",
        "ff_conv_b", "w_down", "final_g"]


def kernel(**inputs):
    import numpy as np
    import concourse.bacc as bacc
    from concourse.bass_utils import run_bass_kernel_spmd

    nc = bacc.Bacc("TRN2", target_bir_lowering=False, num_devices=1)
    arrays, args = {}, []
    for name in _INS:
        a = np.ascontiguousarray(inputs[name])
        arrays[f"in_{name}"] = a
        args.append(nc.dram_tensor(f"in_{name}", a.shape, mybir.dt.from_np(a.dtype), kind="ExternalInput").ap())
    out = nc.dram_tensor("out_x", (1, T, D), F32, kind="ExternalOutput").ap()
    layer(nc, *args, out)
    r = run_bass_kernel_spmd(nc, [arrays], core_ids=[0])
    return r.results[0]["out_x"]
```

```python
from contextlib import ExitStack

import concourse.bass as bass
from concourse import mybir

F32 = mybir.dt.float32
F32R = mybir.dt.float32r
ALU = mybir.AluOpType
ACT = mybir.ActivationFunctionType
AX_X = mybir.AxisListType.X

P = 128
D = 1024
KT = D // P
T = 1024
TC = 256
TA = TC + T
HALF = 512
H = 8
CH = 128
NC = TA // CH
NCC = TC // CH
NL = T // CH
VW = P + 1
GRID = 64
ROWS = T // GRID
AC = 256
NAL = 6 * D // AC
NAL1 = 2 * D // AC
NAS = 5
NBR = 3
PASS = 4
JP = PASS * AC // P
FF = 2816
FT = FF // P
GROUPS = (8, 7, 7)
EPS = 1e-6
NEG = -1e30
BIG = 1e30
EXP_MAX = 88.0
SCALE = float(P) ** -0.5

OFF_Q, OFF_K, OFF_V, OFF_G = 0, D, 2 * D, 3 * D
OFF_O = OFF_G + 4 * H
OFF_SB, OFF_SC, OFF_SX, OFF_MG = OFF_O + D, OFF_O + 2 * D, OFF_O + 3 * D, OFF_O + 4 * D

ADA_B, N1G, N2G, MNG, SCB, SCW = 0, 48, 56, 64, 72, 80
QKW, QKB, FFB, FFW = 128, 176, 192, 256
PAR_ROWS = (SCW + 3 * KT, FFB + FF // P - 128, 128, 9 * (FF // P) - 128)
B_CTX, B_S, B_T, B_G, B_O = 2, 3, 5, 6, 7
B_KV = (B_T, B_G, B_O, B_T, B_G)

SET_IDENT, SET_GBIAS, SET_WRAW, SET_MARKS, SET_RAW, N_SETUP = 2, 9, 10, 13, 16, 17
N_PAR = 11
SCAN = ([*range(NC - 1)], [*range(NCC)][::-1] + [*range(NCC + 1, NC)][::-1])
OUT = (((0, 1, 2), (3, 4, 5), (6, 7)), ((5, 6, 7), (2, 3, 4), (0, 1)))
ROW_ABS, ROW_U, ROW_M, ROW_AX, ROW_WX, ROW_EX = 2, 11, 19, 27, 28, 30
ROW_EXP, ROW_LN, ROW_A, ROW_WK, ROW_EM = 1, 2, 3, 4, 5

V_HEAD = 37

N_GATE = 0
N_HEAD = 1
N_CONV = N_HEAD + 4 * H
N_MIX_C = N_CONV + 3 * KT
N_MIX_M = N_MIX_C + 2 * KT
N_WO = N_MIX_M + 2 * KT
N_FFN = N_WO + KT
N_ALL = N_FFN + 2 * FT + len(GROUPS) * KT


def at(count):
    return count + 1


class Tile:

    def __init__(self, base, per=0, i=0):
        self.slot = base % 2
        self.n = base + per * i if per else base
        self.nth = base // 2 + (per // 2) * i if per else base // 2
        self.base, self.per, self.i = base, per, i

    def ahead(self, k):
        return Tile(self.base + k, self.per, self.i)


class Chain:

    def __init__(self, eng, sem):
        self.eng, self.sem, self.count, self.i, self.first = eng, sem, 0, None, 0

    def step(self, ins):
        ins.then_inc(self.sem, 1)
        self.count += 1
        self.eng.wait_ge(self.sem, self.value())

    def value(self):
        if self.i is None:
            return at(self.count)
        return self.per * (self.i - self.first) + at(self.count)

    def enter(self, i, first, per):
        self.i, self.first, self.per, self.began = i, first, per, self.count

    def leave(self, passes):
        assert self.count - self.began == self.per, (self.count - self.began, self.per)
        self.i = None
        self.count = self.began + passes * self.per


def layer(nc, x, c, ctx, c_ctx, ada_w, ada_b, norm1_g, norm2_g, w_in, qk_conv_w, qk_conv_b, gate_b,
          mnorm_g, w_m_out, sc_conv_w, sc_conv_b, w_c_out, w_o, w_up, ff_conv_w, ff_conv_b, w_down,
          final_g, out):
    ds = bass.ds
    m_rows = nc.dram_tensor("m_rows", (2, H, TA), F32, kind="Internal").ap()
    a_rows = nc.dram_tensor("a_rows", (2, H, TA), F32, kind="Internal").ap()
    a_dram = nc.dram_tensor("branch_a", (KT, P, T), F32, kind="Internal").ap()
    z_dram = nc.dram_tensor("branch_z", (KT, P, T), F32, kind="Internal").ap()

    def rows(w):
        return w.rearrange("(k p) n -> p k n", p=P)

    win, wup, wmo, wco, wo_, wdn = (rows(w[0]) for w in (w_in, w_up, w_m_out, w_c_out, w_o, w_down))
    adw = rows(ada_w[0])
    x_tok = x[0].rearrange("(j p) d -> p j d", p=P)
    ctx_tok = ctx[0].rearrange("(j p) d -> p j d", p=P)
    out_tok = out[0].rearrange("(j p) d -> j p d", p=P)

    ctx_ = ExitStack()
    with ctx_:
        def keep(name, shape, dt=F32):
            return ctx_.enter_context(nc.sbuf_tensor(name, shape, dt))

        def sem(name):
            return ctx_.enter_context(nc.semaphore(name))

        credited = []

        def csem(name):
            credited.append(sem(name))
            return credited[-1]

        op_hi = keep("op_hi", [P, KT, T], F32R)
        op_lo = keep("op_lo", [P, KT, T], F32R)
        w_raw = keep("w_raw", [P, 2, KT, P])
        w_hi = keep("w_hi", [P, 2, KT, P], F32R)
        w_lo = keep("w_lo", [P, 2, KT, P], F32R)
        ident = keep("ident", [P, P])
        ones = keep("ones", [P, P])
        par = keep("par", [P, 4 * P])
        mod = keep("mod", [P, 48, 2])
        gain = keep("gain", [P, 3, KT])
        power = keep("power", [P, KT])
        gate5 = keep("gate5", [P, KT])

        def scoped(*tensors):
            with ExitStack() as s:
                return [s.enter_context(nc.sbuf_tensor(n, sh, dt)) for n, sh, dt in tensors]

        cs = keep("cs", [P, KT, 2])
        st2 = keep("st2", [P, 2, NL])
        st3 = keep("st3", [P, 24])
        ctx_hi, ctx_lo, cols, late, early, *above = scoped(
            ("ctx_hi", [P, KT, TC], F32R), ("ctx_lo", [P, KT, TC], F32R),
            ("cols", [P, 3, NC, 2, H], F32),
            ("late", [P, P], F32), ("early", [P, P], F32),
            ("raw", [P, T + TC + 8], F32),
            ("conv", [P, TA], F32), ("q_t", [P, T], F32), ("og", [P, T], F32), ("k_t", [P, TA], F32),
            ("v_t", [P, TA], F32),
            ("m_bc", [P, 2, T], F32), ("a_bc", [P, 2, TA], F32), ("k_tok", [P, NC, P], F32),
            ("v_tok", [P, NC, VW], F32), ("wgt", [P, NL, CH], F32), ("pt", [P, NL, CH], F32),
            ("qs", [P, 2, T], F32), ("vw", [P, NC, VW], F32), ("state", [P, 2, NC - 1, VW], F32),
            ("h_tok", [P, NL, P], F32), ("tiny", [P, 96], F32), ("h_tmp", [P, 3, P], F32))
        (raw, conv, q_t, og, k_t, v_t, m_bc, a_bc, k_tok, v_tok, wgt, pt, qs, vw, state, h_tok, tiny, h_tmp) = above
        LOW = 2 * KT * TC
        SHARED = LOW + 3 * NC * 2 * H + 2 * P
        HEADS = SHARED + (T + TC + 8) + 3 * TA + 2 * T
        _, x_in, ht, aw0, prow, crow, mrow, stat, gbias, mp = scoped(
            ("below_x", [P, SHARED], F32), ("x_in", [P, NC, D], F32), ("ht", [P, 2, HALF], F32),
            ("aw0", [P, NAS, KT, AC], F32), ("prow", [P, 4, P], F32), ("crow", [2 * KT, P], F32),
            ("mrow", [2, 2 * D], F32), ("stat", [P, 3, 16], F32), ("gbias", [64, 2], F32), ("mp", [64, 2, NC], F32))
        _, g_i, g_f, g_e, g_b, g_m, g_d, g_r, g_s = scoped(
            ("below_g", [P, HEADS], F32), *[(f"g_{n}", [64, TA], F32) for n in "ifebmdrs"])
        _, aw, acc = scoped(("below_aw", [P, HEADS], F32), ("aw", [P, 2, KT, AC], F32),
                            ("acc", [P, PASS, AC], F32))
        (br_hi01, br_lo01, res, gth, b_raw, br_hi27, br_lo27) = scoped(
            ("br_hi01", [P, 2, T], F32R), ("br_lo01", [P, 2, T], F32R),
            ("res", [P, KT, T], F32),
            ("gth", [P, 2, T], F32),
            ("b_raw", [P, NBR, T], F32),
            ("br_hi27", [P, KT - 2, T], F32R), ("br_lo27", [P, KT - 2, T], F32R))
        _, sq, sqsum, u_t, x_j = scoped(("below_sq", [P, LOW + KT * T], F32), ("sq", [P, T], F32),
                                        ("sqsum", [P, T], F32), ("u_t", [P, 2, HALF], F32),
                                        ("x_j", [P, 2, NL, P], F32))
        _, hid_hi, hid_lo, u_h = scoped(("below_hid", [P, LOW + KT * T], F32), ("hid_hi", [P, KT, T], F32R),
                                        ("hid_lo", [P, KT, T], F32R), ("u_h", [P, 2, HALF], F32))
        a_pad, cv, gv, diag = scoped(("a_pad", [P, ROWS + 2, GRID + 2], F32), ("cv", [P, T], F32),
                                     ("gv", [P, T], F32), ("diag", [P, NL // 2, P], F32))
        gbc, junk = scoped(("gbc", [P, D], F32), ("junk", [P, D], F32))
        _, o_out = scoped(("below_out", [P, LOW + KT * T], F32), ("o_out", [P, NL, D], F32))
        ps = ctx_.enter_context(nc.psum_tensor("ps", [P, 8, 512], F32))

        cond_in, par_in, gb_in = sem("cond_in"), sem("par_in"), sem("gb_in")
        x_loaded = [sem(f"x_loaded{b}") for b in range(3)]
        ada_in = [sem(f"ada_in{b}") for b in range(NAS)]
        late_in = [sem(f"late_in{b}") for b in range(2)]
        raw_in = [sem(f"raw_in{b}") for b in range(2)]
        gb_out = sem("rows_out")
        bc_in = sem("bc_in")
        a_out = sem("a_out")
        br_in = [sem(f"br_in{b}") for b in range(NBR)]
        xj_in = [sem(f"xj_in{b}") for b in range(2)]
        gbc_in, y_out = sem("gbc_in"), sem("y_out")

        def csems(names):
            return [csem(n) for n in names.split()]
        setup, = csems("setup")
        cond_turned, cond_ready = csems("cond_turned cond_ready")
        par_turned, par_ready = csems("par_turned par_ready")
        mod_done, mrow_ready, mod_turned, mod_ready = csems("mod_done mrow_ready mod_turned mod_ready")
        sumsq, rms, x_scaled = csems("sumsq rms x_scaled")
        x_turned, x_mod = csems("x_turned x_mod")
        act_hi, act_lo = csems("act_hi act_lo")
        hi_ready, lo_ready = csems("hi_ready lo_ready")
        full = [csem(f"full{b}") for b in range(2)]
        drained = [csem(f"drained{b}") for b in range(2)]
        ctx_full, ctx_drained = csems("ctx_full ctx_drained")
        row_v, row_a, row_turned, row_cols = csems("row_v row_a row_turned row_cols")
        conv_ready, tanh_ready, q_ready, k_ready, og_ready = csems("conv_ready tanh_ready q_ready k_ready og_ready")
        turned, tok_ready = csems("turned tok_ready")
        s_full, expo_ready, wexp_ready, pt_ready = csems("s_full expo_ready wexp_ready pt_ready")
        qs_ready, vw_ready, g_full, state_ready = csems("qs_ready vw_ready g_full state_ready")
        o_full, den_ready, h_ready = csems("o_full den_ready h_ready")
        sq_ready, ss_ready, rn_ready, hn_ready = csems("sq_ready ss_ready rn_ready hn_ready")
        h_turned, at_ready, a_stored = csems("h_turned at_ready a_stored")
        v_step, p_step = csems("v_step p_step")
        acc_ready, mod_read, z_hi_ready = csems("acc_ready mod_read z_hi_ready")
        br_hi_ready, br_lo_ready, mix_ready = csems("br_hi_ready br_lo_ready mix_ready")
        xj_turned, xres_ready, sqsum_ready, stat_done = csems("xj_turned xres_ready sqsum_ready stat_done")
        n2_sum, n2_rms, n2_ready, factor_spread, ut_ready = csems("n2_sum n2_rms n2_ready factor_spread ut_ready")
        pad_ready, cv_ready, gelu_ready, u_ready, uh_ready, ul_ready = csems(
            "pad_ready cv_ready gelu_ready u_ready uh_ready ul_ready")
        f_turned, f_sum, f_rms, f_ready = csems("f_turned f_sum f_rms f_ready")

        block = ctx_.enter_context(nc.Block())

        op = [(op_hi[:, k, :], op_lo[:, k, :]) for k in range(KT)]
        ctx_op = [(ctx_hi[:, k, :], ctx_lo[:, k, :]) for k in range(KT)]
        br = [(br_hi01[:, k, :], br_lo01[:, k, :]) for k in range(2)] + \
             [(br_hi27[:, k, :], br_lo27[:, k, :]) for k in range(KT - 2)]
        hid = [(hid_hi[:, k, :], hid_lo[:, k, :]) for k in range(KT)]

        def products(dst, t, src, sl, ks, first, last, ready=None):
            for k in ks:
                if ready is not None:
                    nc.tensor.wait_ge(act_lo, at(ready + k + 1))
                hi, lo = src[k]
                for w, a in ((w_hi, hi), (w_hi, lo), (w_lo, hi)):
                    ins = nc.tensor.matmul(dst, w[:, t.slot, k, :], a[:, sl],
                                           start=(k == first and w is w_hi and a is hi),
                                           stop=(k == last and w is w_lo))
            return ins

        HALVES = (slice(0, HALF), slice(HALF, T))

        @block.tensor
        def _(pe):
            def weights(t):
                pe.wait_ge(hi_ready, at(t.n + 1))
                pe.wait_ge(lo_ready, at(t.n + 1))

            def half_tile(t, half, between=None, src=op, ready=None):
                if half == 0:
                    weights(t)
                pe.wait_ge(drained[half], at(t.n))
                products(ps[:, half, :], t, src, HALVES[half], range(KT // 2), 0, KT - 1, ready)
                if between:
                    between()
                products(ps[:, half, :], t, src, HALVES[half], range(KT // 2, KT), 0, KT - 1,
                         ready).then_inc(full[half], 1)

            def ctx_tile(t, nth):
                weights(t)
                pe.wait_ge(ctx_drained, at(nth))
                products(ps[:, B_CTX, 0:TC], t, ctx_op, slice(0, TC), range(KT), 0, KT - 1).then_inc(ctx_full, 1)

            pe.wait_ge(setup, at(SET_IDENT))
            pe.wait_ge(cond_in, 32)
            nc.tensor.transpose(ps[:, 0, 0:2 * KT], crow[:, :], ident[0:2 * KT, 0:2 * KT]).then_inc(cond_turned, 1)
            pe.wait_ge(cond_ready, at(2))
            for load in range(NAL1):
                pe.wait_ge(ada_in[load % NAS], 16 * (load // NAS + 1))
                for k in range(KT):
                    ins = nc.tensor.matmul(ps[0:2, B_CTX + load // 2, (load % 2) * AC:(load % 2 + 1) * AC], cs[:, k, :],
                                           aw0[:, load % NAS, k, :], start=(k == 0), stop=(k == KT - 1))
                ins.then_inc(mod_done, 1)
                if load == 3:
                    pe.wait_ge(par_in, 16 * N_PAR)
                    for q, n in enumerate(PAR_ROWS):
                        nc.tensor.transpose(ps[:, 1, q * P:q * P + n], prow[0:n, q, :],
                                            ident[0:n, 0:n]).then_inc(par_turned, 1)
            for jt in range(2 * KT):
                pe.wait_ge(mrow_ready, at(jt // 4 + 1))
                ins = nc.tensor.transpose(ps[:, 0, 2 * jt:2 * jt + 2], mrow[:, jt * P:(jt + 1) * P], ident[0:2, 0:2])
            ins.then_inc(mod_turned, 1)

            def turn_input(t):
                b, k = t // KT, t % KT
                n = 4 if b < 2 else NCC
                if k == 0:
                    pe.wait_ge(x_scaled, at(4 * b + n))
                if t >= 3:
                    pe.wait_ge(x_mod, at(t - 2))
                else:
                    pe.wait_ge(mrow_ready, at(4))
                for j in range(n):
                    ins = nc.tensor.transpose(ps[:, B_S + t % 3, j * P:(j + 1) * P],
                                              x_in[:, 4 * b + j, k * P:(k + 1) * P], ident[:, :])
                ins.then_inc(x_turned, 1)

            for t in range(3):
                turn_input(t)
            weights(Tile(N_GATE))
            for t in range(3 * KT):
                half, k = t // KT, t % KT
                dst, src, sl = ((ps[:, half, :], op, HALVES[half]) if half < 2 else
                                (ps[:, B_CTX, 0:TC], ctx_op, slice(0, TC)))
                pe.wait_ge(act_lo, at(t + 1))
                ins = products(dst, Tile(N_GATE), src, sl, (k,), 0, KT - 1)
                if k == KT - 1:
                    ins.then_inc((full[0], full[1], ctx_full)[half], 1)
                if t + 3 < 3 * KT:
                    turn_input(t + 3)

            for k in range(4):
                t = Tile(N_HEAD + k)
                if k in (1, 2):
                    ctx_tile(t, k)
                for half in range(2):
                    half_tile(t, half)
            for q in range(3):
                pe.wait_ge(row_v if q == 0 else row_a, at(ROW_U if q == 0 else (ROW_WK if q == 1 else ROW_EM)))
                pe.wait_ge(row_cols, at(q))
                for ch in range(NC):
                    ins = nc.tensor.transpose(ps[:, B_S + ch // 8, (ch % 8) * 64:(ch % 8) * 64 + 64],
                                              (g_i, g_e, g_s)[q][:, ch * P:(ch + 1) * P], ident[0:64, 0:64])
                ins.then_inc(row_turned, 1)

            def turn_kv(g, j):
                if j == 0:
                    pe.wait_ge(at_ready, at(2 * g))
                    pe.wait_ge(state_ready, at(6 * g))
                    pe.wait_ge(h_ready, at(6 * g))
                    pe.wait_ge(k_ready, at(g + 1))
                    pe.wait_ge(drained[0], at(N_HEAD + 4 * g + 3))
                    pe.wait_ge(drained[1], at(N_HEAD + 4 * g + 3))
                    pe.wait_ge(ctx_drained, at(2 * g + 3))
                elif j >= 3:
                    pe.wait_ge(tok_ready, at(5 * g + j - 2))
                src = ((k_t, 2), (k_t, 6), (v_t, 2), (v_t, 6), (None, 0))[j]
                for q in range(4):
                    if j < 4:
                        a = src[0][:, (src[1] + q) * P:(src[1] + q + 1) * P]
                    else:
                        a = (k_t if q < 2 else v_t)[:, (q % 2) * P:(q % 2 + 1) * P]
                    ins = nc.tensor.transpose(ps[:, B_KV[j], q * P:(q + 1) * P], a, ident[:, :])
                ins.then_inc(turned, 1)

            def scores(g, j):
                pe.wait_ge(q_ready, at(g + 1))
                pe.wait_ge(k_ready, at(g + 1))
                pe.wait_ge(pt_ready, at(4 * g))
                if j == 0:
                    pe.wait_ge(row_cols, at(3))
                for q in range(4):
                    l = 4 * j + q
                    ins = nc.tensor.matmul(ps[:, B_S + j, q * CH:(q + 1) * CH], k_t[:, TC + l * CH:TC + (l + 1) * CH],
                                           q_t[:, l * CH:(l + 1) * CH], start=True, stop=True)
                ins.then_inc(s_full, 1)

            def outer(g, d, j):
                pe.wait_ge(tok_ready, at(5 * g + 5))
                pe.wait_ge(vw_ready, at(2 * g + d + 1))
                pe.wait_ge(state_ready, at(6 * g + 3 * d + j))
                for q in range(3):
                    ch = SCAN[d][3 * j + q]
                    ins = nc.tensor.matmul(ps[:, B_G, q * VW:(q + 1) * VW], k_tok[:, ch, :], vw[:, ch, :],
                                           start=True, stop=True)
                ins.then_inc(g_full, 1)

            def outputs(g, d, j):
                pe.wait_ge(pt_ready, at(4 * g + 2 * d + 2))
                pe.wait_ge(qs_ready, at(2 * g + d + 1))
                pe.wait_ge(state_ready, at(6 * g + 3 * d + 3))
                pe.wait_ge(h_ready, at(6 * g + 3 * d + j))
                for q, l in enumerate(OUT[d][j]):
                    o = ps[:, B_O, q * VW:(q + 1) * VW]
                    nc.tensor.matmul(o, pt[:, l, :], v_tok[:, NCC + l, :], start=True, stop=False)
                    ins = nc.tensor.matmul(o, qs[:, d, l * CH:(l + 1) * CH],
                                           state[:, d, 1 + (l if d == 0 else NL - 1 - l), :], start=False, stop=True)
                ins.then_inc(o_full, 1)

            def turn_h(g):
                pe.wait_ge(hn_ready, at(g + 1))
                pe.wait_ge(tok_ready, at(5 * g + 5))
                pe.wait_ge(state_ready, at(6 * g + 6))
                for j in range(2):
                    for q in range(4):
                        ins = nc.tensor.transpose(ps[:, B_T + j, q * P:(q + 1) * P], h_tok[:, 4 * j + q, :],
                                                  ident[:, :])
                    ins.then_inc(h_turned, 1)

            def mlstm(g):
                yield lambda: (turn_kv(g, 0), turn_kv(g, 1), scores(g, 0), scores(g, 1))
                yield lambda: (turn_kv(g, 2), turn_kv(g, 3))
                yield lambda: turn_kv(g, 4)
                yield lambda: outer(g, 0, 0)
                yield lambda: outer(g, 0, 1)
                yield lambda: outer(g, 0, 2)
                yield lambda: None
                yield lambda: outputs(g, 0, 0)
                yield lambda: outputs(g, 0, 1)
                yield lambda: (outputs(g, 0, 2), outer(g, 1, 0))
                yield lambda: outer(g, 1, 1)
                yield lambda: outer(g, 1, 2)
                yield lambda: outputs(g, 1, 0)
                yield lambda: outputs(g, 1, 1)
                yield lambda: outputs(g, 1, 2)
                yield lambda: None
                yield lambda: None
                yield lambda: turn_h(g)

            with pe.Fori(1, H) as i:
                steps = mlstm(i - 1)
                for k in range(4):
                    t = Tile(N_HEAD + k, 4, i)
                    if k in (1, 2):
                        ctx_tile(t, 2 * i + k)
                        next(steps)()
                    for half in range(2):
                        half_tile(t, half, next(steps))
                        if (k, half) != (3, 1):
                            next(steps)()
                for step in steps:
                    step()

            def late_modulation(p):
                pe.wait_ge(acc_ready, at(PASS * p + PASS))
                for jt in range(JP):
                    ins = nc.tensor.matmul(ps[:, B_G, jt:jt + 1], acc[:, jt // 2, (jt % 2) * P:(jt % 2 + 1) * P],
                                           ones[:, 0:1], start=True, stop=True)
                ins.then_inc(mod_done, 1)

            steps = mlstm(H - 1)
            for k in range(6):
                for half in range(2):
                    half_tile(Tile(N_CONV + k), half, next(steps, None))
                    next(steps, lambda: None)()
            with pe.Fori(1, KT // 2) as i:
                for k in range(6):
                    for half in range(2):
                        half_tile(Tile(N_CONV + k, 6, i), half)
                    if k == 1:
                        late_modulation(i - 1)

            for stage, base in enumerate((N_MIX_C, N_MIX_M)):
                for k in range(2):
                    for half in range(2):
                        half_tile(Tile(base + k), half)
                if not stage:
                    late_modulation(KT // 2 - 1)
                pe.wait_ge(br_lo_ready, at(KT * (stage + 1)))
                with pe.Fori(0, KT // 2 - 1) as i:
                    for k in range(2):
                        for half in range(2):
                            half_tile(Tile(base + 2 * k + 2, 4, i), half, src=br)
                        for half in range(2):
                            half_tile(Tile(base + 2 * k + 3, 4, i), half)
                for k in range(2):
                    for half in range(2):
                        half_tile(Tile(base + 2 * KT - 2 + k), half, src=br)

            def turn_x(i, slot):
                j = 2 * i + slot
                pe.wait_ge(xj_in[slot], 16 * (i + 1))
                pe.wait_ge(xres_ready, at(j))
                for l in range(NL):
                    ins = nc.tensor.transpose(ps[:, B_S + l // 4, (l % 4) * P:(l % 4 + 1) * P],
                                              x_j[:, slot, l, :], ident[:, :])
                ins.then_inc(xj_turned, 1)

            with pe.Fori(0, KT // 2 - 1) as i:
                for k in range(2):
                    turn_x(i, k)
                    half_tile(Tile(N_WO + k, 2, i), 0, ready=3 * KT)
                    half_tile(Tile(N_WO + k, 2, i), 1)

            def token_sums(half):
                pe.wait_ge(sqsum_ready, at(2 * KT - 1 + half))
                for l in range(NL // 2):
                    ins = nc.tensor.matmul(ps[:, B_O, 4 * half + l:4 * half + l + 1],
                                           sqsum[:, half * HALF + l * P:half * HALF + (l + 1) * P], ones[:, 0:1],
                                           start=True, stop=True)
                ins.then_inc(stat_done, 1)

            def spread(half):
                pe.wait_ge(n2_ready, at(half + 1))
                nc.tensor.matmul(ps[:, B_S + half, :], ones[:, :], diag[:, :, :], start=True,
                                 stop=True).then_inc(factor_spread, 1)

            turn_x(KT // 2 - 1, 0)
            half_tile(Tile(N_WO + KT - 2), 0)
            half_tile(Tile(N_WO + KT - 2), 1)
            turn_x(KT // 2 - 1, 1)
            half_tile(Tile(N_WO + KT - 1), 0)
            half_tile(Tile(N_WO + KT - 1), 1, lambda: token_sums(0))
            spread(0)
            token_sums(1)

            n, done = N_FFN, 0
            for half in range(2):
                for k in range(2):
                    half_tile(Tile(n + k), half, (lambda: spread(1)) if (half, k) == (0, 0) else None,
                              ready=(4 + half) * KT if k == 0 else None)
            for size in GROUPS:
                with pe.Fori(0 if done else 1, size) as i:
                    for k in range(2):
                        for half in range(2):
                            half_tile(Tile(n + k, 2, i), half)
                n += 2 * size
                done += size

                pe.wait_ge(ul_ready, at(done - 1))
                weights(Tile(n))
                for half in range(2):
                    pe.wait_ge(drained[half], at(n))
                    products(ps[:, half, :], Tile(n), hid, HALVES[half], range(size - 1), 0, size - 1)
                pe.wait_ge(ul_ready, at(done))
                for half in range(2):
                    products(ps[:, half, :], Tile(n), hid, HALVES[half], (size - 1,), 0,
                             size - 1).then_inc(full[half], 1)

                def down(t):
                    weights(t)
                    for half in range(2):
                        pe.wait_ge(drained[half], at(t.n))
                        products(ps[:, half, :], t, hid, HALVES[half], range(size), 0, size - 1).then_inc(full[half], 1)
                down(Tile(n + 1))
                with pe.Fori(1, KT // 2) as i:
                    for k in range(2):
                        down(Tile(n + k, 2, i))
                n += KT

            for l in range(NL):
                if l == 0:
                    pe.wait_ge(drained[0], at(N_ALL))
                    pe.wait_ge(drained[1], at(N_ALL))
                if l >= 4:
                    pe.wait_ge(f_ready, at(l - 3))
                for k in range(KT):
                    ins = nc.tensor.transpose(ps[:, 2 * (l % 4) + k // 4, (k % 4) * P:(k % 4 + 1) * P],
                                              res[:, k, l * P:(l + 1) * P], ident[:, :])
                ins.then_inc(f_turned, 1)

        @block.scalar
        def _(act):
            def hi_split(t):
                act.wait_ge(raw_in[t.slot], 16 * (t.nth + 1) + (48 if t.slot == 0 else 0))
                act.wait_ge(full[1], at(t.n - 1))
                nc.scalar.copy(w_hi[:, t.slot], w_raw[:, t.slot]).then_inc(hi_ready, 1)

            act.wait_ge(cond_turned, at(1))
            for v in range(2):
                nc.scalar.activation(cs[:, :, v], ps[:, 0, v * KT:(v + 1) * KT], ACT.Silu).then_inc(cond_ready, 1)

            for b in range(3):
                act.wait_ge(x_loaded[b], 16)
                for j in range(4 if b < 2 else NCC):
                    act.wait_ge(sumsq, at(4 * b + j))
                    nc.scalar.activation(ps[:, B_G:B_G + 2, :].rearrange("p b n -> p (b n)"), x_in[:, 4 * b + j, :],
                                         ACT.Square, accum_out=stat[:, 0, 4 * b + j:4 * b + j + 1]).then_inc(sumsq, 1)

            def modulate(b):
                v, n = (0, HALF) if b < 2 else (1, TC)
                hi = op_hi[:, :, b * HALF:(b + 1) * HALF] if b < 2 else ctx_hi[:, :, :]
                for k in range(KT):
                    t = b * KT + k
                    act.wait_ge(x_turned, at(t + 1))
                    if t >= 2:
                        act.wait_ge(act_lo, at(t - 1))
                    nc.scalar.activation(ht[:, t % 2, 0:n], ps[:, B_S + t % 3, 0:n], ACT.Identity,
                                         scale=gain[:, v, k:k + 1], bias=mod[:, k, v:v + 1]).then_inc(x_mod, 1)
                    if k % 2 == 0:
                        act.wait_ge(x_mod, at(t + 1))
                        nc.scalar.copy(hi[:, k, :], ht[:, t % 2, 0:n]).then_inc(act_hi, 1)

            for n in range(2):
                act.wait_ge(raw_in[n], 64 if n == 0 else 16)
                nc.scalar.copy(w_hi[:, n], w_raw[:, n]).then_inc(hi_ready, 1)
            act.wait_ge(mod_ready, at(3))
            for b in range(3):
                modulate(b)

            for src, lo, n, f, d in ((0, TC, HALF, full[0], drained[0]), (1, TC + HALF, HALF, full[1], drained[1]),
                                     (B_CTX, 0, TC, ctx_full, ctx_drained)):
                act.wait_ge(f, at(1))
                act.wait_ge(act_lo, at(3 * KT))
                nc.scalar.copy(g_i[:, lo:lo + n], ps[0:64, src, 0:n])
                nc.scalar.copy(g_f[:, lo:lo + n], ps[64:128, src, 0:n]).then_inc(d, 1)
            hi_split(Tile(2))
            act.wait_ge(row_v, at(ROW_ABS))
            nc.scalar.activation(g_e[:, :], g_e[:, :], ACT.Exp).then_inc(row_a, 1)
            act.wait_ge(row_a, at(ROW_EXP))
            nc.scalar.activation(g_s[:, :], g_e[:, :], ACT.Ln, bias=1.0).then_inc(row_a, 1)

            def drain_half(i, k, half, dst, waits=()):
                n = N_HEAD + 4 * i + k
                act.wait_ge(full[half], at(n + 1))
                for s, c in waits:
                    act.wait_ge(s, at(c))
                nc.scalar.copy(dst, ps[:, half, :]).then_inc(drained[half], 1)

            def drain_ctx(i, k, dst, waits=()):
                act.wait_ge(ctx_full, at(2 * i + k + 1))
                for s, c in waits:
                    act.wait_ge(s, at(c))
                nc.scalar.copy(dst, ps[:, B_CTX, 0:TC]).then_inc(ctx_drained, 1)

            def o_half(i, half):
                act.wait_ge(full[half], at(N_HEAD + 4 * i + 4))
                act.wait_ge(k_ready, at(i + 1))
                nc.scalar.activation(conv[:, half * HALF:(half + 1) * HALF], ps[:, half, :], ACT.Tanh,
                                     scale=0.5).then_inc(drained[half], 1)

            def tanh_q(i):
                act.wait_ge(conv_ready, at(2 * i + 1))
                act.wait_ge(s_full, at(2 * i))
                act.wait_ge(qs_ready, at(2 * i))
                nc.scalar.activation(q_t[:, :], conv[:, TC:TA], ACT.Tanh, scale=0.5).then_inc(tanh_ready, 1)

            def tanh_k(i):
                act.wait_ge(conv_ready, at(2 * i + 2))
                act.wait_ge(turned, at(5 * i))
                act.wait_ge(s_full, at(2 * i))
                nc.scalar.activation(k_t[:, :], conv[:, :], ACT.Tanh, scale=0.5).then_inc(tanh_ready, 1)

            def q_half(i, half):
                drain_half(i, 0, half, raw[:, 1 + half * HALF:1 + (half + 1) * HALF], ((conv_ready, 2 * i),))

            def k_half(i, half):
                drain_half(i, 1, half, raw[:, 1 + half * HALF:1 + (half + 1) * HALF], ((conv_ready, 2 * i + 1),))

            def k_ctx(i):
                drain_ctx(i, 1, raw[:, T + 3:T + 3 + TC], ((conv_ready, 2 * i),))

            def v_half(i, half):
                drain_half(i, 2, half, v_t[:, TC + half * HALF:TC + (half + 1) * HALF], ((turned, 5 * i),))

            def v_ctx(i):
                drain_ctx(i, 2, v_t[:, 0:TC], ((turned, 5 * i),))

            def kv_tokens(g, j):
                act.wait_ge(turned, at(5 * g + j + 1))
                if j == 0:
                    act.wait_ge(g_full, at(6 * g))
                    act.wait_ge(o_full, at(6 * g))
                    act.wait_ge(row_cols, at(3))
                    act.wait_ge(setup, at(N_SETUP))
                src = ps[:, B_KV[j], :].rearrange("p (c n) -> p c n", n=P)
                if j < 2:
                    nc.scalar.copy(k_tok[:, NCC + 4 * j:NCC + 4 * j + 4, :], src).then_inc(tok_ready, 1)
                elif j < 4:
                    nc.scalar.copy(v_tok[:, NCC + 4 * j - 8:NCC + 4 * j - 4, 0:P], src).then_inc(tok_ready, 1)
                else:
                    nc.scalar.copy(k_tok[:, 0:NCC, :], src[:, 0:NCC, :])
                    nc.scalar.copy(v_tok[:, 0:NCC, 0:P], src[:, NCC:2 * NCC, :]).then_inc(tok_ready, 1)

            def exp_weights(g, d):
                act.wait_ge(expo_ready, at(2 * g + d + 1))
                nc.scalar.activation(wgt[:, :, :], wgt[:, :, :], ACT.Exp, scale=-1.0).then_inc(wexp_ready, 1)

            def denominators(g, d, j):
                m = len(OUT[d][j])
                l0 = OUT[d][j][0]
                act.wait_ge(o_full, at(6 * g + 3 * d + j + 1))
                act.wait_ge(h_ready, at(6 * g + 3 * d))
                nc.scalar.activation(tiny[:, 8 * d + l0:8 * d + l0 + m],
                                     ps[:, B_O, 0:m * VW].rearrange("p (c n) -> p c n", n=VW)[:, :, P],
                                     ACT.Abs).then_inc(den_ready, 1)

            def squares(g):
                act.wait_ge(h_ready, at(6 * g + 6))
                act.wait_ge(pt_ready, at(4 * g + 4))
                nc.scalar.activation(wgt[:, :, :], h_tok[:, :, :], ACT.Square).then_inc(sq_ready, 1)

            def head_tile(i, k):
                return Tile(N_HEAD + k, 4, i)

            q_half(0, 0); q_half(0, 1); hi_split(head_tile(0, 2))
            tanh_q(0); k_ctx(0); k_half(0, 0); k_half(0, 1); hi_split(head_tile(0, 3))
            tanh_k(0); v_ctx(0); v_half(0, 0); v_half(0, 1); hi_split(head_tile(0, 4))
            o_half(0, 0); o_half(0, 1); hi_split(head_tile(0, 5))
            for row, need, scale in ((g_f, ROW_AX, 1.0), (g_e, ROW_WX, 1.0), (g_s, ROW_EX, -1.0)):
                act.wait_ge(row_v, at(need))
                nc.scalar.activation(row[:, :], row[:, :], ACT.Exp, scale=scale).then_inc(row_a, 1)

            with act.Fori(1, H) as i:
                g = i - 1
                kv_tokens(g, 0); kv_tokens(g, 1); exp_weights(g, 0); q_half(i, 0)
                kv_tokens(g, 2); kv_tokens(g, 3); kv_tokens(g, 4); q_half(i, 1); hi_split(head_tile(i, 2))
                exp_weights(g, 1); k_ctx(i); tanh_q(i); k_half(i, 0)
                denominators(g, 0, 0); k_half(i, 1); hi_split(head_tile(i, 3)); denominators(g, 0, 1)
                v_ctx(i); denominators(g, 0, 2); tanh_k(i); v_half(i, 0)
                denominators(g, 1, 0); v_half(i, 1); hi_split(head_tile(i, 4))
                denominators(g, 1, 1); denominators(g, 1, 2); squares(g); o_half(i, 0)
                o_half(i, 1); hi_split(head_tile(i, 5))

            def c_half(half, n):
                act.wait_ge(full[half], at(n + 1))
                act.wait_ge(drained[1], at(n - 1))
                nc.scalar.copy(q_t[:, half * HALF:(half + 1) * HALF], ps[:, half, :]).then_inc(drained[half], 1)

            def conv_tile(k, i=0):
                return Tile(N_CONV + k, 6, i)

            def z_part(hi_tile, n):
                act.wait_ge(drained[0], at(n + 1))
                act.wait_ge(drained[1], at(n + 1))
                nc.scalar.copy(hi_tile, k_t[:, 0:T]).then_inc(z_hi_ready, 1)

            g = H - 1
            kv_tokens(g, 0); kv_tokens(g, 1); exp_weights(g, 0)
            act.wait_ge(qs_ready, at(2 * H)); act.wait_ge(s_full, at(2 * H)); c_half(0, N_CONV)
            kv_tokens(g, 2); kv_tokens(g, 3); kv_tokens(g, 4)
            c_half(1, N_CONV); hi_split(conv_tile(2)); exp_weights(g, 1)
            denominators(g, 0, 0); hi_split(conv_tile(3)); denominators(g, 0, 1); denominators(g, 0, 2)
            hi_split(conv_tile(4)); z_part(br_hi01[:, 0, :], N_CONV + 2)
            denominators(g, 1, 0); c_half(0, N_CONV + 3); denominators(g, 1, 1); denominators(g, 1, 2)
            c_half(1, N_CONV + 3); hi_split(conv_tile(5)); squares(g)
            hi_split(conv_tile(6)); z_part(br_hi01[:, 1, :], N_CONV + 5); hi_split(conv_tile(7))
            act.wait_ge(a_stored, at(H))
            with act.Fori(1, KT // 2) as i:
                for k in range(6):
                    if k % 3 == 0:
                        for half in range(2):
                            c_half(half, N_CONV + 6 * i + k)
                    hi_split(conv_tile(k + 2, i))
                    if k % 3 == 2:
                        z_part(br_hi27[:, ds(2 * i + (k // 3 - 2), 1), :].rearrange("p a n -> p (a n)"),
                               N_CONV + 6 * i + k)

            def gate_half(t, slot, half):
                act.wait_ge(full[half], at(t.n + 1))
                act.wait_ge(drained[half], at(t.n))
                nc.scalar.activation(gth[:, slot, HALVES[half]], ps[:, half, :], ACT.Tanh,
                                     scale=0.5).then_inc(drained[half], 1)

            def branch_hi(k):
                act.wait_ge(br_in[k % NBR], 16 * (k // NBR + 1))
                nc.scalar.copy(br[k][0], b_raw[:, k % NBR, :]).then_inc(br_hi_ready, 1)

            for stage, base in enumerate((N_MIX_C, N_MIX_M)):
                if stage:
                    act.wait_ge(full[1], at(N_MIX_M))
                else:
                    act.wait_ge(acc_ready, at(4 * PASS))
                for k in range(2):
                    for half in range(2):
                        if stage:
                            branch_hi(4 * k + 2 * half)
                            branch_hi(4 * k + 2 * half + 1)
                        gate_half(Tile(base + k), k, half)
                    hi_split(Tile(base + k).ahead(2))
                with act.Fori(0, KT // 2 - 1) as i:
                    for k in range(2):
                        hi_split(Tile(base + 2 * k + 2, 4, i).ahead(2))
                        t = Tile(base + 2 * k + 3, 4, i)
                        for half in range(2):
                            gate_half(t, k, half)
                        hi_split(t.ahead(2))
                if not stage:
                    for k in range(2):
                        hi_split(Tile(base + 2 * KT - 2 + k).ahead(2))

            act.wait_ge(full[1], at(N_MIX_M + 2 * KT - 2))

            def merged(j):
                act.wait_ge(mix_ready, at(2 * j + 2))
                nc.scalar.mul(op_hi[:, j, :], res[:, j, :], 0.5).then_inc(act_hi, 1)
            for j in range(4):
                merged(j)
            hi_split(Tile(N_WO))
            for j in range(4, KT - 1):
                merged(j)
            hi_split(Tile(N_WO + 1))
            merged(KT - 1)

            def residual(j):
                act.wait_ge(xj_turned, at(j + 1))
                act.wait_ge(act_lo, at(4 * KT))
                nc.scalar.copy(res[:, ds(j, 1), :].rearrange("p a (b n) -> p (a b) n", n=HALF),
                               ps[:, B_S:B_S + 2, :]).then_inc(xres_ready, 1)

            with act.Fori(0, KT // 2) as i:
                for k in range(2):
                    residual(2 * i + k)
                    hi_split(Tile(N_WO + k, 2, i).ahead(2))

            def second_norm():
                act.wait_ge(pad_ready, at(1))
                for half, sl in enumerate(HALVES):
                    for k in range(KT):
                        t = KT * half + k
                        act.wait_ge(ut_ready, at(t + 1))
                        if t >= 2:
                            act.wait_ge(act_lo, at(4 * KT + t - 1))
                        nc.scalar.activation(u_h[:, k % 2, :], u_t[:, k % 2, :], ACT.Identity,
                                             scale=gain[:, 2, k:k + 1],
                                             bias=mod[:, 3 * KT + k, 0:1]).then_inc(uh_ready, 1)
                        act.wait_ge(uh_ready, at(t + 1))
                        nc.scalar.copy(op_hi[:, k, sl], u_h[:, k % 2, :]).then_inc(act_hi, 1)
                        if (half, k) == (1, 2):
                            a_half(Tile(N_FFN), 0, 0)

            def a_half(t, f, half):
                act.wait_ge(full[half], at(t.n + 1))
                act.wait_ge(cv_ready, at(f))
                r0 = 1 + half * ROWS // 2
                nc.scalar.copy(a_pad[:, r0:r0 + ROWS // 2, 1:1 + GRID],
                               ps[:, half, :].rearrange("p (r w) -> p r w", w=GRID)).then_inc(drained[half], 1)

            def hidden_tile(n, i, f, first_half=0):
                ta, tg = Tile(n, 2, i), Tile(n + 1, 2, i)
                for half in range(first_half, 2):
                    a_half(ta, f, half)
                hi_split(ta.ahead(2))
                for half in range(2):
                    act.wait_ge(full[half], at(tg.n + 1))
                    act.wait_ge(ul_ready, at(f))
                    nc.scalar.copy(gv[:, HALVES[half]], ps[:, half, :]).then_inc(drained[half], 1)
                hi_split(tg.ahead(2))
                act.wait_ge(cv_ready, at(f + 1))
                nc.scalar.activation(cv[:, :], cv[:, :], ACT.Gelu_apprx_tanh).then_inc(gelu_ready, 1)
                act.wait_ge(u_ready, at(f + 1))
                act.wait_ge(full[1], at(n))
                nc.scalar.copy(hid_hi[:, ds(i, 1), :], gv[:, :]).then_inc(uh_ready, 1)

            n, done = N_FFN, 0
            second_norm()
            for group, size in enumerate(GROUPS):
                if not group:
                    hidden_tile(n, 0, 0, first_half=1)
                with act.Fori(0 if group else 1, size) as i:
                    hidden_tile(n, i, done + i)
                n += 2 * size
                done += size
                last = group == len(GROUPS) - 1
                with act.Fori(0, KT // 2 - last) as i:
                    for k in range(2):
                        hi_split(Tile(n + k, 2, i).ahead(2))
                n += KT

            for l in range(NL):
                act.wait_ge(f_turned, at(l + 1))
                act.wait_ge(f_sum, at(l))
                nc.scalar.activation(junk[:, :], ps[:, 2 * (l % 4):2 * (l % 4) + 2, :].rearrange("p b n -> p (b n)"),
                                     ACT.Square, accum_out=st3[:, l:l + 1]).then_inc(f_sum, 1)

        @block.vector
        def _(dve):
            vec = nc.vector
            chain = Chain(dve, v_step)

            def lo_split(t):
                dve.wait_ge(hi_ready, at(t.n + 1))
                vec.tensor_tensor(w_lo[:, t.slot], w_raw[:, t.slot], w_hi[:, t.slot].bitcast(F32),
                                  ALU.subtract).then_inc(lo_ready, 1)

            def scale_tokens(b):
                dve.wait_ge(rms, at(b + 1))
                for j in range(4 if b < 2 else NCC):
                    vec.tensor_scalar(x_in[:, 4 * b + j, :], x_in[:, 4 * b + j, :],
                                      stat[:, 2, 4 * b + j:4 * b + j + 1], None, ALU.mult).then_inc(x_scaled, 1)

            def low_parts(b):
                n = HALF if b < 2 else TC
                for k in range(KT):
                    t = b * KT + k
                    hi, lo = (a[:, HALVES[b]] for a in op[k]) if b < 2 else ctx_op[k]
                    if k % 2:
                        dve.wait_ge(x_mod, at(t + 1))
                        chain.step(vec.tensor_copy(hi, ht[:, t % 2, 0:n]))
                    else:
                        dve.wait_ge(act_hi, at(t // 2 + 1))
                    vec.tensor_tensor(lo, ht[:, t % 2, 0:n], hi.bitcast(F32), ALU.subtract).then_inc(act_lo, 1)

            for b in range(3):
                scale_tokens(b)
            dve.wait_ge(par_turned, at(4))
            for q, n in enumerate(PAR_ROWS):
                vec.tensor_copy(par[:, q * P:q * P + n], ps[:, 1, q * P:q * P + n]).then_inc(par_ready, 1)
            dve.wait_ge(par_ready, at(4))
            chain.step(vec.tensor_scalar(gate5[:, :], par[:, MNG:MNG + KT], 0.5, None, ALU.mult))
            for b in range(4):
                dve.wait_ge(mod_done, at(2 * b + 2))
                vec.tensor_copy(mrow[:, b * HALF:(b + 1) * HALF], ps[0:2, B_CTX + b, :]).then_inc(mrow_ready, 1)
            lo_split(Tile(0))
            lo_split(Tile(1))
            dve.wait_ge(mod_turned, at(1))
            vec.tensor_tensor(mod[:, 0:2 * KT, :], ps[:, 0, 0:4 * KT].rearrange("p (j v) -> p j v", v=2),
                              par[:, ADA_B:ADA_B + 2 * KT].unsqueeze(2).broadcast_to([P, 2 * KT, 2]),
                              ALU.add).then_inc(mod_ready, 1)
            dve.wait_ge(mod_ready, at(1))
            for v in range(2):
                vec.scalar_tensor_tensor(out=gain[:, v, :], in0=mod[:, KT:2 * KT, v], scalar=1.0,
                                         in1=par[:, N1G:N1G + KT], op0=ALU.add, op1=ALU.mult).then_inc(mod_ready, 1)
            for b in range(3):
                low_parts(b)

            def row(ins):
                ins.then_inc(row_v, 1)
                rows_done[0] += 1
                dve.wait_ge(row_v, at(rows_done[0]))
            rows_done = [0]
            F, B = slice(0, 32), slice(32, 64)

            dve.wait_ge(ctx_drained, at(1))
            dve.wait_ge(drained[0], at(1))
            dve.wait_ge(drained[1], at(1))
            dve.wait_ge(gb_in, 64)
            row(vec.tensor_scalar(g_f[:, :], g_f[:, :], gbias[:, 1:2], None, ALU.add))
            row(vec.scalar_tensor_tensor(out=g_e[:, :], in0=g_f[:, :], scalar=-1.0, in1=g_f[:, :],
                                         op0=ALU.mult, op1=ALU.min))
            lo_split(Tile(2))
            dve.wait_ge(row_a, at(ROW_EXP))
            row(vec.tensor_scalar(g_b[:, :], g_e[:, :], 1.0, None, ALU.add))
            row(vec.scalar_tensor_tensor(out=g_b[:, :], in0=g_b[:, :], scalar=-1.0, in1=g_e[:, :],
                                         op0=ALU.add, op1=ALU.subtract))
            dve.wait_ge(row_a, at(ROW_LN))
            row(vec.tensor_scalar(g_e[:, :], g_e[:, :], -0.5, 1.0, ALU.mult, ALU.add))
            row(vec.tensor_tensor(g_b[:, :], g_b[:, :], g_e[:, :], ALU.mult))
            row(vec.tensor_tensor(g_s[:, :], g_s[:, :], g_b[:, :], ALU.subtract))
            row(vec.scalar_tensor_tensor(out=g_f[:, :], in0=g_f[:, :], scalar=0.0, in1=g_s[:, :],
                                         op0=ALU.min, op1=ALU.subtract))

            def row_sums():
                dve.wait_ge(setup, at(SET_MARKS))
                row(vec.tensor_tensor_scan(g_b[F, :], g_r[F, :], g_f[F, :], 0.0, ALU.mult, ALU.add))
                row(vec.tensor_tensor_scan(g_b[B, ::-1], g_r[B, ::-1], g_f[B, ::-1], 0.0, ALU.mult, ALU.add))
                row(vec.scalar_tensor_tensor(out=g_i[:, :], in0=g_i[:, :], scalar=gbias[:, 0:1], in1=g_b[:, :],
                                             op0=ALU.add, op1=ALU.subtract))

            def row_maxima():
                row(vec.memset(g_d[:, :], 0.0))
                row(vec.tensor_copy(g_d[F, CH::CH], g_b[F, CH - 1:TA - CH:CH]))
                row(vec.tensor_copy(g_d[B, CH - 1:CH], g_b[B, CH:CH + 1]))
                row(vec.tensor_copy(g_d[B, TC + CH - 1:TA - CH:CH], g_b[B, TC + CH::CH]))
                row(vec.tensor_copy(g_d[B, TA - 1:TA], g_b[B, 0:1]))
                row(vec.tensor_tensor_scan(g_m[F, :], g_d[F, :], g_i[F, :], NEG, ALU.add, ALU.max))
                row(vec.tensor_tensor_scan(g_m[B, TC - 1::-1], g_d[B, TC - 1::-1], g_i[B, TC - 1::-1], NEG,
                                           ALU.add, ALU.max))
                row(vec.tensor_tensor_scan(g_m[B, TA - 1:TC - 1:-1], g_d[B, TA - 1:TC - 1:-1],
                                           g_i[B, TA - 1:TC - 1:-1], g_m[B, 0:1], ALU.add, ALU.max))

            def row_factors():
                row(vec.memset(mp[:, :, :], NEG))
                row(vec.tensor_tensor(mp[F, 0, 1:NC], g_m[F, CH - 1:TA - CH:CH], g_d[F, CH::CH], ALU.add))
                row(vec.tensor_tensor(mp[B, 0, 0:1], g_m[B, CH:CH + 1], g_d[B, CH - 1:CH], ALU.add))
                row(vec.tensor_tensor(mp[B, 0, NCC:NC - 1], g_m[B, TC + CH::CH], g_d[B, TC + CH - 1:TA - CH:CH],
                                      ALU.add))
                row(vec.tensor_tensor(mp[B, 0, NC - 1:NC], g_m[B, 0:1], g_d[B, TA - 1:TA], ALU.add))
                row(vec.tensor_copy(mp[F, 1, :], g_m[F, CH - 1::CH]))
                row(vec.tensor_copy(mp[B, 1, :], g_m[B, 0::CH]))

                def chunks(a):
                    return a[:, :].rearrange("p (c n) -> p c n", n=CH)

                def ends(v):
                    return mp[:, v, :].unsqueeze(2).broadcast_to([64, NC, CH])
                row(vec.tensor_tensor(chunks(g_f), ends(0), chunks(g_m), ALU.subtract))
                row(vec.tensor_tensor(chunks(g_e), chunks(g_i), ends(1), ALU.subtract))
                row(vec.tensor_tensor(g_s[:, :], g_b[:, :], g_m[:, :], ALU.add))
                row(vec.tensor_scalar(g_s[:, :], g_s[:, :], -EXP_MAX, None, ALU.max))

            def conv3(src, dst, n, w, b, last):
                chain.step(vec.tensor_scalar(dst, src[:, 1:1 + n], w(1), b, ALU.mult, ALU.add))
                yield
                chain.step(vec.scalar_tensor_tensor(out=dst, in0=src[:, 0:n], scalar=w(0), in1=dst,
                                                    op0=ALU.mult, op1=ALU.add))
                yield
                ins = vec.scalar_tensor_tensor(out=dst, in0=src[:, 2:2 + n], scalar=w(2), in1=dst,
                                               op0=ALU.mult, op1=ALU.add)
                ins.then_inc(conv_ready, 1) if last else chain.step(ins)

            def qk_conv(i, k, n):
                dve.wait_ge(drained[0], at(n + 1))
                dve.wait_ge(drained[1], at(n + 1))
                dve.wait_ge(setup, at(SET_RAW))

                def w(tap):
                    return par[:, ds(i + (QKW + 16 * tap + 8 * k), 1)]
                b = par[:, ds(i + (QKB + 8 * k), 1)]
                if k:
                    dve.wait_ge(ctx_drained, at(2 * i + 2))
                    yield from conv3(raw[:, T + 2:], conv[:, 0:TC], TC, w, b, False)
                    yield
                yield from conv3(raw, conv[:, TC:TA], T, w, b, True)

            def rest(steps):
                for _ in steps:
                    pass

            def q_silu(i):
                dve.wait_ge(tanh_ready, at(2 * i + 1))
                vec.scalar_tensor_tensor(out=q_t[:, :], in0=q_t[:, :], scalar=1.0, in1=conv[:, TC:TA],
                                         op0=ALU.add, op1=ALU.mult).then_inc(q_ready, 1)
                dve.wait_ge(q_ready, at(i + 1))

            def k_silu(i):
                dve.wait_ge(tanh_ready, at(2 * i + 2))
                vec.scalar_tensor_tensor(out=k_t[:, :], in0=k_t[:, :], scalar=1.0, in1=conv[:, :],
                                         op0=ALU.add, op1=ALU.mult).then_inc(k_ready, 1)

            def o_gate(i, n):
                dve.wait_ge(drained[0], at(n + 1))
                dve.wait_ge(drained[1], at(n + 1))
                dve.wait_ge(at_ready, at(2 * i))
                vec.tensor_scalar(og[:, :], conv[:, 0:T], 1.0, None, ALU.add).then_inc(og_ready, 1)
                dve.wait_ge(og_ready, at(i + 1))

            def col(q, g, d, c0, c1, width):
                return cols[:, q, c0:c1, d, ds(g, 1)].broadcast_to([P, c1 - c0, width])

            def exponents(g, d):
                if d == 0:
                    dve.wait_ge(bc_in, 64 * (g + 1))
                    dve.wait_ge(row_cols, at(3))
                else:
                    dve.wait_ge(pt_ready, at(4 * g + 2))
                mask = (late, early)[d][:, :].unsqueeze(1).broadcast_to([P, NL, CH])
                chain.step(vec.tensor_tensor(wgt[:, :, :], m_bc[:, d, :].rearrange("p (c n) -> p c n", n=CH),
                                             col(0, g, d, NCC, NC, CH), ALU.subtract))
                vec.tensor_tensor(wgt[:, :, :], wgt[:, :, :], mask, ALU.max).then_inc(expo_ready, 1)

            def scaled_queries(g, d):
                dve.wait_ge(q_ready, at(g + 1))
                dve.wait_ge(o_full, at(6 * g))
                vec.scalar_tensor_tensor(out=qs[:, d, :], in0=q_t[:, :], scalar=0.5, in1=a_bc[:, d, TC:TA],
                                         op0=ALU.mult, op1=ALU.mult).then_inc(qs_ready, 1)

            def weighted_scores(g, d):
                dve.wait_ge(wexp_ready, at(2 * g + d + 1))
                if d == 0:
                    dve.wait_ge(a_stored, at(g))
                else:
                    dve.wait_ge(o_full, at(6 * g + 3))
                for j in range(2):
                    dve.wait_ge(s_full, at(2 * g + j + 1))
                    vec.scalar_tensor_tensor(out=pt[:, 4 * j:4 * j + 4, :],
                                             in0=ps[:, B_S + j, :].rearrange("p (c n) -> p c n", n=CH),
                                             scalar=SCALE / 4, in1=wgt[:, 4 * j:4 * j + 4, :],
                                             op0=ALU.mult, op1=ALU.mult).then_inc(pt_ready, 1)

            def weighted_values(g, d):
                dve.wait_ge(tok_ready, at(5 * g + 5))
                dve.wait_ge(g_full, at(6 * g + 3 * d))
                vec.scalar_tensor_tensor(out=vw[:, :, :], in0=v_tok[:, :, :], scalar=SCALE / 2,
                                         in1=col(1, g, d, 0, NC, VW), op0=ALU.mult,
                                         op1=ALU.mult).then_inc(vw_ready, 1)

            def carry(g, d, j):
                dve.wait_ge(g_full, at(6 * g + 3 * d + j + 1))
                dve.wait_ge(o_full, at(6 * g))
                for q in range(3):
                    k = 3 * j + q
                    add = ps[:, B_G, q * VW:(q + 1) * VW]
                    if k == 0:
                        ins = vec.tensor_copy(state[:, d, 0, :], add)
                    else:
                        ch = SCAN[d][k]
                        end = ch * CH + (CH - 1 if d == 0 else 0)
                        ins = vec.scalar_tensor_tensor(out=state[:, d, k, :], in0=state[:, d, k - 1, :],
                                                       scalar=a_bc[:, d, end:end + 1], in1=add,
                                                       op0=ALU.mult, op1=ALU.add)
                    if q < 2:
                        chain.step(ins)
                ins.then_inc(state_ready, 1)
                dve.wait_ge(state_ready, at(6 * g + 3 * d + j + 1))

            def heads_out(g, d, j):
                ls = OUT[d][j]
                m, l0 = len(ls), ls[0]
                dve.wait_ge(den_ready, at(6 * g + 3 * d + j + 1))
                dve.wait_ge(h_turned, at(2 * g))
                den, top, rec = (tiny[:, 16 * q + 8 * d + l0:16 * q + 8 * d + l0 + m] for q in range(3))
                chain.step(vec.tensor_tensor(top, den, cols[:, 2, NCC + l0:NCC + l0 + m, d, ds(g, 1)].rearrange(
                    "p c a -> p (c a)"), ALU.max))
                chain.step(vec.reciprocal(rec, top))
                num = ps[:, B_O, 0:m * VW].rearrange("p (c n) -> p c n", n=VW)[:, :, 0:P]
                rec = rec.unsqueeze(2).broadcast_to([P, m, P])
                if d == 0:
                    vec.tensor_tensor(h_tok[:, l0:l0 + m, :], num, rec, ALU.mult).then_inc(h_ready, 1)
                else:
                    chain.step(vec.tensor_tensor(h_tmp[:, 0:m, :], num, rec, ALU.mult))
                    dve.wait_ge(h_ready, at(6 * g + 3))
                    vec.tensor_tensor(h_tok[:, l0:l0 + m, :], h_tok[:, l0:l0 + m, :], h_tmp[:, 0:m, :],
                                      ALU.add).then_inc(h_ready, 1)

            def head_norm(g):
                dve.wait_ge(sq_ready, at(g + 1))
                dve.wait_ge(rn_ready, at(g))
                chain.step(vec.tensor_reduce(tiny[:, 48:56], wgt[:, :, :], AX_X, ALU.add))
                vec.tensor_scalar(tiny[:, 56:64], tiny[:, 48:56], 1.0 / P, EPS, ALU.mult, ALU.add).then_inc(ss_ready, 1)
                dve.wait_ge(rn_ready, at(g + 1))
                vec.tensor_tensor(h_tok[:, :, :], h_tok[:, :, :], tiny[:, 64:72].unsqueeze(2).broadcast_to([P, NL, P]),
                                  ALU.mult).then_inc(hn_ready, 1)

            def head_result(g):
                dve.wait_ge(og_ready, at(g + 1))
                dve.wait_ge(o_full, at(6 * g + 6))
                for j in range(2):
                    dve.wait_ge(h_turned, at(2 * g + j + 1))
                    vec.scalar_tensor_tensor(out=pt[:, 4 * j:4 * j + 4, :].rearrange("p c n -> p (c n)"),
                                             in0=ps[:, B_T + j, :], scalar=gate5[:, ds(g, 1)],
                                             in1=og[:, j * HALF:(j + 1) * HALF], op0=ALU.mult,
                                             op1=ALU.mult).then_inc(at_ready, 1)

            def head_tile(i, k):
                return Tile(N_HEAD + k, 4, i)

            lo_split(head_tile(0, 2))
            rest(qk_conv(0, 0, N_HEAD)); q_silu(0)
            row_sums()
            lo_split(head_tile(0, 3))
            rest(qk_conv(0, 1, N_HEAD + 1)); k_silu(0)
            row_maxima()
            lo_split(head_tile(0, 4))
            row_factors()
            dve.wait_ge(k_ready, at(1))
            o_gate(0, N_HEAD + 3)
            lo_split(head_tile(0, 5))
            for q in range(3):
                dve.wait_ge(row_turned, at(q + 1))
                src = ps[:, B_S:B_S + 2, :].rearrange("p b n -> p (b n)")[:, 0:64 * NC].rearrange(
                    "p (c d h) -> p c d h", d=2, h=32)[:, :, :, 0:H]
                vec.tensor_copy(cols[:, q], src).then_inc(row_cols, 1)

            with dve.Fori(1, H) as i:
                g = i - 1
                chain.enter(i, 1, V_HEAD)
                exponents(g, 0); scaled_queries(g, 0); scaled_queries(g, 1); weighted_scores(g, 0)
                exponents(g, 1); weighted_values(g, 0); carry(g, 0, 0); lo_split(head_tile(i, 2))
                carry(g, 0, 1); rest(qk_conv(i, 0, N_HEAD + 4 * i)); carry(g, 0, 2); q_silu(i)
                weighted_values(g, 1); heads_out(g, 0, 0); lo_split(head_tile(i, 3)); heads_out(g, 0, 1)
                k_conv = qk_conv(i, 1, N_HEAD + 4 * i + 1)
                next(k_conv); next(k_conv); heads_out(g, 0, 2); carry(g, 1, 0)
                next(k_conv); next(k_conv); carry(g, 1, 1); rest(k_conv)
                weighted_scores(g, 1); carry(g, 1, 2); k_silu(i)
                heads_out(g, 1, 0); lo_split(head_tile(i, 4)); heads_out(g, 1, 1); heads_out(g, 1, 2)
                head_norm(g); head_result(g)
                o_gate(i, N_HEAD + 4 * i + 3); lo_split(head_tile(i, 5))
                chain.leave(H - 1)

            def conv_tile(k, i=0):
                return Tile(N_CONV + k, 6, i)

            def c_times_x(half, n):
                dve.wait_ge(full[half], at(n + 1))
                dve.wait_ge(drained[half], at(n))
                vec.tensor_tensor(raw[:, 1 + half * HALF:1 + (half + 1) * HALF], q_t[:, half * HALF:(half + 1) * HALF],
                                  ps[:, half, :], ALU.mult).then_inc(drained[half], 1)

            def sc_conv(j, n):
                dve.wait_ge(drained[0], at(n + 1))
                dve.wait_ge(drained[1], at(n + 1))
                b = par[:, ds(j + SCB, 1)]
                dst = conv[:, TC:TA]
                chain.step(vec.tensor_scalar(dst, raw[:, 1:1 + T], par[:, ds(j + SCW + 8, 1)], b, ALU.mult, ALU.add))
                for tap in (0, 2):
                    chain.step(vec.scalar_tensor_tensor(out=dst, in0=raw[:, tap:tap + T],
                                                        scalar=par[:, ds(j + SCW + 8 * tap, 1)],
                                                        in1=dst, op0=ALU.mult, op1=ALU.add))

            def times_b(j, half, n):
                dve.wait_ge(full[half], at(n + 1))
                dve.wait_ge(br_lo_ready, at(j))
                vec.tensor_tensor(k_t[:, HALVES[half]], conv[:, TC + half * HALF:TC + (half + 1) * HALF],
                                  ps[:, half, :], ALU.mult).then_inc(drained[half], 1)

            def z_low(tiles, j, k):
                hi, lo = (a[:, ds(k, 1), :].rearrange("p a n -> p (a n)") for a in tiles)
                dve.wait_ge(z_hi_ready, at(j + 1))
                vec.tensor_tensor(lo, k_t[:, 0:T], hi.bitcast(F32), ALU.subtract).then_inc(br_lo_ready, 1)

            def mac(p, q):
                dve.wait_ge(late_in[q % 2], 16 * (PASS // 2) * p + 16 * (q // 2 + 1))
                if q == 0:
                    dve.wait_ge(mod_done, at(NAL1 + p))
                for k in range(KT):
                    if k == 0:
                        ins = vec.tensor_scalar(acc[:, q, :], aw[:, q % 2, k, :], cs[:, k, 0:1], None, ALU.mult)
                    else:
                        ins = vec.scalar_tensor_tensor(out=acc[:, q, :], in0=aw[:, q % 2, k, :], scalar=cs[:, k, 0:1],
                                                       in1=acc[:, q, :], op0=ALU.mult, op1=ALU.add)
                    if k < KT - 1:
                        chain.step(ins)
                ins.then_inc(acc_ready, 1)

            def late_modulation(p):
                dve.wait_ge(mod_done, at(NAL1 + 1 + p))
                vec.tensor_tensor(mod[:, ds(JP * p + 2 * KT, JP), 0], ps[:, B_G, 0:JP],
                                  par[:, ds(JP * p + (ADA_B + 2 * KT), JP)], ALU.add).then_inc(mod_read, 1)

            g, n = H - 1, N_CONV
            exponents(g, 0); scaled_queries(g, 0); scaled_queries(g, 1); weighted_scores(g, 0)
            exponents(g, 1); weighted_values(g, 0); carry(g, 0, 0); lo_split(conv_tile(2))
            carry(g, 0, 1); c_times_x(0, n + 1); carry(g, 0, 2); weighted_values(g, 1)
            c_times_x(1, n + 1); lo_split(conv_tile(3)); heads_out(g, 0, 0); heads_out(g, 0, 1)
            sc_conv(0, n + 1)
            dve.wait_ge(turned, at(5 * H))
            heads_out(g, 0, 2); times_b(0, 0, n + 2); weighted_scores(g, 1); carry(g, 1, 0); carry(g, 1, 1)
            times_b(0, 1, n + 2); carry(g, 1, 2); lo_split(conv_tile(4)); z_low((br_hi01, br_lo01), 0, 0)
            heads_out(g, 1, 0); heads_out(g, 1, 1); heads_out(g, 1, 2); lo_split(conv_tile(5))
            head_norm(g); c_times_x(0, n + 4); head_result(g); c_times_x(1, n + 4); lo_split(conv_tile(6))
            sc_conv(1, n + 4); times_b(1, 0, n + 5); times_b(1, 1, n + 5); z_low((br_hi01, br_lo01), 1, 1)
            mac(0, 0); mac(0, 1); lo_split(conv_tile(7)); mac(0, 2); mac(0, 3)
            with dve.Fori(1, KT // 2) as i:
                chain.enter(i, 1, 6 + PASS * (KT - 1))
                for k in range(2):
                    j, n = 2 * i + k, N_CONV + 3 * k + 6 * i
                    lo_split(conv_tile(3 * k + 2, i))
                    c_times_x(0, n + 1); c_times_x(1, n + 1); lo_split(conv_tile(3 * k + 3, i))
                    sc_conv(j, n + 1)
                    times_b(j, 0, n + 2); times_b(j, 1, n + 2); lo_split(conv_tile(3 * k + 4, i))
                    z_low((br_hi27, br_lo27), j, j - 2)
                    if k == 0:
                        late_modulation(i - 1)
                    mac(i, 2 * k); mac(i, 2 * k + 1)
                chain.leave(KT // 2 - 1)

            mtmp = b_raw[:, 0, :]

            def mixed(stage, j, t, slot):
                for half, sl in enumerate(HALVES):
                    dve.wait_ge(full[half], at(t.n + 1))
                    dve.wait_ge(drained[half], at(t.n))
                    dst = res[:, ds(j, 1), sl].rearrange("p a n -> p (a n)")
                    if stage:
                        dve.wait_ge(mix_ready, at(2 * j + half))
                    vec.scalar_tensor_tensor(out=mtmp[:, sl] if stage else dst, in0=gth[:, slot, sl], scalar=1.0,
                                             in1=ps[:, half, :], op0=ALU.add, op1=ALU.mult).then_inc(drained[half], 1)
                    if stage:
                        dve.wait_ge(drained[half], at(t.n + 1))
                        vec.tensor_tensor(dst, dst, mtmp[:, sl], ALU.add).then_inc(mix_ready, 1)

            def branch_lo(k):
                dve.wait_ge(br_hi_ready, at(k + 1))
                vec.tensor_tensor(br[k][1], b_raw[:, k % NBR, :], br[k][0].bitcast(F32),
                                  ALU.subtract).then_inc(br_lo_ready, 1)

            def merged(j):
                dve.wait_ge(act_hi, at(3 * KT // 2 + j + 1))
                vec.scalar_tensor_tensor(out=op_lo[:, j, :], in0=res[:, j, :], scalar=0.5,
                                         in1=op_hi[:, j, :].bitcast(F32), op0=ALU.mult,
                                         op1=ALU.subtract).then_inc(act_lo, 1)

            for stage, base in enumerate((N_MIX_C, N_MIX_M)):
                for k in range(2):
                    if stage:
                        for q in range(4):
                            branch_lo(4 * k + q)
                    lo_split(Tile(base + k + 2))
                if not stage:
                    late_modulation(KT // 2 - 1)
                    dve.wait_ge(mod_read, at(KT // 2))
                    vec.scalar_tensor_tensor(out=gain[:, 2, :], in0=mod[:, 4 * KT:5 * KT, 0], scalar=1.0,
                                             in1=par[:, N2G:N2G + KT], op0=ALU.add, op1=ALU.mult).then_inc(mod_ready, 1)
                with dve.Fori(0, KT // 2 - 1) as i:
                    for k in range(2):
                        t = Tile(base + 2 * k + 2, 4, i)
                        mixed(stage, 2 * i + k, t, k)
                        lo_split(t.ahead(2))
                        lo_split(t.ahead(3))
                if stage:
                    for j in range(4):
                        merged(j)
                mixed(stage, KT - 2, Tile(base + 2 * KT - 2), 0)
                lo_split(Tile(base + 2 * KT))
                if stage:
                    for j in range(4, KT - 1):
                        merged(j)
                mixed(stage, KT - 1, Tile(base + 2 * KT - 1), 1)
                lo_split(Tile(base + 2 * KT + 1))
            merged(KT - 1)

            dve.wait_ge(mod_ready, at(4))
            chain.step(vec.memset(sqsum[:, :], 0.0))
            def mean_squares(half):
                part = slice(4 * half, 4 * half + 4)
                dve.wait_ge(stat_done, at(half + 1))
                vec.tensor_scalar(st2[:, 0, part], ps[:, B_O, part], 1.0 / D, EPS, ALU.mult,
                                  ALU.add).then_inc(n2_sum, 1)

            def factors(half):
                part = slice(4 * half, 4 * half + 4)
                dve.wait_ge(n2_rms, at(half + 1))
                if half:
                    dve.wait_ge(factor_spread, at(1))
                vec.tensor_tensor(diag[:, :, :], ident[:, :].unsqueeze(1).broadcast_to([P, 4, P]),
                                  st2[:, 1, part].unsqueeze(2).broadcast_to([P, 4, P]),
                                  ALU.mult).then_inc(n2_ready, 1)

            def added(i, last=False):
                for k in range(2):
                    t = Tile(N_WO + k, 2, i)
                    dve.wait_ge(xres_ready, at(2 * i + k + 1))
                    for half, sl in enumerate(HALVES):
                        dve.wait_ge(full[half], at(t.n + 1))
                        dst = res[:, ds(2 * i + k, 1), sl].rearrange("p a n -> p (a n)")
                        vec.scalar_tensor_tensor(out=dst, in0=ps[:, half, :],
                                                 scalar=mod[:, ds(2 * i + (2 * KT + k), 1), 0],
                                                 in1=dst, op0=ALU.mult, op1=ALU.add).then_inc(drained[half], 1)
                        dve.wait_ge(drained[half], at(t.n + 1))
                        chain.step(vec.tensor_tensor(sq[:, sl], dst, dst, ALU.mult))
                        vec.tensor_tensor(sqsum[:, sl], sqsum[:, sl], sq[:, sl], ALU.add).then_inc(sqsum_ready, 1)
                        dve.wait_ge(sqsum_ready, at(4 * i + (2 * k + half + 1)))
                        if last and (k, half) == (1, 0):
                            mean_squares(0)
                            factors(0)
                    if not (last and k):
                        lo_split(t.ahead(2))

            with dve.Fori(0, KT // 2 - 1) as i:
                chain.enter(i, 0, 4)
                added(i)
                chain.leave(KT // 2 - 1)

            def scaled(half, k):
                dve.wait_ge(factor_spread, at(half + 1))
                if half or k >= 2:
                    dve.wait_ge(uh_ready, at(KT * half + k - 1))
                vec.tensor_tensor(u_t[:, k % 2, :], res[:, k, HALVES[half]], ps[:, B_S + half, :],
                                  ALU.mult).then_inc(ut_ready, 1)

            def low(half, k):
                dve.wait_ge(act_hi, at(3 * KT // 2 + KT + KT * half + k + 1))
                vec.tensor_tensor(op_lo[:, k, HALVES[half]], u_h[:, k % 2, :], op_hi[:, k, HALVES[half]].bitcast(F32),
                                  ALU.subtract).then_inc(act_lo, 1)

            chain.step(vec.memset(a_pad[:, :, :], 0.0))
            dve.sem_inc(pad_ready, 1)
            added(KT // 2 - 1, True)
            lo_split(Tile(N_FFN + 1))
            for half in range(2):
                for k in range(KT):
                    scaled(half, k)
                    if k:
                        low(half, k - 1)
                    if (half, k) == (0, 1):
                        mean_squares(1)
                    if (half, k) == (0, 3):
                        factors(1)
                low(half, KT - 1)

            n, done = N_FFN, 0
            out3 = cv[:, :].rearrange("p (r w) -> p r w", w=GRID)
            for group, size in enumerate(GROUPS):
                with dve.Fori(0, size) as i:
                    chain.enter(i, 0, 8)
                    f = done + i
                    ta, tg = Tile(n, 2, i), Tile(n + 1, 2, i)
                    lo_split(ta.ahead(2))
                    dve.wait_ge(drained[0], at(ta.n + 1))
                    dve.wait_ge(drained[1], at(ta.n + 1))
                    dve.wait_ge(ul_ready, at(f))
                    chain.step(vec.tensor_scalar(out3, a_pad[:, 1:1 + ROWS, 1:1 + GRID],
                                                 par[:, ds(f + (FFW + 4 * FT), 1)],
                                                 par[:, ds(f + FFB, 1)], ALU.mult, ALU.add))
                    for tap in (0, 1, 2, 3, 5, 6, 7, 8):
                        r, w = tap // 3, tap % 3
                        ins = vec.scalar_tensor_tensor(out=out3, in0=a_pad[:, r:r + ROWS, w:w + GRID],
                                                       scalar=par[:, ds(f + (FFW + tap * FT), 1)], in1=out3,
                                                       op0=ALU.mult, op1=ALU.add)
                        if tap < 8:
                            chain.step(ins)
                    ins.then_inc(cv_ready, 1)
                    lo_split(tg.ahead(2))
                    dve.wait_ge(drained[0], at(tg.n + 1))
                    dve.wait_ge(drained[1], at(tg.n + 1))
                    dve.wait_ge(gelu_ready, at(f + 1))
                    vec.tensor_tensor(gv[:, :], cv[:, :], gv[:, :], ALU.mult).then_inc(u_ready, 1)
                    dve.wait_ge(uh_ready, at(2 * KT + f + 1))
                    vec.tensor_tensor(hid_lo[:, ds(i, 1), :].rearrange("p a n -> p (a n)"), gv[:, :],
                                      hid_hi[:, ds(i, 1), :].rearrange("p a n -> p (a n)").bitcast(F32),
                                      ALU.subtract).then_inc(ul_ready, 1)
                    chain.leave(size)
                n += 2 * size
                done += size

                def down(j, t, more):
                    for half in range(2):
                        dve.wait_ge(full[half], at(t.n + 1))
                        dst = res[:, ds(j, 1), half * HALF:(half + 1) * HALF].rearrange("p a n -> p (a n)")
                        vec.scalar_tensor_tensor(out=dst, in0=ps[:, half, :], scalar=mod[:, ds(j + 5 * KT, 1), 0],
                                                 in1=dst, op0=ALU.mult, op1=ALU.add).then_inc(drained[half], 1)
                    if more:
                        lo_split(t.ahead(2))
                last = group == len(GROUPS) - 1
                with dve.Fori(0, KT // 2 - last) as i:
                    for k in range(2):
                        down(2 * i + k, Tile(n + k, 2, i), True)
                if last:
                    for k in range(2):
                        down(KT - 2 + k, Tile(n + KT - 2 + k), False)
                n += KT

            dve.wait_ge(gbc_in, 16)
            for l in range(NL):
                dve.wait_ge(f_rms, at(l + 1))
                vec.scalar_tensor_tensor(out=o_out[:, l, :],
                                         in0=ps[:, 2 * (l % 4):2 * (l % 4) + 2, :].rearrange("p b n -> p (b n)"),
                                         scalar=st3[:, 16 + l:17 + l], in1=gbc[:, :], op0=ALU.mult,
                                         op1=ALU.mult).then_inc(f_ready, 1)

        @block.gpsimd
        def _(pool):
            for s_ in credited:
                pool.sem_inc(s_, 1)
            made = [0]

            def make(ins):
                ins.then_inc(setup, 1)
                made[0] += 1
                pool.wait_ge(setup, at(made[0]))

            gp = nc.gpsimd
            make(gp.memset(ident[:, :], 0.0))
            make(gp.affine_select(out=ident[:, :], in_=ident[:, :], compare_op=ALU.not_equal, fill=1.0, base=0,
                                  pattern=[[-1, P]], channel_multiplier=1))
            for b in range(3):
                src = ctx_tok if b == 2 else x_tok[:, 4 * b:4 * b + 4, :]
                gp.dma_start(x_in[:, 4 * b:4 * b + (NCC if b == 2 else 4), :], src).then_inc(x_loaded[b], 16)
            make(gp.memset(ones[:, :], 1.0))
            for tri, sign in ((late, 1), (early, -1)):
                make(gp.memset(tri[:, :], 0.0))
                make(gp.affine_select(out=tri[:, :], in_=tri[:, :], compare_op=ALU.is_ge, fill=BIG, base=0,
                                      pattern=[[sign, P]], channel_multiplier=-sign))
            make(gp.memset(power[:, :], -0.5))
            make(gp.memset(gbias[:, :], 0.0))
            make(gp.memset(w_raw[:, 0], 0.0))

            def inverse_root(src, tmp, dst, scale, n, count):
                gp.tensor_scalar(tmp, src, scale, EPS, ALU.mult, ALU.add).then_inc(p_step, 1)
                pool.wait_ge(p_step, at(count))
                return gp.tensor_tensor(dst, tmp, power[:, 0:n], ALU.pow)

            for b in range(3):
                n = 4 if b < 2 else NCC
                pool.wait_ge(sumsq, at(4 * b + n))
                inverse_root(*(stat[:, q, 4 * b:4 * b + n] for q in range(3)), 1.0 / D, n, b + 1).then_inc(rms, 1)

            pool.wait_ge(act_lo, at(3 * KT))
            make(gp.memset(g_r[:, :], 1.0))
            make(gp.memset(g_r[0:32, 0::CH], 0.0))
            make(gp.memset(g_r[32:64, CH - 1::CH], 0.0))
            make(gp.memset(raw[:, 0:1], 0.0))
            make(gp.memset(raw[:, T + 1:T + 3], 0.0))
            make(gp.memset(raw[:, T + TC + 3:T + TC + 4], 0.0))
            pool.wait_ge(row_v, at(ROW_M))
            for d in range(2):
                gp.dma_start(m_rows[d], g_m[32 * d:32 * d + H, :]).then_inc(gb_out, 16)
            pool.wait_ge(row_a, at(ROW_A))
            for d in range(2):
                gp.dma_start(a_rows[d], g_f[32 * d:32 * d + H, :]).then_inc(gb_out, 16)
            pool.wait_ge(gb_out, 64)
            pool.wait_ge(row_cols, at(3))

            def broadcast_rows(g):
                for d in range(2):
                    gp.dma_start(m_bc[:, d, :], m_rows[d, ds(g, 1), TC:TA].broadcast_to([P, T])).then_inc(bc_in, 16)
                    gp.dma_start(a_bc[:, d, :], a_rows[d, ds(g, 1), :].broadcast_to([P, TA])).then_inc(bc_in, 16)
            broadcast_rows(0)
            make(gp.memset(v_tok[:, :, P:VW], 1.0))

            def head_norm(g):
                pool.wait_ge(ss_ready, at(g + 1))
                pool.wait_ge(hn_ready, at(g))
                gp.tensor_tensor(tiny[:, 64:72], tiny[:, 56:64], power[:, :], ALU.pow).then_inc(rn_ready, 1)

            def store_head(g):
                pool.wait_ge(at_ready, at(2 * g + 2))
                gp.dma_start(a_dram[ds(g, 1)].rearrange("a p n -> p (a n)"),
                             pt[:, :, :].rearrange("p c n -> p (c n)")).then_inc(a_out, 16)
                pool.wait_ge(a_out, 16 * (g + 1))
                pool.sem_inc(a_stored, 1)

            with pool.Fori(1, H) as i:
                pool.wait_ge(state_ready, at(6 * i))
                broadcast_rows(i)
                head_norm(i - 1)
                store_head(i - 1)

            def late_load(p, q):
                columns = adw[:, :, ds(PASS * AC * p + (NAL1 + q) * AC, AC)]
                gp.dma_start(aw[:, q % 2], columns).then_inc(late_in[q % 2], 16)
            pool.wait_ge(expo_ready, at(2 * H))
            late_load(0, 0)
            pool.wait_ge(state_ready, at(6 * H))
            late_load(0, 1)
            head_norm(H - 1)
            store_head(H - 1)
            for q in (2, 3):
                pool.wait_ge(acc_ready, at(q - 1))
                late_load(0, q)
            with pool.Fori(1, KT // 2) as p:
                for q in range(PASS):
                    pool.wait_ge(acc_ready, at(PASS * p + (q - 1)))
                    late_load(p, q)

            pool.wait_ge(mod_done, at(NAL1 + KT // 2))
            for k in range(KT):
                if k >= NBR:
                    pool.wait_ge(br_lo_ready, at(KT + k - NBR + 1))
                gp.dma_start(b_raw[:, k % NBR, :], a_dram[k]).then_inc(br_in[k % NBR], 16)

            pool.wait_ge(br_lo_ready, at(2 * KT))
            for k in range(2):
                gp.dma_start(x_j[:, k], x_tok[:, :, k * P:(k + 1) * P]).then_inc(xj_in[k], 16)
            with pool.Fori(1, KT // 2) as i:
                for k in range(2):
                    pool.wait_ge(xj_turned, at(2 * i + (k - 1)))
                    gp.dma_start(x_j[:, k], x_tok[:, :, ds(i * (2 * P) + k * P, P)]).then_inc(xj_in[k], 16)
            for half in range(2):
                part = slice(4 * half, 4 * half + 4)
                pool.wait_ge(n2_sum, at(half + 1))
                gp.tensor_tensor(st2[:, 1, part], st2[:, 0, part], power[:, part], ALU.pow).then_inc(n2_rms, 1)

            pool.wait_ge(ul_ready, at(FT))
            gp.dma_start(gbc[:, :], final_g.rearrange("(a d) -> a d", a=1).broadcast_to([P, D])).then_inc(gbc_in, 16)
            for l in range(NL):
                pool.wait_ge(f_sum, at(l + 1))
                inverse_root(*(st3[:, 8 * q + l:8 * q + l + 1] for q in range(3)), 1.0 / D, 1, 4 + l).then_inc(f_rms, 1)

        @block.sync
        def _(sp):
            def par_rows(row, src, n):
                sp.dma_start(prow[row % P:row % P + n, row // P, :], src).then_inc(par_in, 16)

            def tiles(v, pattern="(t p) -> t p"):
                return v.rearrange(pattern, p=P)
            sp.dma_start(crow[0:KT, :], tiles(c[0])).then_inc(cond_in, 16)
            sp.dma_start(crow[KT:2 * KT, :], tiles(c_ctx)).then_inc(cond_in, 16)

            def ada_load(n):
                sp.dma_start(aw0[:, n % NAS], adw[:, :, n * AC:(n + 1) * AC]).then_inc(ada_in[n % NAS], 16)
            ada_load(0)
            ada_load(1)
            par_rows(ADA_B, tiles(ada_b[0]), 48)
            par_rows(N1G, tiles(norm1_g[0]), KT)
            par_rows(N2G, tiles(norm2_g[0]), KT)
            par_rows(MNG, tiles(mnorm_g[0]), KT)
            par_rows(SCB, tiles(sc_conv_b[0]), KT)
            par_rows(SCW, tiles(sc_conv_w[0], "a (t p) -> (a t) p"), 3 * KT)
            par_rows(QKW, tiles(qk_conv_w[0], "a (t p) -> (a t) p"), 6 * KT)
            par_rows(QKB, tiles(qk_conv_b[0]), 2 * KT)
            par_rows(FFB, tiles(ff_conv_b[0]), FT)
            ffw = tiles(ff_conv_w[0], "a b (t p) -> (a b t) p")
            par_rows(FFW, ffw[0:P], P)
            par_rows(FFW + P, ffw[P:9 * FT], 9 * FT - P)
            for n in range(2, NAS):
                ada_load(n)
            sp.wait_ge(setup, at(SET_GBIAS))
            gb = gate_b[0].rearrange("(g h a) -> g h a", g=4, a=1)
            for d in range(2):
                for k in range(2):
                    sp.dma_start(gbias[32 * d:32 * d + H, k:k + 1], gb[2 * d + k]).then_inc(gb_in, 16)
            sp.wait_ge(setup, at(SET_WRAW))
            for k in range(2):
                for d in range(2):
                    c0 = 64 * k + 32 * d
                    w0 = OFF_G + H * (2 * d + k)
                    sp.dma_start(w_raw[:, 0, :, c0:c0 + H], win[:, :, w0:w0 + H]).then_inc(raw_in[0], 16)

            for n in range(NAS, NAL1):
                sp.wait_ge(mod_done, at(n - NAS + 1))
                ada_load(n)

            def load(t, src, col, kt=KT):
                columns = src[:, :, ds(col, P)]
                sp.wait_ge(lo_ready, at(t.n - 1))
                sp.dma_start(w_raw[:, t.slot, 0:kt], columns).then_inc(raw_in[t.slot], 16)

            with sp.Fori(0, H) as i:
                for k, off in enumerate((OFF_Q, OFF_K, OFF_V, OFF_O)):
                    load(Tile(N_HEAD + k, 4, i), win, i * P + off)
            with sp.Fori(0, KT // 2) as i:
                for k in range(6):
                    load(Tile(N_CONV + k, 6, i), win, i * (2 * P) + (k // 3 * P + (OFF_SC, OFF_SX, OFF_SB)[k % 3]))
            for base, off, w in ((N_MIX_C, OFF_MG + D, wco), (N_MIX_M, OFF_MG, wmo)):
                for k in range(2):
                    load(Tile(base + k), win, off + k * P)
                with sp.Fori(0, KT // 2 - 1) as i:
                    for k in range(2):
                        load(Tile(base + 2 * k + 2, 4, i), w, i * (2 * P) + k * P)
                        load(Tile(base + 2 * k + 3, 4, i), win, i * (2 * P) + (off + (k + 2) * P))
                for k in range(2):
                    load(Tile(base + 2 * KT - 2 + k), w, (KT - 2 + k) * P)
            with sp.Fori(0, KT // 2) as i:
                for k in range(2):
                    load(Tile(N_WO + k, 2, i), wo_, i * (2 * P) + k * P)
            n, done = N_FFN, 0
            for size in GROUPS:
                with sp.Fori(0, size) as i:
                    load(Tile(n, 2, i), wup, i * P + done * P)
                    load(Tile(n + 1, 2, i), wup, i * P + (FF + done * P))
                n += 2 * size
                with sp.Fori(0, KT // 2) as i:
                    for k in range(2):
                        load(Tile(n + k, 2, i), wdn[:, done:done + size, :], i * (2 * P) + k * P, size)
                n += KT
                done += size
            for l in range(NL):
                sp.wait_ge(f_ready, at(l + 1))
                sp.dma_start(out_tok[l], o_out[:, l, :]).then_inc(y_out, 16)
            sp.wait_ge(y_out, 16 * NL)


_INS = ["x", "c", "ctx", "c_ctx", "ada_w", "ada_b", "norm1_g", "norm2_g", "w_in", "qk_conv_w", "qk_conv_b",
        "gate_b", "mnorm_g", "w_m_out", "sc_conv_w", "sc_conv_b", "w_c_out", "w_o", "w_up", "ff_conv_w",
        "ff_conv_b", "w_down", "final_g"]


def kernel(**inputs):
    import numpy as np
    import concourse.bacc as bacc
    from concourse.bass_utils import run_bass_kernel_spmd

    nc = bacc.Bacc("TRN2", target_bir_lowering=False, num_devices=1)
    arrays, args = {}, []
    for name in _INS:
        a = np.ascontiguousarray(inputs[name])
        arrays[f"in_{name}"] = a
        args.append(nc.dram_tensor(f"in_{name}", a.shape, mybir.dt.from_np(a.dtype), kind="ExternalInput").ap())
    out = nc.dram_tensor("out_x", (1, T, D), F32, kind="ExternalOutput").ap()
    layer(nc, *args, out)
    r = run_bass_kernel_spmd(nc, [arrays], core_ids=[0])
    return r.results[0]["out_x"]
```
